# Optimizing a Trainium2 kernel written in Bass

```python
import jax, jax.numpy as jnp
from jax import lax
import numpy as np
import jax
import jax.numpy as jnp

D_MODEL = 1024
BATCH = 1
SEQ = 1024
DEPTH = 1

GLA_HEADS = 4
GLA_KEY_DIM = D_MODEL // 2
GLA_VALUE_DIM = D_MODEL
GLA_HEAD_K = GLA_KEY_DIM // GLA_HEADS
GLA_HEAD_V = GLA_VALUE_DIM // GLA_HEADS
GATE_RANK = 16
GATE_NORMALIZER = 16.0
CHUNK = 64
POOL_GROUPS = 4
POOL_WIDTH = D_MODEL // 2
POOL_GROUP_W = POOL_WIDTH // POOL_GROUPS
POOL_OUT_GROUP_W = D_MODEL // POOL_GROUPS
POOL_WINDOWS = (2, 4, 8, 16)
N_BRANCHES = 2
D_FF = -(-8 * D_MODEL // (3 * 256)) * 256
IN_WIDTH = 2 * GLA_KEY_DIM + 2 * GLA_VALUE_DIM + 2 * GATE_RANK + POOL_WIDTH + N_BRANCHES * D_MODEL
EPS = 1e-6


def rmsnorm(x, g):
    xf = x.astype(jnp.float32)
    y = xf * lax.rsqrt(jnp.mean(xf * xf, axis=-1, keepdims=True) + EPS)
    return (y * g.astype(jnp.float32)).astype(x.dtype)

def gla_chunked(q, k, v, log_a, include_diag):
    bsz, heads, length, dk = q.shape
    dv = v.shape[-1]
    n = length // CHUNK
    q = q.reshape(bsz, heads, n, CHUNK, dk).astype(jnp.float32)
    k = k.reshape(bsz, heads, n, CHUNK, dk).astype(jnp.float32)
    v = v.reshape(bsz, heads, n, CHUNK, dv).astype(jnp.float32)
    b = jnp.cumsum(log_a.reshape(bsz, heads, n, CHUNK, dk).astype(jnp.float32), axis=3)
    b_last = b[:, :, :, -1:, :]
    q_e = q * jnp.exp(b)
    k_e = k * jnp.exp(-b)
    k_d = k * jnp.exp(b_last - b)
    mask = jnp.tril(jnp.ones((CHUNK, CHUNK), dtype=bool), 0 if include_diag else -1)
    scores = jnp.einsum('bhncd,bhnsd->bhncs', q_e, k_e)
    scores = jnp.where(mask, scores, 0.0)
    o_intra = jnp.einsum('bhncs,bhnse->bhnce', scores, v)
    kv = jnp.einsum('bhnsd,bhnse->bhnde', k_d, v)
    decay = jnp.exp(b_last[:, :, :, 0, :])

    def step(state, inp):
        kv_n, dec_n = inp
        return dec_n[..., None] * state + kv_n, state

    s0 = jnp.zeros((bsz, heads, dk, dv), jnp.float32)
    _, s_in = lax.scan(step, s0, (jnp.moveaxis(kv, 2, 0), jnp.moveaxis(decay, 2, 0)))
    s_in = jnp.moveaxis(s_in, 0, 2)
    o_inter = jnp.einsum('bhncd,bhnde->bhnce', q_e, s_in)
    return (o_intra + o_inter).reshape(bsz, heads, length, dv)

def to_heads(t, heads):
    bsz, length, width = t.shape
    return t.reshape(bsz, length, heads, width // heads).transpose(0, 2, 1, 3)

def multiscale_pool(u):
    bsz, length, _ = u.shape
    ug = u.reshape(bsz, length, POOL_GROUPS, POOL_GROUP_W).astype(jnp.float32)
    cs = jnp.concatenate([jnp.zeros((bsz, 1, POOL_GROUPS, POOL_GROUP_W), jnp.float32),
                          jnp.cumsum(ug, axis=1)], axis=1)
    pos = jnp.arange(length)[:, None]
    win = jnp.array(POOL_WINDOWS, dtype=jnp.int32)[None, :]
    lo = jnp.clip(pos - win // 2, 0, length)
    hi = jnp.clip(pos + win - win // 2, 0, length)
    gi = jnp.arange(POOL_GROUPS)[None, :]
    window_sum = cs[:, hi, gi] - cs[:, lo, gi]
    count = (hi - lo).astype(jnp.float32)[None, :, :, None]
    return window_sum / count - ug

def first_inputs(seed: int = 0) -> dict:
    key = jax.random.key(seed)
    ks = jax.random.split(key, 16)

    def nrm(k, shape, scale):
        return jax.random.normal(k, shape, jnp.float32) * scale

    return {
        'x': nrm(ks[0], (BATCH, SEQ, D_MODEL), 1.0),
        'norm_mix': 1.0 + nrm(ks[1], (DEPTH, D_MODEL), 0.05),
        'w_in': nrm(ks[2], (DEPTH, D_MODEL, IN_WIDTH), D_MODEL ** -0.5),
        'w_decay_up_fwd': nrm(ks[3], (DEPTH, GATE_RANK, GLA_KEY_DIM), GATE_RANK ** -0.5),
        'b_decay_fwd': nrm(ks[4], (DEPTH, GLA_KEY_DIM), 0.1),
        'w_decay_up_bwd': nrm(ks[5], (DEPTH, GATE_RANK, GLA_KEY_DIM), GATE_RANK ** -0.5),
        'b_decay_bwd': nrm(ks[6], (DEPTH, GLA_KEY_DIM), 0.1),
        'gla_norm': 1.0 + nrm(ks[7], (DEPTH, GLA_VALUE_DIM), 0.05),
        'w_branch_gla': nrm(ks[8], (DEPTH, GLA_VALUE_DIM, D_MODEL), GLA_VALUE_DIM ** -0.5),
        'w_pool_group': nrm(ks[9], (DEPTH, POOL_GROUPS, POOL_GROUP_W, POOL_OUT_GROUP_W), POOL_GROUP_W ** -0.5),
        'pool_scale': 1.0 + nrm(ks[10], (DEPTH, D_MODEL), 0.05),
        'w_out': nrm(ks[11], (DEPTH, D_MODEL, D_MODEL), D_MODEL ** -0.5),
        'norm_ffn': 1.0 + nrm(ks[12], (DEPTH, D_MODEL), 0.05),
        'w_ffn_in': nrm(ks[13], (DEPTH, D_MODEL, 2 * D_FF), D_MODEL ** -0.5),
        'w_ffn_out': nrm(ks[14], (DEPTH, D_FF, D_MODEL), D_FF ** -0.5),
        'norm_final': 1.0 + nrm(ks[15], (D_MODEL,), 0.05),
    }

def first_block(x, norm_mix, w_in, w_decay_up_fwd, b_decay_fwd, w_decay_up_bwd, b_decay_bwd,
              gla_norm, w_branch_gla, w_pool_group, pool_scale, w_out, norm_ffn,
              w_ffn_in, w_ffn_out, norm_final):
    bsz, length, _ = x.shape
    split_sizes = [GLA_KEY_DIM, GLA_KEY_DIM, GLA_VALUE_DIM, GLA_VALUE_DIM, GATE_RANK, GATE_RANK,
                   POOL_WIDTH, D_MODEL, D_MODEL]
    split_points = [int(p) for p in np.cumsum(split_sizes)[:-1]]
    for l in range(DEPTH):
        h = rmsnorm(x, norm_mix[l])
        proj = h @ w_in[l]
        q, k, v, r, lr_f, lr_b, u, g_a, g_b = jnp.split(proj, split_points, axis=-1)

        log_a_f = jax.nn.log_sigmoid((lr_f @ w_decay_up_fwd[l] + b_decay_fwd[l]).astype(jnp.float32)) / GATE_NORMALIZER
        log_a_b = jax.nn.log_sigmoid((lr_b @ w_decay_up_bwd[l] + b_decay_bwd[l]).astype(jnp.float32)) / GATE_NORMALIZER
        qh = to_heads(q, GLA_HEADS) * (GLA_HEAD_K ** -0.5)
        kh = to_heads(k, GLA_HEADS)
        vh = to_heads(v, GLA_HEADS)
        af = to_heads(log_a_f, GLA_HEADS)
        ab = to_heads(log_a_b, GLA_HEADS)
        o_fwd = gla_chunked(qh, kh, vh, af, include_diag=True)
        o_bwd = jnp.flip(gla_chunked(jnp.flip(qh, 2), jnp.flip(kh, 2), jnp.flip(vh, 2), jnp.flip(ab, 2),
                                     include_diag=False), 2)
        o = o_fwd + o_bwd
        o = o * lax.rsqrt(jnp.mean(o * o, axis=-1, keepdims=True) + EPS)
        o = o.transpose(0, 2, 1, 3).reshape(bsz, length, GLA_VALUE_DIM) * gla_norm[l].astype(jnp.float32)
        o = (o * jax.nn.silu(r.astype(jnp.float32))).astype(x.dtype)
        y_a = o @ w_branch_gla[l]

        pooled = multiscale_pool(u)
        y_b = jnp.einsum('blgc,gcd->blgd', pooled, w_pool_group[l]).reshape(bsz, length, D_MODEL)
        y_b = (y_b * pool_scale[l]).astype(x.dtype)

        merged = jax.nn.sigmoid(g_a) * y_a + jax.nn.sigmoid(g_b) * y_b
        x = x + merged @ w_out[l]

        h2 = rmsnorm(x, norm_ffn[l])
        gate, up = jnp.split(h2 @ w_ffn_in[l], 2, axis=-1)
        x = x + (jax.nn.silu(gate) * up) @ w_ffn_out[l]
    return rmsnorm(x, norm_final)


ML_HEADS = 4
ML_QK = 64
ML_V = 128
ML_CONV = 4
ML_CHUNK = 64
MLA_HEADS = 8
MLA_NOPE = 64
MLA_ROPE = 32
MLA_V = 64
MLA_Q_RANK = 256
MLA_KV_RANK = 128
ROPE_THETA = 10000.0
Q_BLOCK = 128
D_FF_2 = 4 * D_MODEL

ML_WIDTH = ML_HEADS * ML_V
MLA_WIDTH = MLA_HEADS * MLA_V
MIX_WIDTH = ML_WIDTH + MLA_WIDTH
QK_COLS = 2 * ML_HEADS * ML_QK
GATE_COLS = 2 * ML_HEADS
IN_WIDTH_2 = QK_COLS + 2 * ML_WIDTH + GATE_COLS + MLA_Q_RANK + MLA_KV_RANK + MLA_ROPE


def rmsnorm_2(x, g):
    xf = x.astype(jnp.float32)
    y = xf * lax.rsqrt(jnp.mean(xf * xf, axis=-1, keepdims=True) + EPS)
    return (y * g.astype(jnp.float32)).astype(x.dtype)

def rope_tables(positions):
    inv = 1.0 / (ROPE_THETA ** (jnp.arange(0, MLA_ROPE, 2, dtype=jnp.float32) / MLA_ROPE))
    ang = positions.astype(jnp.float32)[..., None] * inv
    return jnp.cos(ang), jnp.sin(ang)

def apply_rope(x, cos, sin):
    xf = x.astype(jnp.float32)
    x1, x2 = jnp.split(xf, 2, axis=-1)
    return jnp.concatenate([x1 * cos - x2 * sin, x1 * sin + x2 * cos], axis=-1).astype(x.dtype)

def causal_conv(x, w, b):
    K = w.shape[0]
    S = x.shape[1]
    xp = jnp.pad(x, ((0, 0), (K - 1, 0), (0, 0)))
    return sum(xp[:, k:k + S] * w[k] for k in range(K)) + b

def mlstm_chunkwise(q, k, v, i_pre, f_pre):
    B, S, H, dk = q.shape
    dv = v.shape[-1]
    L = ML_CHUNK
    NC = S // L
    f32 = jnp.float32

    def chunk(t):
        t = t.reshape((B, NC, L, H) + t.shape[3:])
        return jnp.moveaxis(t, 3, 1)

    qc = chunk(q).astype(f32)
    kc = chunk(k).astype(f32) * (dk ** -0.5)
    vc = chunk(v).astype(f32)
    ig = chunk(i_pre).astype(f32)
    logf = jax.nn.log_sigmoid(chunk(f_pre).astype(f32))
    b = jnp.cumsum(logf, axis=-1)
    b_end = b[..., -1]

    a = b_end[..., None] - b + ig
    m_loc = jnp.max(a, axis=-1)
    w_loc = jnp.exp(a - m_loc[..., None])
    C_loc = jnp.einsum('bhcl,bhcld,bhcle->bhcde', w_loc, kc, vc)
    n_loc = jnp.einsum('bhcl,bhcld->bhcd', w_loc, kc)

    def step(carry, xs):
        C, n, m = carry
        Cl, nl, ml, bl = xs
        m_new = jnp.maximum(bl + m, ml)
        s_prev = jnp.exp(bl + m - m_new)
        s_loc = jnp.exp(ml - m_new)
        C_new = s_prev[..., None, None] * C + s_loc[..., None, None] * Cl
        n_new = s_prev[..., None] * n + s_loc[..., None] * nl
        return (C_new, n_new, m_new), (C, n, m)

    init = (jnp.zeros((B, H, dk, dv), f32), jnp.zeros((B, H, dk), f32), jnp.zeros((B, H), f32))
    xs = (jnp.moveaxis(C_loc, 2, 0), jnp.moveaxis(n_loc, 2, 0),
          jnp.moveaxis(m_loc, 2, 0), jnp.moveaxis(b_end, 2, 0))
    _, (C_prev, n_prev, m_prev) = lax.scan(step, init, xs)
    C_prev = jnp.moveaxis(C_prev, 0, 2)
    n_prev = jnp.moveaxis(n_prev, 0, 2)
    m_prev = jnp.moveaxis(m_prev, 0, 2)

    causal = jnp.tril(jnp.ones((L, L), dtype=bool))
    D = b[..., :, None] - b[..., None, :] + ig[..., None, :]
    D = jnp.where(causal, D, -jnp.inf)
    m_inter = b + m_prev[..., None]
    m_comb = jnp.maximum(jnp.max(D, axis=-1), m_inter)
    Dw = jnp.exp(D - m_comb[..., None])
    inter_w = jnp.exp(m_inter - m_comb)
    s = jnp.einsum('bhcid,bhcjd->bhcij', qc, kc) * Dw
    num = jnp.einsum('bhcij,bhcje->bhcie', s, vc) + inter_w[..., None] * jnp.einsum('bhcid,bhcde->bhcie', qc, C_prev)
    den = jnp.sum(s, axis=-1) + inter_w * jnp.einsum('bhcid,bhcd->bhci', qc, n_prev)
    h = num / jnp.maximum(jnp.abs(den), jnp.exp(-m_comb))[..., None]
    return jnp.moveaxis(h, 1, 3).reshape(B, S, H, dv)

def causal_block_attention(q, k, v):
    B, S, H, dq = q.shape
    dv = v.shape[-1]
    nb = S // Q_BLOCK
    scale = dq ** -0.5
    kf = k.astype(jnp.float32)
    vf = v.astype(jnp.float32)
    qb = jnp.transpose(q.reshape(B, nb, Q_BLOCK, H, dq), (1, 0, 3, 2, 4))
    kpos = jnp.arange(S)

    def one_block(args):
        qblk, bi = args
        sc = jnp.einsum('bhqd,bkhd->bhqk', qblk.astype(jnp.float32), kf) * scale
        qpos = bi * Q_BLOCK + jnp.arange(Q_BLOCK)
        sc = jnp.where(kpos[None, :] <= qpos[:, None], sc, -jnp.inf)
        p = jax.nn.softmax(sc, axis=-1)
        return jnp.einsum('bhqk,bkhd->bqhd', p, vf)

    out = lax.map(one_block, (qb, jnp.arange(nb)))
    return jnp.transpose(out, (1, 0, 2, 3, 4)).reshape(B, S, H * dv)

def token_mixer(a, cos, sin, w_in, b_gates, conv_w, conv_b, ml_head_norm,
                q_norm, w_uq, kv_norm, w_ukv, w_out):
    B, S, _ = a.shape
    proj = a @ w_in
    o0 = QK_COLS
    o1 = o0 + ML_WIDTH
    o2 = o1 + ML_WIDTH
    o3 = o2 + GATE_COLS
    o4 = o3 + MLA_Q_RANK
    o5 = o4 + MLA_KV_RANK
    qk_ml = proj[..., :o0]
    v_ml = proj[..., o0:o1]
    o_ml = proj[..., o1:o2]
    gates = proj[..., o2:o3] + b_gates
    c_q = proj[..., o3:o4]
    c_kv = proj[..., o4:o5]
    k_r = proj[..., o5:]

    qk_ml = jax.nn.silu(causal_conv(qk_ml, conv_w, conv_b))
    q_ml = qk_ml[..., :QK_COLS // 2].reshape(B, S, ML_HEADS, ML_QK)
    k_ml = qk_ml[..., QK_COLS // 2:].reshape(B, S, ML_HEADS, ML_QK)
    h_ml = mlstm_chunkwise(q_ml, k_ml, v_ml.reshape(B, S, ML_HEADS, ML_V),
                           gates[..., :ML_HEADS], gates[..., ML_HEADS:])
    h_ml = rmsnorm_2(h_ml, ml_head_norm.reshape(ML_HEADS, ML_V))
    h_ml = h_ml * jax.nn.sigmoid(o_ml.astype(jnp.float32)).reshape(B, S, ML_HEADS, ML_V)
    h_ml = h_ml.reshape(B, S, ML_WIDTH).astype(a.dtype)

    q = (rmsnorm_2(c_q, q_norm) @ w_uq).reshape(B, S, MLA_HEADS, MLA_NOPE + MLA_ROPE)
    q = jnp.concatenate([q[..., :MLA_NOPE],
                         apply_rope(q[..., MLA_NOPE:], cos[:, :, None, :], sin[:, :, None, :])], axis=-1)
    kv = (rmsnorm_2(c_kv, kv_norm) @ w_ukv).reshape(B, S, MLA_HEADS, MLA_NOPE + MLA_V)
    k_rope = apply_rope(k_r, cos, sin)[:, :, None, :]
    k = jnp.concatenate([kv[..., :MLA_NOPE],
                         jnp.broadcast_to(k_rope, (B, S, MLA_HEADS, MLA_ROPE))], axis=-1)
    h_mla = causal_block_attention(q, k, kv[..., MLA_NOPE:]).astype(a.dtype)

    return jnp.concatenate([h_ml, h_mla], axis=-1) @ w_out

def second_inputs(seed: int = 0) -> dict:
    key = jax.random.key(seed)
    ks = jax.random.split(key, 20)

    def nrm(k, shape, scale):
        return jax.random.normal(k, shape, jnp.float32) * scale

    def gain(k, shape):
        return 1.0 + 0.05 * jax.random.normal(k, shape, jnp.float32)

    x = nrm(ks[0], (BATCH, SEQ, D_MODEL), 1.0)
    positions = jnp.broadcast_to(jnp.arange(SEQ, dtype=jnp.int32), (BATCH, SEQ))
    b_gates = jnp.concatenate([nrm(ks[3], (DEPTH, ML_HEADS), 0.1),
                               3.0 + nrm(ks[4], (DEPTH, ML_HEADS), 0.1)], axis=-1)
    return {
        'x': x,
        'positions': positions,
        'norm_pre_mix': gain(ks[1], (DEPTH, D_MODEL)),
        'w_in': nrm(ks[2], (DEPTH, D_MODEL, IN_WIDTH_2), D_MODEL ** -0.5),
        'b_gates': b_gates,
        'conv_w': nrm(ks[5], (DEPTH, ML_CONV, QK_COLS), ML_CONV ** -0.5),
        'conv_b': nrm(ks[6], (DEPTH, QK_COLS), 0.02),
        'ml_head_norm': gain(ks[7], (DEPTH, ML_WIDTH)),
        'q_norm': gain(ks[8], (DEPTH, MLA_Q_RANK)),
        'w_uq': nrm(ks[9], (DEPTH, MLA_Q_RANK, MLA_HEADS * (MLA_NOPE + MLA_ROPE)), MLA_Q_RANK ** -0.5),
        'kv_norm': gain(ks[10], (DEPTH, MLA_KV_RANK)),
        'w_ukv': nrm(ks[11], (DEPTH, MLA_KV_RANK, MLA_HEADS * (MLA_NOPE + MLA_V)), MLA_KV_RANK ** -0.5),
        'w_out': nrm(ks[12], (DEPTH, MIX_WIDTH, D_MODEL), MIX_WIDTH ** -0.5),
        'norm_post_mix': gain(ks[13], (DEPTH, D_MODEL)),
        'norm_pre_mlp': gain(ks[14], (DEPTH, D_MODEL)),
        'w_up': nrm(ks[15], (DEPTH, D_MODEL, D_FF_2), D_MODEL ** -0.5),
        'w_down': nrm(ks[16], (DEPTH, D_FF_2, D_MODEL), D_FF_2 ** -0.5),
        'norm_post_mlp': gain(ks[17], (DEPTH, D_MODEL)),
    }

def second_block(x, positions, norm_pre_mix, w_in, b_gates, conv_w, conv_b, ml_head_norm,
              q_norm, w_uq, kv_norm, w_ukv, w_out, norm_post_mix, norm_pre_mlp,
              w_up, w_down, norm_post_mlp):
    cos, sin = rope_tables(positions)
    for l in range(DEPTH):
        a = rmsnorm_2(x, norm_pre_mix[l])
        mix = token_mixer(a, cos, sin, w_in[l], b_gates[l], conv_w[l], conv_b[l], ml_head_norm[l],
                          q_norm[l], w_uq[l], kv_norm[l], w_ukv[l], w_out[l])
        x = x + rmsnorm_2(mix, norm_post_mix[l])
        m = rmsnorm_2(x, norm_pre_mlp[l])
        y = jnp.square(jax.nn.relu(m @ w_up[l])) @ w_down[l]
        x = x + rmsnorm_2(y, norm_post_mlp[l])
    return x


def setup_inputs(seed=0):
    out = dict(first_inputs(seed))
    for name, value in second_inputs(seed + 1).items():
        if name != "x":
            out[name + "_2"] = value
    return out


def reference(
    x, norm_mix, w_in, w_decay_up_fwd, b_decay_fwd, w_decay_up_bwd, b_decay_bwd, gla_norm,
    w_branch_gla, w_pool_group, pool_scale, w_out, norm_ffn, w_ffn_in, w_ffn_out, norm_final,
    positions_2, norm_pre_mix_2, w_in_2, b_gates_2, conv_w_2, conv_b_2, ml_head_norm_2,
    q_norm_2, w_uq_2, kv_norm_2, w_ukv_2, w_out_2, norm_post_mix_2, norm_pre_mlp_2, w_up_2,
    w_down_2, norm_post_mlp_2,
):
    x = first_block(
        x, norm_mix, w_in, w_decay_up_fwd, b_decay_fwd, w_decay_up_bwd, b_decay_bwd, gla_norm,
        w_branch_gla, w_pool_group, pool_scale, w_out, norm_ffn, w_ffn_in, w_ffn_out,
        norm_final,
    )
    return second_block(
        x, positions_2, norm_pre_mix_2, w_in_2, b_gates_2, conv_w_2, conv_b_2, ml_head_norm_2,
        q_norm_2, w_uq_2, kv_norm_2, w_ukv_2, w_out_2, norm_post_mix_2, norm_pre_mlp_2, w_up_2,
        w_down_2, norm_post_mlp_2,
    )


_drawn_inputs = setup_inputs


def setup_inputs(seed=0):
    import zlib

    import numpy as np

    out = dict(_drawn_inputs(seed))
    spreads = {}
    factors = {'b_decay_fwd': 3.6,
     'b_decay_bwd': 3.493,
     'conv_b_2': 23.009,
     'q_norm_2': 6.955,
     'kv_norm_2': 4.3,
     'ml_head_norm_2': 8.0}
    for name, (base, spread) in spreads.items():
        noise = np.random.default_rng([zlib.crc32(name.encode()), seed]).standard_normal(out[name].shape)
        drawn = base * np.exp(spread * noise) if base else spread * noise
        out[name] = jnp.asarray(drawn.astype(out[name].dtype))
    for name, factor in factors.items():
        out[name] = (out[name] * factor).astype(out[name].dtype)
    return out
```

```python
from contextlib import ExitStack

import concourse.bass as bass
from concourse import mybir

ALU = mybir.AluOpType
ACT = mybir.ActivationFunctionType
AX = mybir.AxisListType
F32 = mybir.dt.float32
F32R = mybir.dt.float32r
I32 = mybir.dt.int32
BF16 = mybir.dt.bfloat16

P = 128
D = 1024
T = 1024
KT = D // P
HALF = 512
EPS = 1e-6
GH = 4
C = T // P
D_FF = 2816
D_FF2 = 4096
BIG = 3.0e38

VEC_ROWS = [("norm_mix", 8), ("gla_norm", 8), ("pool_scale", 8), ("norm_ffn", 8), ("norm_final", 8),
            ("norm_pre_mix_2", 8), ("norm_post_mix_2", 8), ("norm_pre_mlp_2", 8),
            ("norm_post_mlp_2", 8), ("b_decay_fwd", 4), ("b_decay_bwd", 4), ("conv_w_2", 16),
            ("conv_b_2", 4), ("ml_head_norm_2", 4), ("q_norm_2", 2), ("kv_norm_2", 1)]
VEC = {}
NVEC = 0
for _name, _n in VEC_ROWS:
    VEC[_name] = NVEC
    NVEC += _n

G = 4
F1 = D_FF // P
F2 = D_FF2 // P
G1 = [G] * (F1 // G) + ([F1 % G] if F1 % G else [])
G2 = [G] * (F2 // G)
U_IN = 0
N_IN = 45
U_YA = U_IN + N_IN
U_WO = U_YA + KT
U_F1 = U_WO + KT
N_F1 = 2 * F1 + KT * len(G1)
U_IN2 = U_F1 + N_F1
N_IN2 = 17
U_QKV = U_IN2 + N_IN2
U_WO2 = U_QKV + 16
U_F2 = U_WO2 + KT
N_F2 = F2 + KT * len(G2)
U_END = U_F2 + N_F2

NORMS = [("mix", 8), ("ffn", 8), ("final", 8), ("mix2", 8), ("cq", 2), ("ckv", 1), ("post_mix", 8),
         ("mlp", 8), ("post_mlp", 8)]
NORM_AT = {}
SQ_BASE = {}
_b = 0
for _i, (_name, _n) in enumerate(NORMS):
    NORM_AT[_name] = _i
    SQ_BASE[_name] = _b
    _b += _n

THREE = {U_IN2 + 16} | {U_QKV + 2 * h for h in range(8)}
LANDED = []
_c = [0, 0]
for _u in range(U_END):
    _c[_u % 2] += 48 if _u in THREE else 16
    LANDED.append(_c[_u % 2])


def par(u):
    return u % 2


def nth(u):
    return u // 2 + 1


class Step:

    def __init__(self, c, s=0, i=0):
        self.c, self.s, self.i = c, s, i

    def __add__(self, k):
        return Step(self.c + k, self.s, self.i)

    def times(self, m, plus=0):
        v = self.c * m + plus
        return self.i * (self.s * m) + v if self.s else v

    @property
    def par(self):
        return self.c % 2

    def nth(self, plus=0):
        v = self.c // 2 + 1 + plus
        return self.i * (self.s // 2) + v if self.s else v

    def landed(self):
        return self.i * (8 * self.s) + LANDED[self.c] if self.s else LANDED[self.c]


SEMS = ("h_neg p_norm pt_out w_hi w_split unit_done sq_done sq_added norm_sum norm_mean rstd_ready hi_ready lo_ready "
        "consts_ready x_loaded vec_loaded vec_t xt_tr cols_ready xt_ev x_spilled gla_loaded "
        "qk_loaded v_loaded r_loaded wup_zero z_ready vt_ready sc_ready kdt_ready kv_ready "
        "o_ready o_sum o_stored z_log vtok_ready e_ready sc_fwd kdtok_ready osq_ready r_silu o_rstd o_hi "
        "rmask_ready z_min la_ready b_step dec_ready qk_weighted sc_tile state_step o_norm o_gate "
        "o_lo wpool_loaded u_loaded yb_ready gates_sig merged_hi pool_consts pool_step "
        "pooled_ready merged_lo yb_scaled merged_ready gate_silu act_hi act_full act_lo fin_done "
        "mla_loaded latent_hi rope_sin kr_copied vh_tok p_ready mixa_hi ang_step "
        "latent_lo rope_ready kr_part kr_rope csq_ready q_a q_rope rs_inv mixa_lo s_stat "
        "vh_t s_ready pt_ready pv_ready gates_loaded conv_loaded mv_loaded om_loaded "
        "f_log conv_silu am_cols mv_tok om_sig st_exp h_sq h_rstd mixm_hi ml_consts w_ready "
        "m_step g_step conv_step st_e st_w h_step mixm_lo am_t mv_t st_ready ho_ready ht_t "
        "y_scaled x_added up_sq sq_hi sq_lo acc_zero out_t out_ev").split()
PAIRED = ("o_back gab_loaded out_stored r_bc_loaded r_stored stored unit_out w_landed x_back").split()


def two_block_kernel(nc, A, out):
    ctx = ExitStack()

    def dram(name, shape):
        return nc.dram_tensor(name, shape, F32, kind="Internal").ap()

    x_in = A["x"][0]
    w_in = A["w_in"][0].rearrange("(k p) n -> p k n", p=P)
    w_ya = A["w_branch_gla"][0].rearrange("(k p) n -> p k n", p=P)
    w_out = A["w_out"][0].rearrange("(k p) n -> p k n", p=P)
    w_f1 = A["w_ffn_in"][0].rearrange("(k p) n -> p k n", p=P)
    w_f1o = A["w_ffn_out"][0].rearrange("(k p) n -> p k n", p=P)
    w_in2 = A["w_in_2"][0].rearrange("(k p) n -> p k n", p=P)
    w_uq = A["w_uq_2"][0].rearrange("(k p) n -> p k n", p=P)
    w_ukv = A["w_ukv_2"][0].rearrange("(k p) n -> p k n", p=P)
    w_out2 = A["w_out_2"][0].rearrange("(k p) n -> p k n", p=P)
    w_up = A["w_up_2"][0].rearrange("(k p) n -> p k n", p=P)
    w_down = A["w_down_2"][0].rearrange("(k p) n -> p k n", p=P)

    proj = dram("proj", (N_IN * P, T))
    proj2 = dram("proj2", (N_IN2 * P, T))
    o_d = dram("gla_out", (D, T))
    x_d = dram("x_feature_major", (D, T))
    x2_d = dram("x_block2", (D, T))
    x3_d = dram("x_after_mixer2", (D, T))
    r_d = dram("mlstm_log_weights", (C * 4, T))

    def tile_of(t, j, n=1):
        return t[j * P:(j + n) * P, :].rearrange("(k p) t -> p k t", p=P)

    with ctx:
        def sb(name, shape, dt=F32, c=ctx):
            return c.enter_context(nc.sbuf_tensor(name, shape, dt))

        S = {n: ctx.enter_context(nc.semaphore(n)) for n in SEMS}
        for n in PAIRED:
            S[n] = [ctx.enter_context(nc.semaphore(f"{n}{i}")) for i in range(2)]

        PS = [ctx.enter_context(nc.psum_tensor(f"ps{i}", [P, T], F32)) for i in range(4)]

        acc = sb("acc", [P, KT, T])
        raw = sb("w_raw", [P, 2, KT * P])
        whi = sb("w_hi_t", [P, 2, KT * P], F32R)
        wlo = sb("w_lo_t", [P, 2, KT * P], F32R)
        stage = sb("stage", [P, 2, T])
        ssq = sb("ssq", [P, T])
        rstd = sb("rstd", [P, T])
        ident = sb("ident", [P, P])
        ones = sb("ones", [P, P])
        maskb = sb("maskb", [P, P])
        ident16 = sb("ident16", [P, P], BF16)
        negm16 = sb("negm16", [P, P], BF16)
        cols = sb("cols", [P, NVEC])
        small = sb("small", [P, 64])

        def col(name, k):
            return cols[:, VEC[name] + k:VEC[name] + k + 1]

        with ExitStack() as s:
            vtok = sb("vtok", [P, C, 256], F32, s)
            sct = sb("sct", [P, C, P], F32, s)
            St = sb("states", [P, 2, C, 256], F32, s)
            qi = sb("qi", [P, 2, T], F32, s)
            qs = sb("qs", [P, T], F32, s)
            ks = sb("ks", [P, T], F32, s)
            lt = sb("lt", [P, T], F32, s)
            kdtok = sb("kdtok", [P, C, P], F32, s)
            bt = sb("bt", [P, T], F32, s)
            kd = sb("kd", [P, T], F32, s)
            mn = sb("mn", [P, T], F32, s)
            wup = sb("wup", [32, 2, HALF], F32, s)
            with ExitStack() as s2:
                xin = sb("xin", [P, C, T], F32, s2)
                vrow = sb("vrow", [P, P], F32, s2)
            with ExitStack() as s2:
                h1hi = sb("h1hi", [P, KT, T], F32R, s2)
                h1lo = sb("h1lo", [P, KT, T], F32R, s2)
        s_m2 = ExitStack()
        m2hi = sb("m2hi", [P, KT, T], F32R, s_m2)
        m2lo = sb("m2lo", [P, KT, T], F32R, s_m2)
        with ExitStack() as s:
            oback = sb("oback", [P, KT, T], F32, s)
        with ExitStack() as s:
            m1hi = sb("m1hi", [P, KT, T], F32R, s)
            m1lo = sb("m1lo", [P, KT, T], F32R, s)
            wpool = sb("wpool", [P, 4, 256], F32, s)
        with ExitStack() as s:
            g1hi = sb("g1hi", [P, KT, T], F32R, s)
            g1lo = sb("g1lo", [P, KT, T], F32R, s)
        with ExitStack() as s:
            kT = sb("kT", [P, 8, T], F32, s)
            Vt = sb("Vt", [P, C, 8, 64], F32, s)
            x4 = sb("x4", [P, 4, T], F32, s)
        with ExitStack() as s:
            qk = sb("qk", [P, 4, T], F32, s)
            Wt = sb("Wt", [P, C, T], F32, s)
            vaug = sb("vaug", [P, C, 130], F32, s)
            cb = sb("cb", [P, T + 4], F32, s)
            hq = sb("hq", [P, C, P], F32, s)
        s_m2.close()
        with ExitStack() as s:
            xr = sb("xr", [P, KT, T], F32, s)
            orow = sb("orow", [P, 2, T], F32, s)
        with ExitStack() as s:
            a2hi = sb("a2hi", [P, KT, T], F32R, s)
            a2lo = sb("a2lo", [P, KT, T], F32R, s)
            h3hi = sb("h3hi", [P, KT, T], F32R, s)
            h3lo = sb("h3lo", [P, KT, T], F32R, s)

        gq, gk, gv, gr = acc[:, 0, :], acc[:, 1, :], acc[:, 2:4, :], acc[:, 4:6, :]
        rmask, bm = acc[:, 6, :], acc[:, 7, :]
        bg = small[0:4, 0:2]
        z32 = small[:, 2:34]
        lrT = ssq[0:32, :]
        block = ctx.enter_context(nc.Block())


        def load_unit(sp, u, src, nk=KT, parts=None):
            if u.c >= 2:
                sp.wait_ge(S["w_split"], u.times(1, -1))
            dst = raw[:, u.par, 0:nk * P].rearrange("p (k c) -> p k c", k=nk)
            for (a, b, s_) in parts or [(0, P, src)]:
                sp.dma_start(dst[:, :, a:b], s_).then_inc(S["w_landed"][u.par], 16)

        def split_unit(pool, u, nk=KT):
            n = nk * P
            r, h, lo = raw[:, u.par, 0:n], whi[:, u.par, 0:n], wlo[:, u.par, 0:n]
            pool.wait_ge(S["w_landed"][u.par], u.landed())
            if u.c >= 2:
                pool.wait_ge(S["unit_done"], u.times(1, -1))
            pool.tensor_tensor(h, r, ones[:, 0:1].to_broadcast([P, n]), ALU.mult).then_inc(S["w_hi"], 1)
            pool.wait_ge(S["w_hi"], u.times(1, 1))
            pool.tensor_tensor(lo, r, h.bitcast(F32), ALU.subtract).then_inc(S["w_split"], 1)

        def mm_unit(pe, u, xhi, xlo, nk=KT, wait_k=None, pair=None):
            pe.wait_ge(S["w_split"], u.times(1, 1))
            if pair is not None:
                pe.wait_ge(S["unit_out"][(u.c - 1) % 2], nth(u.c - 1))
            elif u.c >= 2:
                pe.wait_ge(S["unit_out"][u.par], u.nth(-1))
            out = PS[u.par if pair is None else pair]
            for k in range(nk):
                if wait_k:
                    wait_k(k)
                w_h = whi[:, u.par, k * P:(k + 1) * P]
                w_l = wlo[:, u.par, k * P:(k + 1) * P]
                for n, (w, x) in enumerate(((w_h, xhi), (w_h, xlo), (w_l, xhi))):
                    for b in range(2):
                        mm = pe.matmul(out[:, b * HALF:(b + 1) * HALF], w,
                                       x[:, k, b * HALF:(b + 1) * HALF],
                                       start=(k == 0 and n == 0), stop=(k == nk - 1 and n == 2))
            mm.then_inc(S["unit_done"], 1)


        def norm_square(act, name, k, src):
            m = SQ_BASE[name] + k
            if m >= 2:
                act.wait_ge(S["sq_added"], m - 1)
            act.activation(stage[:, m % 2, :], src, ACT.Square).then_inc(S["sq_done"], 1)

        def norm_add(dve, name, k):
            m = SQ_BASE[name] + k
            n = NORM_AT[name]
            dve.wait_ge(S["sq_done"], m + 1)
            if k == 0:
                if n:
                    dve.wait_ge(S["rstd_ready"], n)
                dve.tensor_copy(ssq[:, :], stage[:, m % 2, :]).then_inc(S["sq_added"], 1)
            else:
                dve.wait_ge(S["sq_added"], m)
                dve.tensor_tensor(ssq[:, :], ssq[:, :], stage[:, m % 2, :], ALU.add)\
                   .then_inc(S["sq_added"], 1)

        def norm_sum(pe, name, nk):
            pe.wait_ge(S["sq_added"], SQ_BASE[name] + nk)
            for b in range(2):
                mm = pe.matmul(PS[2][:, b * HALF:(b + 1) * HALF], ones[:, :],
                               ssq[:, b * HALF:(b + 1) * HALF], start=True, stop=True)
            mm.then_inc(S["norm_sum"], 1)

        def norm_mean(dve, name, nk):
            n = NORM_AT[name] + 1
            dve.wait_ge(S["norm_sum"], n)
            dve.tensor_scalar(ssq[:, :], PS[2][:, :], 1.0 / (nk * P), EPS, ALU.mult, ALU.add)\
               .then_inc(S["norm_mean"], 1)
            dve.wait_ge(S["norm_mean"], 2 * n - 1)
            dve.reciprocal(ssq[:, :], ssq[:, :]).then_inc(S["norm_mean"], 1)

        def norm_root(act, name, dst):
            act.wait_ge(S["norm_mean"], 2 * (NORM_AT[name] + 1))
            act.activation(dst, ssq[:, :], ACT.Sqrt).then_inc(S["rstd_ready"], 1)

        def scale_hi(act, k, src, g, hi):
            act.activation(hi[:, k, :], src, ACT.Copy, scale=g).then_inc(S["hi_ready"], 1)

        def scale_lo(dve, at, k, src, g, hi, lo):
            dve.wait_ge(S["hi_ready"], at + k + 1)
            dve.scalar_tensor_tensor(out=lo[:, k, :], in0=src, scalar=g, in1=hi[:, k, :].bitcast(F32),
                                     op0=ALU.mult, op1=ALU.subtract).then_inc(S["lo_ready"], 1)

        OPERAND = {"mix": 0, "ffn": 8, "mix2": 16, "mlp": 24}

        def norm_act(act, name, ready, g=None, hi=None, src=acc, nk=KT, dst=rstd):
            for k in range(nk):
                ready(act, k)
                if hi is not None:
                    scale_hi(act, k, src[:, k, :], col(g, k), hi)
                norm_square(act, name, k, src[:, k, :])
            norm_root(act, name, dst[:, :])

        def norm_dve(dve, name, ready, g=None, hi=None, lo=None, src=acc, nk=KT):
            for k in range(nk):
                if hi is not None:
                    scale_lo(dve, OPERAND[name], k, src[:, k, :], col(g, k), hi, lo)
                norm_add(dve, name, k)
            norm_mean(dve, name, nk)

        def lo_wait(pe, name):
            return lambda k: pe.wait_ge(S["lo_ready"], OPERAND[name] + k + 1)

        def no_wait(eng, k):
            pass

        def stores_before(u, first, before):
            f = first if first % 2 == u.par else first + 1
            return u.nth(-(f // 2 + 1) + before[u.par])

        def store_dve(dve, u, first, before, pair=None):
            dve.wait_ge(S["unit_done"], u.times(1, 1))
            if not (u.s == 0 and stores_before(u, first, before) == 0):
                v = stores_before(u, first, before)
                dve.wait_ge(S["stored"][u.par], v * 16)
            dve.tensor_tensor(stage[:, u.par, :], PS[u.par if pair is None else pair][:, :], rstd[:, :],
                              ALU.mult).then_inc(S["unit_out"][u.par], 1)

        def store_act(act, u, dst):
            act.wait_ge(S["unit_out"][u.par], u.nth())
            act.dma_start(dst, stage[:, u.par, :]).then_inc(S["stored"][u.par], 16)

        ALL_IN = (16 * ((N_IN + 1) // 2), 16 * (N_IN // 2))
        B2 = ((N_IN + 1) // 2, N_IN // 2)
        N0_IN2 = sum((U_IN2 + j) % 2 == 0 for j in range(N_IN2))
        ALL_IN2 = (ALL_IN[0] + 16 * N0_IN2, ALL_IN[1] + 16 * (N_IN2 - N0_IN2))

        def all_stored(eng, counts):
            for i in range(2):
                eng.wait_ge(S["stored"][i], counts[i])

        def ffn_order(groups, per_tile, u0, name):
            order = [("in", 0)]
            for g in range(1, len(groups)):
                order += [("in", g), ("out", g - 1)]
            order.append(("out", len(groups) - 1))
            seg, u = [], u0
            for kind, g in order:
                seg.append((kind, g, u))
                u += per_tile * groups[g] if kind == "in" else KT
            return seg

        SEG1 = ffn_order(G1, 2, U_F1, "f1")
        SEG2 = ffn_order(G2, 1, U_F2, "f2")

        def run_ffn(eng, seg, groups, per_tile, do):
            full = sum(g == G for g in groups)
            loops = (full - 1) // 2
            stride = 2 * (per_tile * G + KT)
            do(eng, seg[0][0], Step(0), Step(seg[0][2]), G)
            with eng.Fori(0, loops) as i:
                for kind, g, u in seg[1:5]:
                    do(eng, kind, Step(g, 2, i), Step(u, stride, i), G)
            for kind, g, u in seg[1 + 4 * loops:]:
                do(eng, kind, Step(g), Step(u), groups[g])

        N_CONST = 9

        def start_pool(pool):
            pool.memset(ident[:, :], 0.0).then_inc(S["consts_ready"], 1)
            pool.memset(ones[:, :], 1.0).then_inc(S["consts_ready"], 1)
            pool.memset(maskb[:, :], 1.0).then_inc(S["consts_ready"], 1)
            pool.memset(negm16[:, :], 0.0).then_inc(S["consts_ready"], 1)
            pool.memset(ident16[:, :], 0.0).then_inc(S["consts_ready"], 1)
            pool.wait_ge(S["consts_ready"], 5)
            pool.affine_select(out=ident[:, :], in_=ident[:, :], compare_op=ALU.not_equal, fill=1.0, base=0,
                               pattern=[[-1, P]], channel_multiplier=1).then_inc(S["consts_ready"], 1)
            pool.affine_select(out=maskb[:, :], in_=maskb[:, :], compare_op=ALU.is_gt, fill=0.0, base=0,
                               pattern=[[-1, P]], channel_multiplier=1).then_inc(S["consts_ready"], 1)
            pool.affine_select(out=negm16[:, :], in_=negm16[:, :], compare_op=ALU.is_ge, fill=-BIG, base=0,
                               pattern=[[-1, P]], channel_multiplier=1).then_inc(S["consts_ready"], 1)
            pool.affine_select(out=ident16[:, :], in_=ident16[:, :], compare_op=ALU.not_equal, fill=1.0, base=0,
                               pattern=[[-1, P]], channel_multiplier=1).then_inc(S["consts_ready"], 1)

        def start_sp(sp):
            for h in range(2):
                sp.dma_start(xin[:, 4 * h:4 * h + 4, :],
                             x_in[4 * h * P:(4 * h + 4) * P, :].rearrange("(c p) d -> p c d", p=P))\
                  .then_inc(S["x_loaded"], 16)
            for name, n in VEC_ROWS:
                v = A[name][0] if len(A[name].shape) > 1 else A[name]
                if len(v.shape) == 2:
                    v = v.rearrange("a n -> (a n)")
                sp.dma_start(vrow[VEC[name]:VEC[name] + n, :], v.rearrange("(k p) -> k p", p=P))\
                  .then_inc(S["vec_loaded"], 16)

        def start_pe(pe):
            pe.wait_ge(S["consts_ready"], N_CONST)
            pe.wait_ge(S["vec_loaded"], 16 * len(VEC_ROWS))
            pe.transpose(PS[2][:, 0:NVEC], vrow[0:NVEC, :], ident[0:NVEC, 0:NVEC]).then_inc(S["vec_t"], 1)
            pe.wait_ge(S["x_loaded"], 32)
            for h in range(2):
                for k in range(KT):
                    n = h * KT + k
                    if n >= 4:
                        pe.wait_ge(S["xt_ev"], n - 3)
                    bank = PS[n % 4 // 2][:, n % 2 * HALF:n % 2 * HALF + HALF]
                    for c in range(4):
                        tr = pe.transpose(bank[:, c * P:(c + 1) * P],
                                          xin[:, 4 * h + c, k * P:(k + 1) * P], ident[:, :])
                    tr.then_inc(S["xt_tr"], 1)

        def start_act(act):
            act.wait_ge(S["vec_t"], 1)
            act.activation(cols[:, :], PS[2][:, 0:NVEC], ACT.Copy).then_inc(S["cols_ready"], 1)
            for h in range(2):
                for k in range(KT):
                    n = h * KT + k
                    act.wait_ge(S["xt_tr"], n + 1)
                    act.activation(acc[:, k, h * HALF:(h + 1) * HALF],
                                   PS[n % 4 // 2][:, n % 2 * HALF:n % 2 * HALF + HALF], ACT.Copy)\
                       .then_inc(S["xt_ev"], 1)
            act.wait_ge(S["xt_ev"], 2 * KT)
            act.dma_start(tile_of(x_d, 0, KT), acc[:, :, :]).then_inc(S["x_spilled"], 16)
            act.wait_ge(S["cols_ready"], 1)

        LR0 = 3072
        REST0 = LR0 + 32

        def in_steps(eng, do):
            for j in range(2):
                do(eng, Step(j), j * P, j)
            with eng.Fori(0, 11) as i:
                for j in range(2):
                    do(eng, Step(2 + j, 2, i), i * (2 * P) + (2 + j) * P, None, i * (2 * P) + (2 + j) * P)
            do(eng, Step(24), LR0, 24)

        def in_sp(sp):
            def do(e, u, c0, j, r0=None):
                load_unit(e, u, w_in[:, :, bass.ds(c0, P)] if j is None else w_in[:, :, c0:c0 + P])
            in_steps(sp, do)

        def in_pool(pool):
            in_steps(pool, lambda e, u, c0, j, r0=None: split_unit(e, u))

        def in_pe(pe):
            def do(e, u, c0, j, r0=None):
                first = j == 0
                mm_unit(e, u, h1hi, h1lo, wait_k=lo_wait(e, "mix") if first else None)
                if first:
                    norm_sum(e, "mix", KT)
            in_steps(pe, do)

        def in_act(act):
            def do(e, u, c0, j, r0=None):
                store_act(e, u, proj[bass.ds(r0, P), :] if j is None else proj[j * P:(j + 1) * P, :])
            in_steps(act, do)

        def in_dve(dve):
            dve.wait_ge(S["rstd_ready"], NORM_AT["mix"] + 1)
            in_steps(dve, lambda e, u, c0, j, r0=None: store_dve(e, u, 0, (0, 0)))

        NORM16 = 1.0 / 16.0
        QSCALE = float(P) ** -0.5
        MID, END = (63, 64), (P - 1, 0)
        Ering = [lt[:, :], mn[:, :]]
        MID0 = 25
        MIDS = (N_IN - MID0) // GH

        def order(d):
            return list(range(C)) if d == 0 else list(range(C - 1, -1, -1))

        def mid_weights(sp, u):
            c0 = REST0 + (u - MID0) * P
            if u < N_IN:
                load_unit(sp, Step(u), w_in[:, :, c0:c0 + P])
            else:
                ya_wo_unit(sp, u - N_IN)

        def gla_sp(sp):
            for u in (MID0, MID0 + 1):
                mid_weights(sp, u)
            sp.wait_ge(S["x_spilled"], 16)
            for i in range(2):
                sp.wait_ge(S["stored"][i], 16 * ((MID0 + 1 - i) // 2))
            sp.dma_start(lrT, proj[24 * P:24 * P + 32, :]).then_inc(S["gla_loaded"], 16)

            def qkv(h):
                if h:
                    sp.wait_ge(S["qk_weighted"], 8 * h)
                sp.dma_start(gq, proj[h * P:(h + 1) * P, :]).then_inc(S["qk_loaded"], 16)
                sp.dma_start(gk, proj[(4 + h) * P:(5 + h) * P, :]).then_inc(S["qk_loaded"], 16)
                if h:
                    sp.wait_ge(S["vt_ready"], 2 * h)
                sp.dma_start(gv, tile_of(proj, 8 + 2 * h, 2)).then_inc(S["v_loaded"], 16)

            def gate(h):
                if h:
                    sp.wait_ge(S["o_gate"], 4 * h)
                sp.dma_start(gr, tile_of(proj, 16 + 2 * h, 2)).then_inc(S["r_loaded"], 16)

            qkv(0)
            gate(0)
            for h in range(GH):
                for i in range(MIDS):
                    u = Step(MID0 + MIDS * h + i)
                    sp.wait_ge(S["unit_out"][u.par], u.nth())
                    sp.dma_start(proj[u.c * P:(u.c + 1) * P, :], stage[:, u.par, :])\
                      .then_inc(S["stored"][u.par], 16)
                    mid_weights(sp, u.c + 2)
                    if i == 2 and h < GH - 1:
                        qkv(h + 1)
                if h < GH - 1:
                    gate(h + 1)

        def mid_pool(pool):
            for u in range(MID0, N_IN):
                split_unit(pool, Step(u))

        def wup_pool(pool):
            pool.memset(wup[:, :, :], 0.0).then_inc(S["wup_zero"], 1)

        def wup_sp(sp):
            sp.wait_ge(S["wup_zero"], 1)
            sp.dma_start(wup[0:16, 0, :], A["w_decay_up_fwd"][0]).then_inc(S["gla_loaded"], 16)
            sp.dma_start(wup[16:32, 1, :], A["w_decay_up_bwd"][0]).then_inc(S["gla_loaded"], 16)

        def gla_pe(pe):
            pe.wait_ge(S["gla_loaded"], 48)
            pe.wait_ge(S["unit_out"][1], MID0 // 2)

            def z(h, d):
                if d == 0 and h:
                    pe.wait_ge(S["o_norm"], 3 * h - 1)
                if d == 1:
                    pe.wait_ge(S["sc_fwd"], h + 1)
                for b in range(2):
                    mm = pe.matmul(PS[3 - 2 * d][:, b * HALF:(b + 1) * HALF], wup[:, d, h * P:(h + 1) * P],
                                   lrT[:, b * HALF:(b + 1) * HALF], start=True, stop=True)
                mm.then_inc(S["z_ready"], 1)

            def turn_v(h):
                pe.wait_ge(S["v_loaded"], 16 * (h + 1))
                if h:
                    pe.wait_ge(S["o_gate"], 4 * h - 1)
                for half in range(2):
                    if half:
                        pe.wait_ge(S["z_min"], 2 * h + 1)
                        pe.wait_ge(S["z_log"], 6 * h + 1)
                    for c in range(4):
                        for e in range(2):
                            tr = pe.transpose(PS[2 + half][:, c * 256 + e * P:c * 256 + (e + 1) * P],
                                              gv[:, e, (4 * half + c) * P:(4 * half + c + 1) * P], ident[:, :])
                    tr.then_inc(S["vt_ready"], 1)

            def scores(h, d):
                n = 2 * h + d
                pe.wait_ge(S["qk_weighted"], 4 * n + 3)
                if d == 0 and h:
                    pe.wait_ge(S["o_gate"], 4 * h - 3)
                if d == 1:
                    pe.wait_ge(S["z_min"], n + 1)
                    pe.wait_ge(S["z_log"], 3 * n + 1)
                for c in range(C):
                    mm = pe.matmul(PS[1][:, c * P:(c + 1) * P], ks[:, c * P:(c + 1) * P],
                                   qs[:, c * P:(c + 1) * P], start=True, stop=True)
                mm.then_inc(S["sc_ready"], 1)

            def turn_k(h, d):
                n = 2 * h + d
                pe.wait_ge(S["qk_weighted"], 4 * n + 4)
                pe.wait_ge(S["vtok_ready"], 2 * h + 2)
                if n:
                    pe.wait_ge(S["state_step"], 7 * n)
                for c in range(C):
                    tr = pe.transpose(PS[2][:, c * P:(c + 1) * P], kd[:, c * P:(c + 1) * P], ident[:, :])
                tr.then_inc(S["kdt_ready"], 1)

            def keys_values(h, d):
                pe.wait_ge(S["kdtok_ready"], 2 * h + d + 1)
                for i, c in enumerate(order(d)[:C - 1]):
                    mm = pe.matmul(PS[3 - i // 4][:, i % 4 * 256:(i % 4 + 1) * 256], kdtok[:, c, :],
                                   vtok[:, c, :], start=True, stop=True)
                    if i == 3:
                        mm.then_inc(S["kv_ready"], 1)
                mm.then_inc(S["kv_ready"], 1)

            def output(h):
                pe.wait_ge(S["sc_tile"], h + 1)
                pe.wait_ge(S["state_step"], 14 * h + 14)
                pe.wait_ge(S["qk_weighted"], 8 * h + 5)
                for e in range(2):
                    for c in range(C):
                        o = PS[1 + e][:, c * P:(c + 1) * P]
                        terms = [(vtok[:, c, e * P:(e + 1) * P], sct[:, c, :])]
                        if c > 0:
                            terms.append((St[:, 0, c, e * P:(e + 1) * P], qi[:, 0, c * P:(c + 1) * P]))
                        if c < C - 1:
                            terms.append((St[:, 1, c, e * P:(e + 1) * P], qi[:, 1, c * P:(c + 1) * P]))
                        for i, (w, x) in enumerate(terms):
                            mm = pe.matmul(o, w, x, start=(i == 0), stop=(i == len(terms) - 1))
                    mm.then_inc(S["o_ready"], 1)

            def square_sum(h):
                pe.wait_ge(S["o_norm"], 3 * h + 1)
                for b in range(2):
                    mm = pe.matmul(PS[3][:, b * HALF:(b + 1) * HALF], ones[:, :],
                                   mn[:, b * HALF:(b + 1) * HALF], start=True, stop=True)
                mm.then_inc(S["o_sum"], 1)

            def mid_unit(h, i):
                mm_unit(pe, Step(MID0 + MIDS * h + i), h1hi, h1lo, pair=0)

            for h in range(GH):
                z(h, 0)
                mid_unit(h, 0)
                turn_v(h)
                scores(h, 0)
                turn_k(h, 0)
                z(h, 1)
                keys_values(h, 0)
                mid_unit(h, 1)
                mid_unit(h, 2)
                scores(h, 1)
                turn_k(h, 1)
                keys_values(h, 1)
                mid_unit(h, 3)
                output(h)
                mid_unit(h, 4)
                square_sum(h)

        def gla_act(act):
            def store_o(h):
                for e in range(2):
                    act.wait_ge(S["o_gate"], 2 * (2 * h + e + 1))
                    act.dma_start(o_d[(2 * h + e) * P:(2 * h + e + 1) * P, :], (kd if e == 0 else bt)[:, :])\
                       .then_inc(S["o_stored"], 16)

            for h in range(GH):
                for d in range(2):
                    n = 2 * h + d
                    bias = col("b_decay_bwd" if d else "b_decay_fwd", h)
                    act.wait_ge(S["z_ready"], n + 1)
                    if n:
                        act.wait_ge(S["qk_weighted"], 4 * n - 1)
                    act.activation(lt[:, :], PS[3 - 2 * d][:, :], ACT.Abs, bias=bias).then_inc(S["z_log"], 1)
                    act.wait_ge(S["z_log"], 3 * n + 1)
                    act.activation(lt[:, :], lt[:, :], ACT.Exp, scale=-1.0).then_inc(S["z_log"], 1)
                    act.wait_ge(S["z_log"], 3 * n + 2)
                    act.activation(lt[:, :], lt[:, :], ACT.Ln, bias=1.0).then_inc(S["z_log"], 1)
                    if d == 0 and h:
                        store_o(h - 1)
                    for i, (ready, src, scale) in enumerate(
                            ((1, bt, NORM16), (2, bm, NORM16), (2, bm, -NORM16), (3, bm, NORM16))):
                        m = 4 * n + i
                        act.wait_ge(S["b_step"], 3 * n + ready)
                        if m >= 2:
                            act.wait_ge(S["qk_weighted"], m - 1)
                        act.activation(Ering[m % 2], src[:, :], ACT.Exp, scale=scale).then_inc(S["e_ready"], 1)
                    if d == 0:
                        for half in range(2):
                            act.wait_ge(S["vt_ready"], 2 * h + half + 1)
                            if h:
                                act.wait_ge(S["o_ready"], 2 * h)
                            act.activation(vtok[:, 4 * half:4 * half + 4, :],
                                           PS[2 + half][:, :].rearrange("p (c e) -> p c e", c=4), ACT.Copy)\
                               .then_inc(S["vtok_ready"], 1)
                    if d == 0:
                        act.wait_ge(S["sc_ready"], n + 1)
                        if h:
                            act.wait_ge(S["o_ready"], 2 * h)
                        act.activation(sct[:, :, :], PS[1][:, :].rearrange("p (c s) -> p c s", c=C), ACT.Copy)\
                           .then_inc(S["sc_fwd"], 1)
                    act.wait_ge(S["kdt_ready"], n + 1)
                    if n:
                        act.wait_ge(S["kv_ready"], 2 * n)
                    act.activation(kdtok[:, :, :], PS[2][:, :].rearrange("p (c s) -> p c s", c=C), ACT.Copy)\
                       .then_inc(S["kdtok_ready"], 1)
                for e in range(2):
                    act.wait_ge(S["o_ready"], 2 * h + e + 1)
                    act.activation((qs if e == 0 else ks)[:, :], PS[1 + e][:, :], ACT.Square)\
                       .then_inc(S["osq_ready"], 1)
                act.wait_ge(S["r_loaded"], 16 * (h + 1))
                act.activation(gr, gr, ACT.Silu).then_inc(S["r_silu"], 1)
                act.wait_ge(S["o_norm"], 3 * h + 3)
                act.activation(mn[:, :], mn[:, :], ACT.Sqrt).then_inc(S["o_rstd"], 1)
            store_o(GH - 1)

        def gla_dve(dve):
            dve.wait_ge(S["x_spilled"], 16)
            dve.memset(rmask, 1.0).then_inc(S["rmask_ready"], 1)
            dve.wait_ge(S["rmask_ready"], 1)
            r3 = rmask.rearrange("p (c t) -> p c t", c=C)
            dve.memset(r3[:, :, 0:1], 0.0).then_inc(S["rmask_ready"], 1)
            dve.wait_ge(S["rmask_ready"], 2)
            dve.wait_ge(S["cols_ready"], 1)

            def evacuate(h, i):
                store_dve(dve, Step(MID0 + MIDS * h + i), 0, (0, 0), pair=0)

            for h in range(GH):
                for d in range(2):
                    n = 2 * h + d
                    bias = col("b_decay_bwd" if d else "b_decay_fwd", h)
                    dve.wait_ge(S["z_log"], 3 * n + 1)
                    if n:
                        dve.wait_ge(S["qk_weighted"], 4 * n)
                    if h and d == 0:
                        dve.wait_ge(S["o_gate"], 4 * h)
                    dve.tensor_scalar(mn[:, :], PS[3 - 2 * d][:, :], bias, 0.0, ALU.add, ALU.min)\
                       .then_inc(S["z_min"], 1)
                    dve.wait_ge(S["z_log"], 3 * n + 3)
                    dve.wait_ge(S["z_min"], n + 1)
                    dve.tensor_tensor(mn[:, :], mn[:, :], lt[:, :], ALU.subtract).then_inc(S["la_ready"], 1)
                    dve.wait_ge(S["la_ready"], n + 1)
                    if n:
                        dve.wait_ge(S["e_ready"], 4 * n)
                    if h and d == 0:
                        dve.wait_ge(S["o_stored"], 32 * h)
                    st = slice(None) if d == 0 else slice(None, None, -1)
                    dve.tensor_tensor_scan(bt[:, st], rmask, mn[:, st], 0.0, ALU.mult, ALU.add)\
                       .then_inc(S["b_step"], 1)
                    dve.wait_ge(S["b_step"], 3 * n + 1)
                    b3 = bt[:, :].rearrange("p (c t) -> p c t", c=C)
                    bm3 = bm.rearrange("p (c t) -> p c t", c=C)
                    dve.tensor_tensor(bm3, b3, b3[:, :, MID[d]:MID[d] + 1].to_broadcast([P, C, P]),
                                      ALU.subtract).then_inc(S["b_step"], 1)
                    if d == 0:
                        dve.wait_ge(S["qk_loaded"], 32 * (h + 1))
                    if d == 1:
                        evacuate(h, 1)
                    m = 4 * n
                    dve.wait_ge(S["e_ready"], m + 1)
                    e3 = Ering[0].rearrange("p (c t) -> p c t", c=C)
                    dve.tensor_copy(small[:, 40:40 + C].rearrange("p (c o) -> p c o", o=1),
                                    e3[:, :, END[d]:END[d] + 1]).then_inc(S["dec_ready"], 1)
                    if h:
                        dve.wait_ge(S["o_ready"], 2 * h)
                    dve.scalar_tensor_tensor(out=qi[:, d, :], in0=gq, scalar=QSCALE, in1=Ering[0],
                                             op0=ALU.mult, op1=ALU.mult).then_inc(S["qk_weighted"], 1)
                    dve.wait_ge(S["e_ready"], m + 2)
                    if n:
                        dve.wait_ge(S["sc_ready"], n)
                    if h and d == 0:
                        dve.wait_ge(S["o_norm"], 3 * h - 2)
                    dve.scalar_tensor_tensor(out=qs[:, :], in0=gq, scalar=QSCALE, in1=Ering[1],
                                             op0=ALU.mult, op1=ALU.mult).then_inc(S["qk_weighted"], 1)
                    dve.wait_ge(S["e_ready"], m + 3)
                    dve.tensor_tensor(bm3, b3[:, :, END[d]:END[d] + 1].to_broadcast([P, C, P]), b3,
                                      ALU.subtract).then_inc(S["b_step"], 1)
                    dve.tensor_tensor(ks[:, :], gk, Ering[0], ALU.mult).then_inc(S["qk_weighted"], 1)
                    if d == 0:
                        evacuate(h, 0)
                    dve.wait_ge(S["e_ready"], m + 4)
                    if n:
                        dve.wait_ge(S["kdt_ready"], n)
                    dve.tensor_tensor(kd[:, :], gk, Ering[1], ALU.mult).then_inc(S["qk_weighted"], 1)
                    if d == 1:
                        evacuate(h, 2)
                    if d == 1:
                        dve.wait_ge(S["sc_ready"], n + 1)
                        dve.wait_ge(S["sc_fwd"], h + 1)
                        dve.copy_predicated(
                            sct[:, :, :],
                            maskb[:, :].bitcast(I32).rearrange("p (o s) -> p o s", o=1).to_broadcast([P, C, P]),
                            PS[1][:, :].rearrange("p (c s) -> p c s", c=C)).then_inc(S["sc_tile"], 1)
                    od = order(d)
                    dve.wait_ge(S["dec_ready"], n + 1)
                    for i in range(C - 1):
                        if i == 0:
                            dve.wait_ge(S["kv_ready"], 2 * n + 1)
                        if i == 4:
                            dve.wait_ge(S["kv_ready"], 2 * n + 2)
                        kv = PS[3 - i // 4][:, i % 4 * 256:(i % 4 + 1) * 256]
                        if i == 0:
                            ins = dve.tensor_copy(St[:, d, od[1], :], kv)
                        else:
                            dve.wait_ge(S["state_step"], (C - 1) * n + i)
                            ins = dve.scalar_tensor_tensor(
                                out=St[:, d, od[i + 1], :], in0=St[:, d, od[i], :],
                                scalar=small[:, 40 + od[i]:41 + od[i]], in1=kv, op0=ALU.mult, op1=ALU.add)
                        ins.then_inc(S["state_step"], 1)
                evacuate(h, 3)
                dve.wait_ge(S["osq_ready"], 2 * h + 2)
                dve.tensor_tensor(mn[:, :], qs[:, :], ks[:, :], ALU.add).then_inc(S["o_norm"], 1)
                evacuate(h, 4)
                dve.wait_ge(S["o_sum"], h + 1)
                dve.tensor_scalar(mn[:, :], PS[3][:, :], 1.0 / 256, EPS, ALU.mult, ALU.add)\
                   .then_inc(S["o_norm"], 1)
                dve.wait_ge(S["o_norm"], 3 * h + 2)
                dve.reciprocal(mn[:, :], mn[:, :]).then_inc(S["o_norm"], 1)
                dve.wait_ge(S["o_rstd"], h + 1)
                dve.wait_ge(S["r_silu"], h + 1)
                dve.wait_ge(S["kdt_ready"], 2 * h + 2)
                for e in range(2):
                    t = (kd if e == 0 else bt)[:, :]
                    dve.scalar_tensor_tensor(out=t, in0=PS[1 + e][:, :], scalar=col("gla_norm", 2 * h + e),
                                             in1=mn[:, :], op0=ALU.mult, op1=ALU.mult)\
                       .then_inc(S["o_gate"], 1)
                    dve.wait_ge(S["o_gate"], 2 * (2 * h + e + 1) - 1)
                    dve.tensor_tensor(t, t, gr[:, e, :], ALU.mult).then_inc(S["o_gate"], 1)

        ub, csb, pooled = acc[:, 0, :], acc[:, 1:3, :].rearrange("p a t -> p (a t)"), acc[:, 3, :]
        gab = [(acc[:, 4, :], acc[:, 6, :]), (acc[:, 5, :], acc[:, 7, :])]
        ones_row = ssq
        Z0 = 8

        def ya_wo_unit(sp, j):
            w = w_ya if j < KT else w_out
            load_unit(sp, Step(U_YA + j), w[:, :, j % KT * P:(j % KT + 1) * P])

        def merge_sp(sp):
            sp.wait_ge(S["o_stored"], 32 * (GH - 1))
            sp.wait_ge(S["unit_done"], N_IN)
            sp.wait_ge(S["z_ready"], 2 * GH)
            sp.dma_start(oback[:, 0:6, :], tile_of(o_d, 0, 6)).then_inc(S["o_back"][0], 16)
            sp.wait_ge(S["o_gate"], 4 * GH)
            all_stored(sp, ALL_IN)
            sp.dma_start(wpool[:, :, :], A["w_pool_group"][0].rearrange("g c d -> c g d"))\
              .then_inc(S["wpool_loaded"], 16)
            for j in range(KT):
                g = j // 2
                if j % 2 == 0:
                    if g:
                        sp.wait_ge(S["pooled_ready"], g)
                    sp.dma_start(ub, proj[(25 + g) * P:(26 + g) * P, :]).then_inc(S["u_loaded"], 16)
                if j >= 2:
                    sp.wait_ge(S["merged_ready"], j - 1)
                a, b = gab[j % 2]
                sp.dma_start(a, proj[(29 + j) * P:(30 + j) * P, :]).then_inc(S["gab_loaded"][j % 2], 16)
                sp.dma_start(b, proj[(37 + j) * P:(38 + j) * P, :]).then_inc(S["gab_loaded"][j % 2], 16)
                if j == 0:
                    sp.wait_ge(S["o_stored"], 32 * GH)
                    sp.dma_start(oback[:, 6:8, :], tile_of(o_d, 6, 2)).then_inc(S["o_back"][1], 16)
                ya_wo_unit(sp, j + 2)

        def merge_pe(pe):
            pe.wait_ge(S["wpool_loaded"], 16)
            pe.wait_ge(S["o_gate"], 4 * GH)
            for j in range(KT):
                mm_unit(pe, Step(U_YA + j), m2hi, m2lo,
                        wait_k=(lambda k: pe.wait_ge(S["o_lo"], k + 1)) if j == 0 else None)
                pe.wait_ge(S["pooled_ready"], j // 2 + 1)
                if j:
                    pe.wait_ge(S["yb_scaled"], j)
                for b in range(2):
                    mm = pe.matmul(PS[2][:, b * HALF:(b + 1) * HALF], wpool[:, j // 2, j % 2 * P:(j % 2 + 1) * P],
                                   pooled[:, b * HALF:(b + 1) * HALF], start=True, stop=True)
                mm.then_inc(S["yb_ready"], 1)

        def merge_act(act):
            act.wait_ge(S["o_ready"], 2 * GH)
            for k in range(KT):
                act.wait_ge(S["o_back"][k // 6], 16)
                act.activation(m2hi[:, k, :], oback[:, k, :], ACT.Copy).then_inc(S["o_hi"], 1)
            for j in range(KT):
                a, b = gab[j % 2]
                act.wait_ge(S["gab_loaded"][j % 2], 32 * (j // 2 + 1))
                act.activation(a, a, ACT.Sigmoid).then_inc(S["gates_sig"], 1)
                act.activation(b, b, ACT.Sigmoid).then_inc(S["gates_sig"], 1)
                act.wait_ge(S["merged_ready"], j + 1)
                act.activation(m1hi[:, j, :], stage[:, j % 2, :], ACT.Copy).then_inc(S["merged_hi"], 1)

        def merge_dve(dve):
            dve.wait_ge(S["o_stored"], 32 * GH)
            for k in range(KT):
                dve.wait_ge(S["o_hi"], k + 1)
                dve.tensor_tensor(m2lo[:, k, :], oback[:, k, :], m2hi[:, k, :].bitcast(F32), ALU.subtract)\
                   .then_inc(S["o_lo"], 1)
            all_stored(dve, ALL_IN)
            dve.wait_ge(S["z_ready"], 2 * GH)
            dve.memset(ones_row[:, :], 1.0).then_inc(S["pool_consts"], 1)
            dve.memset(csb[:, 0:Z0 + 1], 0.0).then_inc(S["pool_consts"], 1)
            dve.wait_ge(S["pool_consts"], 1)

            def pool(g):
                w = 2 << g
                h = w // 2
                dve.wait_ge(S["u_loaded"], 16 * (g + 1))
                dve.tensor_tensor_scan(csb[:, Z0 + 1:Z0 + 1 + T], ones_row[:, :], ub, 0.0, ALU.mult, ALU.add)\
                   .then_inc(S["pool_step"], 1)
                dve.wait_ge(S["pool_step"], 3 * g + 1)
                dve.tensor_copy(csb[:, Z0 + 1 + T:Z0 + 8 + T], csb[:, Z0 + T:Z0 + T + 1].to_broadcast([P, 7]))\
                   .then_inc(S["pool_step"], 1)
                dve.wait_ge(S["pool_step"], 3 * g + 2)
                dve.wait_ge(S["pool_consts"], 2)
                if g:
                    dve.wait_ge(S["yb_ready"], 2 * g)
                dve.tensor_tensor(pooled, csb[:, Z0 + h:Z0 + h + T], csb[:, Z0 - h:Z0 - h + T], ALU.subtract)\
                   .then_inc(S["pool_step"], 1)
                dve.wait_ge(S["pool_step"], 3 * g + 3)
                edges = [(t, t + h) for t in range(h)] + [(t, T - t + h) for t in range(T - h + 1, T)]
                dve.scalar_tensor_tensor(out=pooled[:, h:T - h + 1], in0=pooled[:, h:T - h + 1], scalar=1.0 / w,
                                         in1=ub[:, h:T - h + 1], op0=ALU.mult, op1=ALU.subtract)
                for n, (t, count) in enumerate(edges):
                    ins = dve.scalar_tensor_tensor(out=pooled[:, t:t + 1], in0=pooled[:, t:t + 1],
                                                   scalar=1.0 / count, in1=ub[:, t:t + 1],
                                                   op0=ALU.mult, op1=ALU.subtract)
                ins.then_inc(S["pooled_ready"], 1)

            def split_lo(j):
                dve.wait_ge(S["merged_hi"], j + 1)
                dve.tensor_tensor(m1lo[:, j, :], stage[:, j % 2, :], m1hi[:, j, :].bitcast(F32), ALU.subtract)\
                   .then_inc(S["merged_lo"], 1)

            for j in range(KT):
                a, b = gab[j % 2]
                u = Step(U_YA + j)
                if j % 2 == 0:
                    pool(j // 2)
                if j:
                    split_lo(j - 1)
                dve.wait_ge(S["yb_ready"], j + 1)
                dve.wait_ge(S["gates_sig"], 2 * j + 2)
                dve.scalar_tensor_tensor(out=b, in0=PS[2][:, :], scalar=col("pool_scale", j), in1=b,
                                         op0=ALU.mult, op1=ALU.mult).then_inc(S["yb_scaled"], 1)
                dve.wait_ge(S["unit_done"], u.times(1, 1))
                dve.wait_ge(S["gates_sig"], 2 * j + 1)
                dve.tensor_tensor(a, PS[u.par][:, :], a, ALU.mult).then_inc(S["unit_out"][u.par], 1)
                dve.wait_ge(S["unit_out"][u.par], u.nth())
                dve.wait_ge(S["yb_scaled"], j + 1)
                dve.tensor_tensor(stage[:, j % 2, :], a, b, ALU.add).then_inc(S["merged_ready"], 1)
            split_lo(KT - 1)

        def wo_sp(sp):
            sp.wait_ge(S["merged_ready"], KT)
            sp.wait_ge(S["pooled_ready"], 4)
            sp.wait_ge(S["yb_ready"], KT)
            for i in range(2):
                sp.dma_start(acc[:, 4 * i:4 * i + 4, :], tile_of(x_d, 4 * i, 4)).then_inc(S["x_back"][i], 16)
            for j in range(KT + 2, 2 * KT):
                ya_wo_unit(sp, j)

        def wo_pe(pe):
            for j in range(KT):
                mm_unit(pe, Step(U_WO + j), m1hi, m1lo,
                        wait_k=(lambda k: pe.wait_ge(S["merged_lo"], k + 1)) if j == 0 else None)

        def add_dve(dve, u, j, ready=None):
            dve.wait_ge(S["unit_done"], u.times(1, 1))
            dve.tensor_tensor(acc[:, j, :], PS[u.par][:, :], acc[:, j, :], ALU.add)\
               .then_inc(S["unit_out"][u.par], 1)

        def wo_dve(dve):
            for j in range(KT):
                if j % 4 == 0:
                    dve.wait_ge(S["x_back"][j // 4], 16)
                add_dve(dve, Step(U_WO + j), j)

        def after_unit(u0):
            def ready(eng, k):
                u = Step(u0 + k)
                eng.wait_ge(S["unit_out"][u.par], u.nth())
            return ready

        def f1_count(g):
            return g.times(G)

        def f1_sp(sp):
            def do(e, kind, g, u, size):
                for t in range(size if kind == "in" else 0):
                    c0 = g.times(G * P, t * P)
                    load_unit(e, u + 2 * t, w_f1[:, :, bass.ds(c0, P)])
                    c1 = g.times(G * P, D_FF + t * P)
                    load_unit(e, u + (2 * t + 1), w_f1[:, :, bass.ds(c1, P)])
                for j in range(KT if kind == "out" else 0):
                    load_unit(e, u + j, w_f1o[:, bass.ds(g.times(G), size), j * P:(j + 1) * P], size)
            run_ffn(sp, SEG1, G1, 2, do)

        def f1_pool(pool):
            def do(e, kind, g, u, size):
                for t in range(2 * size if kind == "in" else KT):
                    split_unit(e, u + t, KT if kind == "in" else size)
            run_ffn(pool, SEG1, G1, 2, do)

        def f1_pe(pe):
            first = [True]

            def do(e, kind, g, u, size):
                if kind == "in":
                    for t in range(2 * size):
                        mm_unit(e, u + t, m2hi, m2lo, wait_k=lo_wait(e, "ffn") if first[0] else None)
                        if first[0]:
                            norm_sum(e, "ffn", KT)
                        first[0] = False
                else:
                    e.wait_ge(S["act_lo"], g.times(G, size))
                    s0 = G * g.par
                    for j in range(KT):
                        mm_unit(e, u + j, m1hi[:, s0:s0 + size, :], m1lo[:, s0:s0 + size, :], size)
            run_ffn(pe, SEG1, G1, 2, do)

        def f1_act(act):
            def do(e, kind, g, u, size):
                for t in range(size if kind == "in" else 0):
                    ug = u + 2 * t
                    e.wait_ge(S["unit_out"][ug.par], ug.nth())
                    e.activation(stage[:, 0, :], stage[:, 0, :], ACT.Silu).then_inc(S["gate_silu"], 1)
                    e.wait_ge(S["act_full"], g.times(G, t + 1))
                    e.activation(m1hi[:, G * g.par + t, :], ssq[:, :], ACT.Copy).then_inc(S["act_hi"], 1)
            run_ffn(act, SEG1, G1, 2, do)

        def f1_dve(dve):
            def do(e, kind, g, u, size):
                if kind == "out":
                    for j in range(KT):
                        add_dve(e, u + j, j)
                    return
                for t in range(size):
                    n = g.times(G, t + 1)
                    ug, uu = u + 2 * t, u + (2 * t + 1)
                    e.wait_ge(S["unit_done"], ug.times(1, 1))
                    e.tensor_tensor(stage[:, 0, :], PS[ug.par][:, :], rstd[:, :], ALU.mult)\
                     .then_inc(S["unit_out"][ug.par], 1)
                    e.wait_ge(S["unit_out"][ug.par], ug.nth())
                    e.wait_ge(S["unit_done"], uu.times(1, 1))
                    e.tensor_tensor(stage[:, 1, :], PS[uu.par][:, :], rstd[:, :], ALU.mult)\
                     .then_inc(S["unit_out"][uu.par], 1)
                    e.wait_ge(S["unit_out"][uu.par], uu.nth())
                    e.wait_ge(S["gate_silu"], n)
                    e.tensor_tensor(ssq[:, :], stage[:, 0, :], stage[:, 1, :], ALU.mult)\
                     .then_inc(S["act_full"], 1)
                    e.wait_ge(S["act_hi"], n)
                    e.wait_ge(S["act_full"], n)
                    e.tensor_tensor(m1lo[:, G * g.par + t, :], ssq[:, :],
                                    m1hi[:, G * g.par + t, :].bitcast(F32), ALU.subtract)\
                     .then_inc(S["act_lo"], 1)
            dve.wait_ge(S["rstd_ready"], NORM_AT["ffn"] + 1)
            run_ffn(dve, SEG1, G1, 2, do)

        def fin_dve(dve):
            dve.wait_ge(S["rstd_ready"], NORM_AT["final"] + 1)
            for k in range(KT):
                dve.scalar_tensor_tensor(out=acc[:, k, :], in0=acc[:, k, :], scalar=col("norm_final", k),
                                         in1=rstd[:, :], op0=ALU.mult, op1=ALU.mult)\
                   .then_inc(S["fin_done"], 1)

        def spill2_act(act):
            act.wait_ge(S["fin_done"], KT)
            act.dma_start(tile_of(x2_d, 0, KT), acc[:, :, :]).then_inc(S["x_spilled"], 16)

        KR0 = 1928
        IN2_COLS = [j * P for j in range(12)] + [1536, 1544, 1672, 1800]

        def in2_sp(sp):
            for j, c0 in enumerate(IN2_COLS):
                load_unit(sp, Step(U_IN2 + j), w_in2[:, :, c0:c0 + P])
            load_unit(sp, Step(U_IN2 + 16), None, parts=[
                (0, 96, w_in2[:, :, KR0 - 64:KR0 + 32]), (96, 112, w_in2[:, :, KR0 + 16:KR0 + 32]),
                (112, 128, w_in2[:, :, KR0:KR0 + 16])])

        def in2_pool(pool):
            for j in range(N_IN2):
                split_unit(pool, Step(U_IN2 + j))

        def in2_pe(pe):
            for j in range(N_IN2):
                mm_unit(pe, Step(U_IN2 + j), g1hi, g1lo, wait_k=lo_wait(pe, "mix2") if j == 0 else None)
                if j == 0:
                    norm_sum(pe, "mix2", KT)

        def in2_act(act):
            for j in range(N_IN2):
                store_act(act, Step(U_IN2 + j), proj2[j * P:(j + 1) * P, :])

        def in2_dve(dve):
            dve.wait_ge(S["rstd_ready"], NORM_AT["mix2"] + 1)
            for j in range(N_IN2):
                store_dve(dve, Step(U_IN2 + j), U_IN2, B2)

        RP = slice(64, 128)
        NOPE, RO, SW = slice(0, 64), slice(64, 96), slice(96, 128)
        CS, CSQ, RK, VTH = x4[:, 0, :], x4[:, 1, :], x4[:, 2, :], x4[:, 3, :]
        ptab = small[:, 36:39]
        MAGIC = 12582912.0
        PI = 3.1415925
        TWO_PI = (6.28125, 0.0019350051879882812, 3.019915981956753e-07)
        QK_SCALE = 96.0 ** -0.5
        qT = acc
        NQ = [(h, i) for h in range(8) for i in range(C)]

        def mla_sp(sp):
            all_stored(sp, ALL_IN2)
            sp.wait_ge(S["x_spilled"], 32)
            sp.dma_start(kT[:, 4:8, :], tile_of(proj2, 13, 4)).then_inc(S["mla_loaded"], 16)
            sp.dma_start(stage[:, 0, :].bitcast(I32), A["positions_2"].to_broadcast([P, T]))\
              .then_inc(S["mla_loaded"], 16)
            sp.dma_start(ptab, A["rope_table"]).then_inc(S["mla_loaded"], 16)
            for h in range(8):
                q0 = h * 96
                load_unit(sp, Step(U_QKV + 2 * h), None, 2, parts=[
                    (0, 96, w_uq[:, :, q0:q0 + 96]), (96, 112, w_uq[:, :, q0 + 80:q0 + 96]),
                    (112, 128, w_uq[:, :, q0 + 64:q0 + 80])])
                load_unit(sp, Step(U_QKV + 2 * h + 1), w_ukv[:, :, h * P:(h + 1) * P], 1)

        def mla_pool(pool):
            for h in range(8):
                split_unit(pool, Step(U_QKV + 2 * h), 2)
                split_unit(pool, Step(U_QKV + 2 * h + 1), 1)

        def mla_act(act):
            act.wait_ge(S["mla_loaded"], 48)
            for k in range(2):
                act.activation(m2hi[:, k, :], kT[:, 4 + k, :], ACT.Copy, scale=col("q_norm_2", k))\
                   .then_inc(S["latent_hi"], 1)
            act.activation(m2hi[:, 2, :], kT[:, 6, :], ACT.Copy, scale=col("kv_norm_2", 0))\
               .then_inc(S["latent_hi"], 1)
            act.wait_ge(S["ang_step"], 10)
            act.activation(CS[RP, :], CSQ[RP, :], ACT.Sin).then_inc(S["rope_sin"], 1)
            norm_act(act, "cq", no_wait, src=kT[:, 4:6, :], nk=2)
            norm_act(act, "ckv", no_wait, src=kT[:, 6:7, :], nk=1, dst=RK)
            act.wait_ge(S["kr_rope"], 1)
            act.activation(kT[RO, :, :], VTH[RO, :].rearrange("p (o t) -> p o t", o=1).to_broadcast([32, 8, T]),
                           ACT.Copy).then_inc(S["kr_copied"], 1)
            for h in range(8):
                act.wait_ge(S["vh_t"], h + 1)
                act.activation(Vt[:, :, h, :], PS[3][:, 0:HALF].rearrange("p (c e) -> p c e", c=C), ACT.Copy)\
                   .then_inc(S["vh_tok"], 1)
            for n, (h, i) in enumerate(NQ):
                N = (i + 1) * P
                act.wait_ge(S["s_stat"], 2 * n + 2)
                if n >= 2:
                    act.wait_ge(S["pt_ready"], n - 1)
                act.activation(x4[:, n % 2, 0:N], PS[n % 2][:, 0:N], ACT.Exp, bias=sm(n, 1), scale=QK_SCALE,
                               accum_out=sm(n, 2)).then_inc(S["p_ready"], 1)
                if n:
                    pt_copy(act, n - 1)
                if n and (n - 1) % 16 == 15:
                    mixa(act, (n - 1) // 16)
            pt_copy(act, 63)
            mixa(act, 3)

        def sm(n, what):
            c = 40 + 5 * (n % 2) + what
            return small[:, c:c + 1]

        def pt_copy(act, n):
            N = (n % C + 1) * P
            act.wait_ge(S["pt_ready"], n + 1)
            if n:
                act.wait_ge(S["pv_ready"], n)
            act.activation(x4[:, 2, 0:N], PS[2][:, 0:N], ACT.Copy).then_inc(S["pt_out"], 1)

        def mixa(act, pair):
            act.wait_ge(S["pv_ready"], 16 * (pair + 1))
            act.activation(m2hi[:, 4 + pair, :], PS[3][:, :], ACT.Copy).then_inc(S["mixa_hi"], 1)

        def mla_dve(dve):
            dve.wait_ge(S["mla_loaded"], 48)
            dve.tensor_copy(CS[RP, :], stage[RP, 0, :].bitcast(I32)).then_inc(S["ang_step"], 1)
            dve.wait_ge(S["ang_step"], 1)
            dve.tensor_scalar(CS[RP, :], CS[RP, :], ptab[RP, 0:1], None, ALU.mult).then_inc(S["ang_step"], 1)
            dve.wait_ge(S["ang_step"], 2)
            dve.tensor_scalar(CSQ[RP, :], CS[RP, :], ptab[RP, 1:2], 0.15915494309189535, ALU.add, ALU.mult)\
               .then_inc(S["ang_step"], 1)
            dve.wait_ge(S["ang_step"], 3)
            dve.tensor_scalar(CSQ[RP, :], CSQ[RP, :], MAGIC, None, ALU.add).then_inc(S["ang_step"], 1)
            dve.wait_ge(S["ang_step"], 4)
            dve.tensor_scalar(CSQ[RP, :], CSQ[RP, :], MAGIC, None, ALU.subtract).then_inc(S["ang_step"], 1)
            for i, part in enumerate(TWO_PI):
                dve.wait_ge(S["ang_step"], 3 + i + 2)
                dve.scalar_tensor_tensor(out=CS[RP, :], in0=CSQ[RP, :], scalar=-part, in1=CS[RP, :],
                                         op0=ALU.mult, op1=ALU.add).then_inc(S["ang_step"], 1)
            dve.wait_ge(S["ang_step"], 8)
            dve.tensor_scalar(CSQ[RP, :], CS[RP, :], ptab[RP, 1:2], PI, ALU.add, ALU.min).then_inc(S["ang_step"], 1)
            dve.wait_ge(S["ang_step"], 9)
            dve.tensor_scalar(CSQ[RP, :], CSQ[RP, :], -PI, None, ALU.max).then_inc(S["ang_step"], 1)
            for k in range(2):
                dve.wait_ge(S["latent_hi"], k + 1)
                dve.scalar_tensor_tensor(out=m2lo[:, k, :], in0=kT[:, 4 + k, :], scalar=col("q_norm_2", k),
                                         in1=m2hi[:, k, :].bitcast(F32), op0=ALU.mult, op1=ALU.subtract)\
                   .then_inc(S["latent_lo"], 1)
            dve.wait_ge(S["latent_hi"], 3)
            dve.scalar_tensor_tensor(out=m2lo[:, 2, :], in0=kT[:, 6, :], scalar=col("kv_norm_2", 0),
                                     in1=m2hi[:, 2, :].bitcast(F32), op0=ALU.mult, op1=ALU.subtract)\
               .then_inc(S["latent_lo"], 1)
            norm_dve(dve, "cq", no_wait, nk=2)
            dve.wait_ge(S["rope_sin"], 1)
            dve.tensor_scalar(CS[RP, :], CS[RP, :], ptab[RP, 2:3], None, ALU.mult).then_inc(S["rope_ready"], 1)
            dve.wait_ge(S["rope_ready"], 1)
            dve.tensor_tensor(VTH[RO, :], kT[RO, 7, :], CS[RO, :], ALU.mult).then_inc(S["kr_part"], 1)
            dve.tensor_tensor(CSQ[RO, :], kT[SW, 7, :], CS[SW, :], ALU.mult).then_inc(S["kr_part"], 1)
            dve.wait_ge(S["kr_part"], 1)
            dve.wait_ge(S["kr_part"], 2)
            norm_dve(dve, "ckv", no_wait, nk=1)
            dve.tensor_tensor(VTH[RO, :], VTH[RO, :], CSQ[RO, :], ALU.add).then_inc(S["kr_rope"], 1)
            dve.wait_ge(S["kr_rope"], 1)
            dve.wait_ge(S["rstd_ready"], NORM_AT["ckv"] + 1)
            dve.tensor_tensor(CSQ[RP, :], CS[RP, :], rstd[RP, :], ALU.mult).then_inc(S["csq_ready"], 1)
            dve.wait_ge(S["csq_ready"], 1)
            dve.wait_ge(S["kr_copied"], 1)
            for h in range(8):
                uq, uk = Step(U_QKV + 2 * h), Step(U_QKV + 2 * h + 1)
                q, k = PS[uq.par], PS[uk.par]
                dve.wait_ge(S["unit_done"], uq.times(1, 1))
                dve.tensor_tensor(qT[NOPE, h, :], q[NOPE, :], rstd[NOPE, :], ALU.mult)
                dve.tensor_tensor(qT[RO, h, :], q[RO, :], CSQ[RO, :], ALU.mult).then_inc(S["q_a"], 1)
                dve.tensor_tensor(CS[RO, :], q[SW, :], CSQ[SW, :], ALU.mult).then_inc(S["unit_out"][uq.par], 1)
                dve.wait_ge(S["unit_out"][uq.par], uq.nth())
                dve.wait_ge(S["q_a"], h + 1)
                dve.tensor_tensor(qT[RO, h, :], qT[RO, h, :], CS[RO, :], ALU.add).then_inc(S["q_rope"], 1)
                dve.wait_ge(S["unit_done"], uk.times(1, 1))
                dve.tensor_tensor(kT[NOPE, h, :], k[NOPE, :], RK[NOPE, :], ALU.mult)
                if h:
                    dve.wait_ge(S["vh_t"], h)
                dve.tensor_tensor(VTH[RP, :], k[RP, :], RK[RP, :], ALU.mult).then_inc(S["unit_out"][uk.par], 1)

            def normalise(n):
                N = (n % C + 1) * P
                dve.wait_ge(S["p_ready"], n + 1)
                dve.reciprocal(sm(n, 3), sm(n, 2)).then_inc(S["rs_inv"], 1)
                dve.wait_ge(S["rs_inv"], n + 1)
                dve.tensor_scalar(x4[:, n % 2, 0:N], x4[:, n % 2, 0:N], sm(n, 3), None, ALU.mult)\
                   .then_inc(S["p_norm"], 1)

            def mixa_low(pair):
                dve.wait_ge(S["mixa_hi"], pair + 1)
                dve.tensor_tensor(m2lo[:, 4 + pair, :], PS[3][:, :], m2hi[:, 4 + pair, :].bitcast(F32),
                                  ALU.subtract).then_inc(S["mixa_lo"], 1)

            for n, (h, i) in enumerate(NQ):
                N = (i + 1) * P
                dve.wait_ge(S["s_ready"], n + 1)
                dve.tensor_reduce(sm(n, 0), PS[n % 2][:, 0:N], AX.X, ALU.max).then_inc(S["s_stat"], 1)
                dve.wait_ge(S["s_stat"], 2 * n + 1)
                dve.tensor_scalar(sm(n, 1), sm(n, 0), -QK_SCALE, None, ALU.mult).then_inc(S["s_stat"], 1)
                if n:
                    normalise(n - 1)
                if n > 1 and (n - 2) % 16 == 15:
                    mixa_low((n - 2) // 16)
            normalise(63)
            mixa_low(3)

        def mla_pe(pe):
            norm_sum(pe, "cq", 2)
            pe.wait_ge(S["norm_mean"], 2 * (NORM_AT["cq"] + 1) - 1)
            norm_sum(pe, "ckv", 1)
            pe.wait_ge(S["latent_lo"], 2)
            pe.wait_ge(S["latent_lo"], 3)
            for h in range(8):
                uq, uk = Step(U_QKV + 2 * h), Step(U_QKV + 2 * h + 1)
                mm_unit(pe, uq, m2hi, m2lo, 2)
                mm_unit(pe, uk, m2hi[:, 2:3, :], m2lo[:, 2:3, :], 1)
                pe.wait_ge(S["unit_out"][uk.par], uk.nth())
                if h:
                    pe.wait_ge(S["vh_tok"], h)
                for c in range(C):
                    tr = pe.transpose(PS[3][:, c * 64:(c + 1) * 64], VTH[RP, c * P:(c + 1) * P],
                                      ident[RP, RP])
                tr.then_inc(S["vh_t"], 1)
            pe.wait_ge(S["q_rope"], 8)
            pe.wait_ge(S["vh_tok"], 8)

            def scores(n):
                h, i = NQ[n]
                N = (i + 1) * P
                if n >= 2:
                    pe.wait_ge(S["p_ready"], n - 1)
                for b in range(0, N, HALF):
                    w = min(HALF, N - b)
                    last = b + w == N
                    mm = pe.matmul(PS[n % 2][:, b:b + w], qT[0:96, h, i * P:(i + 1) * P],
                                   kT[0:96, h, b:b + w], start=True, stop=True)
                mm = pe.matmul(PS[n % 2][:, N - P:N], ident16[:, :], negm16[:, :], start=False, stop=True,
                               skip_group_check=True)
                mm.then_inc(S["s_ready"], 1)

            def turn(n):
                pe.wait_ge(S["p_norm"], n + 1)
                if n:
                    pe.wait_ge(S["pt_out"], n)
                for j in range(n % C + 1):
                    tr = pe.transpose(PS[2][:, j * P:(j + 1) * P], x4[:, n % 2, j * P:(j + 1) * P], ident[:, :])
                tr.then_inc(S["pt_ready"], 1)

            def values(n):
                h, i = NQ[n]
                if n % 16 == 0 and n:
                    pe.wait_ge(S["mixa_lo"], n // 16)
                pe.wait_ge(S["pt_out"], n + 1)
                o = PS[3][h % 2 * 64:h % 2 * 64 + 64, i * P:(i + 1) * P]
                for j in range(i + 1):
                    mm = pe.matmul(o, Vt[:, j, h, :], x4[:, 2, j * P:(j + 1) * P], start=(j == 0), stop=(j == i))
                mm.then_inc(S["pv_ready"], 1)

            scores(0)
            scores(1)
            for n in range(64):
                turn(n)
                if n + 2 < 64:
                    scores(n + 2)
                values(n)

        ig, lf, fz, mrow = acc[0:4, 0, :], acc[0:4, 1, :], acc[0:4, 2, :], acc[0:4, 3, :]
        grow, arow, on4 = acc[0:4, 4, :], acc[0:4, 7, :], ssq[0:4, :]
        rrow = [acc[0:4, 5, :], acc[0:4, 6, :]]
        acol, emcol = small[:, 0:32], rstd[:, 0:32]
        vTm, omT, ht, mtmp = acc[:, 4, :], acc[:, 5, :], acc[:, 6, :], acc[:, 7, :]
        wrap = rstd[:, 64:128]
        den, ssh = rstd[:, 64:72], rstd[:, 72:80]

        def mlstm_sp(sp):
            sp.wait_ge(S["mixa_lo"], 4)
            sp.dma_start(ig, proj2[12 * P:12 * P + 4, :]).then_inc(S["gates_loaded"], 16)
            sp.dma_start(fz, proj2[12 * P + 4:12 * P + 8, :]).then_inc(S["gates_loaded"], 16)
            sp.dma_start(small[0:4, 60:61], A["b_gates_2"][:, 0:4].rearrange("a h -> h a"))\
              .then_inc(S["gates_loaded"], 16)
            sp.dma_start(small[0:4, 61:62], A["b_gates_2"][:, 4:8].rearrange("a h -> h a"))\
              .then_inc(S["gates_loaded"], 16)
            for J in range(C):
                sp.wait_ge(S["g_step"], 3 * J + 3)
                sp.dma_start(r_d[J * 4:J * 4 + 4, J * P:T], rrow[J % 2][:, J * P:T])\
                  .then_inc(S["r_stored"][J % 2], 16)
            for t in range(4):
                if t:
                    sp.wait_ge(S["conv_step"], 4 * t)
                sp.dma_start(cb[:, 3:3 + T], proj2[t * P:(t + 1) * P, :]).then_inc(S["conv_loaded"], 16)
            for i in range(2):
                sp.wait_ge(S["r_stored"][i], 16 * C // 2)
            sp.wait_ge(S["am_t"], 1)
            for h in range(4):
                if h:
                    sp.wait_ge(S["mv_t"], h)
                sp.dma_start(vTm, proj2[(4 + h) * P:(5 + h) * P, :]).then_inc(S["mv_loaded"], 16)
                if h:
                    sp.wait_ge(S["h_step"], 7 * h)
                sp.dma_start(omT, proj2[(8 + h) * P:(9 + h) * P, :]).then_inc(S["om_loaded"], 16)
                for J in range(C):
                    n = h * C + J
                    if n >= 2:
                        sp.wait_ge(S["w_ready"], n - 1)
                    sp.dma_start(stage[:, n % 2, J * P:T],
                                 r_d[J * 4 + h:J * 4 + h + 1, J * P:T].to_broadcast([P, T - J * P]))\
                      .then_inc(S["r_bc_loaded"][n % 2], 16)

        def mlstm_act(act):
            act.wait_ge(S["gates_loaded"], 64)
            bf = small[0:4, 61:62]
            act.activation(lf, fz, ACT.Abs, bias=bf).then_inc(S["f_log"], 1)
            act.wait_ge(S["f_log"], 1)
            act.activation(lf, lf, ACT.Exp, scale=-1.0).then_inc(S["f_log"], 1)
            act.wait_ge(S["f_log"], 2)
            act.activation(lf, lf, ACT.Ln, bias=1.0).then_inc(S["f_log"], 1)
            for t in range(4):
                act.wait_ge(S["conv_step"], 4 * t + 4)
                act.activation(qk[:, t, :], qk[:, t, :], ACT.Silu).then_inc(S["conv_silu"], 1)
            act.wait_ge(S["am_t"], 1)
            act.activation(acol, PS[2][:, 0:32], ACT.Copy).then_inc(S["am_cols"], 1)
            act.activation(emcol, PS[2][:, 32:64], ACT.Exp, scale=-1.0).then_inc(S["am_cols"], 1)
            for h in range(4):
                act.wait_ge(S["mv_t"], h + 1)
                if h:
                    act.wait_ge(S["ho_ready"], h)
                act.activation(vaug[:, :, 0:P], PS[3][:, :].rearrange("p (c e) -> p c e", c=C), ACT.Copy)\
                   .then_inc(S["mv_tok"], 1)
                act.wait_ge(S["om_loaded"], 16 * (h + 1))
                act.activation(omT, omT, ACT.Sigmoid).then_inc(S["om_sig"], 1)
                for J in range(C):
                    n = h * C + J
                    act.wait_ge(S["st_e"], n + 1)
                    act.activation(stage[:, n % 2, J * P:T], stage[:, n % 2, J * P:T], ACT.Exp)\
                       .then_inc(S["st_exp"], 1)
                act.wait_ge(S["h_step"], 7 * h + 3)
                for i in range(C):
                    act.activation(hq[:, i, :], ht[:, i * P:(i + 1) * P], ACT.Square,
                                   accum_out=ssh[:, i:i + 1]).then_inc(S["h_sq"], 1)
                act.wait_ge(S["h_step"], 7 * h + 5)
                act.activation(ssh, ssh, ACT.Sqrt).then_inc(S["h_rstd"], 1)
                act.wait_ge(S["h_step"], 7 * h + 7)
                act.activation(m2hi[:, h, :], mtmp, ACT.Copy).then_inc(S["mixm_hi"], 1)

        def mlstm_pool(pool):
            pool.wait_ge(S["mixa_lo"], 4)
            pool.memset(cb[:, 0:3], 0.0).then_inc(S["ml_consts"], 1)
            pool.memset(vaug[:, :, P:P + 1], 1.0).then_inc(S["ml_consts"], 1)
            for n in range(4 * C):
                J = n % C
                pool.wait_ge(S["st_w"], n + 1)
                blk = Wt[:, J, J * P:(J + 1) * P]
                pool.affine_select(out=blk, in_=blk, compare_op=ALU.is_ge, fill=0.0, base=0,
                                   pattern=[[1, P]], channel_multiplier=-1).then_inc(S["w_ready"], 1)

        def mlstm_dve(dve):
            dve.wait_ge(S["gates_loaded"], 64)
            bi, bf = small[0:4, 60:61], small[0:4, 61:62]
            dve.memset(on4, 1.0).then_inc(S["m_step"], 1)
            dve.tensor_scalar(ig, ig, bi, None, ALU.add).then_inc(S["m_step"], 1)
            dve.wait_ge(S["f_log"], 1)
            dve.tensor_scalar(fz, fz, bf, 0.0, ALU.add, ALU.min).then_inc(S["m_step"], 1)
            dve.wait_ge(S["f_log"], 3)
            dve.wait_ge(S["m_step"], 3)
            dve.tensor_tensor(lf, fz, lf, ALU.subtract).then_inc(S["m_step"], 1)
            dve.wait_ge(S["m_step"], 4)
            dve.wait_ge(S["m_step"], 2)
            dve.tensor_tensor_scan(mrow, lf, ig, 0.0, ALU.add, ALU.max).then_inc(S["m_step"], 1)
            dve.wait_ge(S["m_step"], 5)
            dve.wait_ge(S["m_step"], 1)
            for J in range(C):
                s = slice(J * P, T)
                b = slice(J * P, (J + 1) * P)
                if J:
                    dve.wait_ge(S["g_step"], 3 * J)
                dve.tensor_tensor_scan(grow[:, s], on4[:, s], lf[:, s], 0.0, ALU.mult, ALU.add)\
                   .then_inc(S["g_step"], 1)
                dve.wait_ge(S["g_step"], 3 * J + 1)
                dve.tensor_tensor(arow[:, b], ig[:, b], grow[:, b], ALU.subtract).then_inc(S["g_step"], 1)
                if J >= 2:
                    dve.wait_ge(S["r_stored"][J % 2], 16 * (J // 2))
                dve.tensor_tensor(rrow[J % 2][:, s], grow[:, s], mrow[:, s], ALU.subtract)\
                   .then_inc(S["g_step"], 1)
            dve.wait_ge(S["ml_consts"], 1)
            for t in range(4):
                dve.wait_ge(S["conv_loaded"], 16 * (t + 1))
                dve.tensor_scalar(qk[:, t, :], cb[:, 3:3 + T], col("conv_w_2", 12 + t), col("conv_b_2", t),
                                  ALU.mult, ALU.add).then_inc(S["conv_step"], 1)
                for k in range(3):
                    dve.wait_ge(S["conv_step"], 4 * t + k + 1)
                    dve.scalar_tensor_tensor(out=qk[:, t, :], in0=cb[:, k:k + T],
                                             scalar=col("conv_w_2", 4 * k + t), in1=qk[:, t, :],
                                             op0=ALU.mult, op1=ALU.add)\
                       .then_inc(S["conv_step"], 1)
            dve.wait_ge(S["am_cols"], 2)
            for h in range(4):
                for J in range(C):
                    n = h * C + J
                    s = slice(J * P, T)
                    e = stage[:, n % 2, s]
                    dve.wait_ge(S["r_bc_loaded"][n % 2], 16 * (n // 2 + 1))
                    dve.tensor_scalar(e, e, acol[:, 4 * J + h:4 * J + h + 1], 0.0, ALU.add, ALU.min)\
                       .then_inc(S["st_e"], 1)
                    if n % C:
                        weigh(dve, n - 1)
                weigh(dve, h * C + C - 1)
                outputs(dve, h)

        def weigh(dve, n):
            J = n % C
            s = slice(J * P, T)
            dve.wait_ge(S["st_exp"], n + 1)
            dve.wait_ge(S["st_ready"], n + 1)
            if n // C and J == 0:
                dve.wait_ge(S["ho_ready"], n // C)
            dve.scalar_tensor_tensor(out=Wt[:, J, s], in0=PS[n % 2][:, s], scalar=0.125,
                                     in1=stage[:, n % 2, s], op0=ALU.mult, op1=ALU.mult)\
               .then_inc(S["st_w"], 1)

        def ho(i):
            bank = i // 3
            return PS[2 + bank // 2][:, bank % 2 * HALF + i % 3 * 129:bank % 2 * HALF + (i % 3 + 1) * 129]

        def outputs(dve, h):
            dve.wait_ge(S["ho_ready"], h + 1)
            for i in range(C):
                c = 4 * i + h
                ins = dve.scalar_tensor_tensor(out=den[:, i:i + 1], in0=ho(i)[:, P:P + 1], scalar=-1.0,
                                               in1=emcol[:, c:c + 1], op0=ALU.mult, op1=ALU.max)
            ins.then_inc(S["h_neg"], 1)
            dve.wait_ge(S["h_neg"], h + 1)
            for i in range(C):
                ins = dve.tensor_tensor(den[:, i:i + 1], ho(i)[:, P:P + 1], den[:, i:i + 1], ALU.max)
            ins.then_inc(S["h_step"], 1)
            dve.wait_ge(S["h_step"], 7 * h + 1)
            dve.reciprocal(den, den).then_inc(S["h_step"], 1)
            dve.wait_ge(S["h_step"], 7 * h + 2)
            for i in range(C):
                ins = dve.tensor_scalar(ht[:, i * P:(i + 1) * P], ho(i)[:, 0:P], den[:, i:i + 1], None, ALU.mult)
            ins.then_inc(S["h_step"], 1)
            dve.wait_ge(S["h_sq"], C * (h + 1))
            dve.tensor_scalar(ssh, ssh, 1.0 / P, EPS, ALU.mult, ALU.add).then_inc(S["h_step"], 1)
            dve.wait_ge(S["h_step"], 7 * h + 4)
            dve.reciprocal(ssh, ssh).then_inc(S["h_step"], 1)
            dve.wait_ge(S["h_rstd"], h + 1)
            dve.wait_ge(S["h_step"], 7 * h + 3)
            for i in range(C):
                ins = dve.tensor_scalar(ht[:, i * P:(i + 1) * P], ht[:, i * P:(i + 1) * P], ssh[:, i:i + 1],
                                        None, ALU.mult)
            ins.then_inc(S["h_step"], 1)
            dve.wait_ge(S["ht_t"], h + 1)
            dve.wait_ge(S["om_sig"], h + 1)
            dve.scalar_tensor_tensor(out=mtmp, in0=PS[3][:, :], scalar=col("ml_head_norm_2", h), in1=omT,
                                     op0=ALU.mult, op1=ALU.mult).then_inc(S["h_step"], 1)
            dve.wait_ge(S["mixm_hi"], h + 1)
            dve.tensor_tensor(m2lo[:, h, :], mtmp, m2hi[:, h, :].bitcast(F32), ALU.subtract)\
               .then_inc(S["mixm_lo"], 1)

        def mlstm_pe(pe):
            pe.wait_ge(S["g_step"], 3 * (C) - 1)
            pe.wait_ge(S["mixa_lo"], 4)
            for w, row in enumerate((arow, mrow)):
                for i in range(C):
                    tr = pe.transpose(PS[2][:, 32 * w + 4 * i:32 * w + 4 * i + 4], row[:, i * P:(i + 1) * P],
                                      ident[0:4, 0:4])
            tr.then_inc(S["am_t"], 1)
            pe.wait_ge(S["conv_silu"], 4)
            for h in range(4):
                pe.wait_ge(S["mv_loaded"], 16 * (h + 1))
                if h:
                    pe.wait_ge(S["h_step"], 7 * h)
                for c in range(C):
                    tr = pe.transpose(PS[3][:, c * P:(c + 1) * P], vTm[:, c * P:(c + 1) * P], ident[:, :])
                tr.then_inc(S["mv_t"], 1)
                hp = slice(h % 2 * 64, h % 2 * 64 + 64)
                for J in range(C):
                    n = h * C + J
                    if n >= 2:
                        pe.wait_ge(S["st_w"], n - 1)
                    for a, b in ((J * P, HALF), (max(J * P, HALF), T)):
                        if a < b:
                            mm = pe.matmul(PS[n % 2][:, a:b], qk[hp, 2 + h // 2, J * P:(J + 1) * P],
                                           qk[hp, h // 2, a:b], start=True, stop=True)
                    mm.then_inc(S["st_ready"], 1)
                pe.wait_ge(S["mv_tok"], h + 1)
                pe.wait_ge(S["ml_consts"], 2)
                pe.wait_ge(S["am_cols"], 2)
                pe.wait_ge(S["w_ready"], C * (h + 1))
                for i in range(C):
                    for J in range(i + 1):
                        mm = pe.matmul(ho(i), Wt[:, J, i * P:(i + 1) * P], vaug[:, J, 0:129],
                                       start=(J == 0), stop=(J == i))
                mm.then_inc(S["ho_ready"], 1)
                pe.wait_ge(S["h_step"], 7 * h + 6)
                for c in range(C):
                    tr = pe.transpose(PS[3][:, c * P:(c + 1) * P], ht[:, c * P:(c + 1) * P], ident[:, :])
                tr.then_inc(S["ht_t"], 1)

        def wo2_sp(sp):
            for j in range(2, KT):
                load_unit(sp, Step(U_WO2 + j), w_out2[:, :, j * P:(j + 1) * P])
            last = Step(U_WO2 + KT - 1)
            sp.wait_ge(S["unit_done"], last.times(1, 1))
            for i in range(2):
                sp.dma_start(xr[:, 4 * i:4 * i + 4, :], tile_of(x2_d, 4 * i, 4)).then_inc(S["x_back"][i], 16)

        def wo2_pe(pe):
            for j in range(KT):
                if j == 0:
                    pe.wait_ge(S["mixm_lo"], 4)
                mm_unit(pe, Step(U_WO2 + j), m2hi, m2lo)
            norm_sum(pe, "post_mix", KT)

        def wo2_dve(dve):
            for j in range(KT):
                u = Step(U_WO2 + j)
                dve.wait_ge(S["unit_done"], u.times(1, 1))
                dve.tensor_copy(acc[:, j, :], PS[u.par][:, :]).then_inc(S["unit_out"][u.par], 1)
            norm_dve(dve, "post_mix", no_wait)
            dve.wait_ge(S["rstd_ready"], NORM_AT["post_mix"] + 1)
            for k in range(KT):
                dve.scalar_tensor_tensor(out=acc[:, k, :], in0=acc[:, k, :], scalar=col("norm_post_mix_2", k),
                                         in1=rstd[:, :], op0=ALU.mult, op1=ALU.mult)\
                   .then_inc(S["y_scaled"], 1)
                dve.wait_ge(S["y_scaled"], k + 1)
                dve.wait_ge(S["x_back"][k // 4], 32)
                dve.tensor_tensor(acc[:, k, :], acc[:, k, :], xr[:, k, :], ALU.add).then_inc(S["x_added"], 1)

        def spill3_act(act):
            act.wait_ge(S["x_added"], KT)
            act.dma_start(tile_of(x3_d, 0, KT), acc[:, :, :]).then_inc(S["x_spilled"], 16)

        def f2_sp(sp):
            def do(e, kind, g, u, size):
                for t in range(size if kind == "in" else 0):
                    if u.s == 0 and g.c == 0 and t < 2:
                        continue
                    load_unit(e, u + t, w_up[:, :, bass.ds(g.times(G * P, t * P), P)])
                for j in range(KT if kind == "out" else 0):
                    load_unit(e, u + j, w_down[:, bass.ds(g.times(G), size), j * P:(j + 1) * P], size)
            run_ffn(sp, SEG2, G2, 1, do)

        def f2_pool(pool):
            def do(e, kind, g, u, size):
                for t in range(size if kind == "in" else KT):
                    split_unit(e, u + t, KT if kind == "in" else size)
            run_ffn(pool, SEG2, G2, 1, do)

        def f2_pe(pe):
            first = [True]

            def do(e, kind, g, u, size):
                if kind == "in":
                    for t in range(size):
                        mm_unit(e, u + t, h3hi, h3lo, wait_k=lo_wait(e, "mlp") if first[0] else None)
                        if first[0]:
                            norm_sum(e, "mlp", KT)
                        first[0] = False
                else:
                    e.wait_ge(S["sq_lo"], g.times(G, size))
                    s0 = G * g.par
                    for j in range(KT):
                        mm_unit(e, u + j, a2hi[:, s0:s0 + size, :], a2lo[:, s0:s0 + size, :], size)
            run_ffn(pe, SEG2, G2, 1, do)

        def f2_act(act):
            def do(e, kind, g, u, size):
                for t in range(size if kind == "in" else 0):
                    n = g.times(G, t + 1)
                    ut = u + t
                    e.wait_ge(S["unit_out"][ut.par], ut.nth())
                    e.activation(stage[:, 1, :], stage[:, 0, :], ACT.Square).then_inc(S["up_sq"], 1)
                    e.wait_ge(S["up_sq"], n)
                    e.activation(a2hi[:, G * g.par + t, :], stage[:, 1, :], ACT.Copy).then_inc(S["sq_hi"], 1)
            run_ffn(act, SEG2, G2, 1, do)

        def f2_dve(dve):
            def do(e, kind, g, u, size):
                if kind == "out":
                    for j in range(KT):
                        if u.s == 0 and g.c == 0:
                            raise ValueError("the first down segment is in the loop")
                        add_dve(e, u + j, j)
                    return
                for t in range(size):
                    n = g.times(G, t + 1)
                    ut = u + t
                    e.wait_ge(S["unit_done"], ut.times(1, 1))
                    e.scalar_tensor_tensor(out=stage[:, 0, :], in0=PS[ut.par][:, :], scalar=0.0,
                                           in1=rstd[:, :], op0=ALU.max, op1=ALU.mult)\
                     .then_inc(S["unit_out"][ut.par], 1)
                    e.wait_ge(S["sq_hi"], n)
                    e.tensor_tensor(a2lo[:, G * g.par + t, :], stage[:, 1, :],
                                    a2hi[:, G * g.par + t, :].bitcast(F32), ALU.subtract)\
                     .then_inc(S["sq_lo"], 1)
            dve.wait_ge(S["rstd_ready"], NORM_AT["mlp"] + 1)
            dve.wait_ge(S["x_spilled"], 48)
            dve.memset(acc[:, :, :], 0.0).then_inc(S["acc_zero"], 1)
            dve.wait_ge(S["acc_zero"], 1)
            run_ffn(dve, SEG2, G2, 1, do)

        def end_sp(sp):
            sp.wait_ge(S["unit_done"], U_END)
            for i in range(2):
                sp.dma_start(xr[:, 4 * i:4 * i + 4, :], tile_of(x3_d, 4 * i, 4)).then_inc(S["x_back"][i], 16)
            for c in range(C):
                sp.wait_ge(S["out_ev"], c + 1)
                sp.dma_start(out[0, c * P:(c + 1) * P, :], orow[:, c % 2, :]).then_inc(S["out_stored"][c % 2], 16)
            for i in range(2):
                sp.wait_ge(S["out_stored"][i], 16 * C // 2)

        def end_dve(dve):
            norm_dve(dve, "post_mlp", no_wait)
            dve.wait_ge(S["rstd_ready"], NORM_AT["post_mlp"] + 1)
            for k in range(KT):
                dve.scalar_tensor_tensor(out=acc[:, k, :], in0=acc[:, k, :], scalar=col("norm_post_mlp_2", k),
                                         in1=rstd[:, :], op0=ALU.mult, op1=ALU.mult)\
                   .then_inc(S["y_scaled"], 1)
                dve.wait_ge(S["y_scaled"], KT + k + 1)
                dve.wait_ge(S["x_back"][k // 4], 48)
                dve.tensor_tensor(acc[:, k, :], acc[:, k, :], xr[:, k, :], ALU.add).then_inc(S["x_added"], 1)

        def end_pe(pe):
            norm_sum(pe, "post_mlp", KT)
            pe.wait_ge(S["x_added"], KT + 8)
            for c in range(C):
                if c >= 2:
                    pe.wait_ge(S["out_ev"], c - 1)
                for k in range(KT):
                    tr = pe.transpose(PS[c % 2][:, k * P:(k + 1) * P], acc[:, k, c * P:(c + 1) * P], ident[:, :])
                tr.then_inc(S["out_t"], 1)

        def end_act(act):
            for c in range(C):
                act.wait_ge(S["out_t"], c + 1)
                if c >= 2:
                    act.wait_ge(S["out_stored"][c % 2], 16 * (c // 2))
                act.activation(orow[:, c % 2, :], PS[c % 2][:, :], ACT.Copy).then_inc(S["out_ev"], 1)

        @block.sync
        def _(sp):
            start_sp(sp)
            wup_sp(sp)
            in_sp(sp)
            gla_sp(sp)
            merge_sp(sp)
            wo_sp(sp)
            f1_sp(sp)
            in2_sp(sp)
            mla_sp(sp)
            for j in range(2):
                load_unit(sp, Step(U_WO2 + j), w_out2[:, :, j * P:(j + 1) * P])
            mlstm_sp(sp)
            wo2_sp(sp)
            for t in range(2):
                load_unit(sp, Step(U_F2 + t), w_up[:, :, t * P:(t + 1) * P])
            f2_sp(sp)
            end_sp(sp)

        @block.gpsimd
        def _(pool):
            start_pool(pool)
            wup_pool(pool)
            in_pool(pool)
            mid_pool(pool)
            for j in range(2 * KT):
                split_unit(pool, Step(U_YA + j))
            f1_pool(pool)
            in2_pool(pool)
            mla_pool(pool)
            for j in range(2):
                split_unit(pool, Step(U_WO2 + j))
            mlstm_pool(pool)
            for j in range(2, KT):
                split_unit(pool, Step(U_WO2 + j))
            f2_pool(pool)

        @block.scalar
        def _(act):
            start_act(act)
            norm_act(act, "mix", no_wait, "norm_mix", h1hi)
            in_act(act)
            gla_act(act)
            merge_act(act)
            norm_act(act, "ffn", after_unit(U_WO), "norm_ffn", m2hi)
            f1_act(act)
            norm_act(act, "final", after_unit(U_IN2 - KT))
            norm_act(act, "mix2", lambda e, k: e.wait_ge(S["fin_done"], k + 1), "norm_pre_mix_2", g1hi)
            spill2_act(act)
            in2_act(act)
            mla_act(act)
            mlstm_act(act)
            norm_act(act, "post_mix", after_unit(U_WO2))
            norm_act(act, "mlp", lambda e, k: e.wait_ge(S["x_added"], k + 1), "norm_pre_mlp_2", h3hi)
            spill3_act(act)
            f2_act(act)
            norm_act(act, "post_mlp", after_unit(U_END - KT))
            end_act(act)

        @block.tensor
        def _(pe):
            start_pe(pe)
            in_pe(pe)
            gla_pe(pe)
            merge_pe(pe)
            wo_pe(pe)
            f1_pe(pe)
            norm_sum(pe, "final", KT)
            in2_pe(pe)
            mla_pe(pe)
            mlstm_pe(pe)
            wo2_pe(pe)
            f2_pe(pe)
            end_pe(pe)

        @block.vector
        def _(dve):
            norm_dve(dve, "mix", no_wait, "norm_mix", h1hi, h1lo)
            in_dve(dve)
            gla_dve(dve)
            merge_dve(dve)
            wo_dve(dve)
            norm_dve(dve, "ffn", no_wait, "norm_ffn", m2hi, m2lo)
            f1_dve(dve)
            norm_dve(dve, "final", no_wait)
            fin_dve(dve)
            norm_dve(dve, "mix2", no_wait, "norm_pre_mix_2", g1hi, g1lo)
            in2_dve(dve)
            mla_dve(dve)
            mlstm_dve(dve)
            wo2_dve(dve)
            norm_dve(dve, "mlp", no_wait, "norm_pre_mlp_2", h3hi, h3lo)
            f2_dve(dve)
            end_dve(dve)


OUTS = [((1, T, D), "float32")]


def rope_table():
    import numpy as np
    inv = (1.0 / (10000.0 ** (np.arange(0, 32, 2, dtype=np.float32) / 32))).astype(np.float32)
    t = np.zeros((P, 3), np.float32)
    t[:, 2] = 1.0
    for q in range(4):
        r = slice(64 + 16 * q, 80 + 16 * q)
        t[r, 0] = inv
        t[r, 1] = np.pi / 2 if q < 2 else 0.0
        t[r, 2] = -1.0 if q == 2 else 1.0
    return t


def kernel(**inputs):
    import numpy as np
    import concourse.bacc as bacc
    from concourse.bass_utils import run_bass_kernel_spmd

    nc = bacc.Bacc("TRN2", target_bir_lowering=False, num_devices=1)
    arrays, aps = {}, {}
    for name, a in {**inputs, "rope_table": rope_table()}.items():
        a = np.ascontiguousarray(a)
        arrays[f"in_{name}"] = a
        aps[name] = nc.dram_tensor(f"in_{name}", a.shape, mybir.dt.from_np(a.dtype), kind="ExternalInput").ap()
    shape, dtype = OUTS[0]
    out = nc.dram_tensor("out_0", shape, mybir.dt.from_np(np.dtype(dtype)), kind="ExternalOutput").ap()
    two_block_kernel(nc, aps, out)
    r = run_bass_kernel_spmd(nc, [arrays], core_ids=[0])
    return r.results[0]["out_0"]
```

```python
from contextlib import ExitStack

import concourse.bass as bass
from concourse import mybir

ALU = mybir.AluOpType
ACT = mybir.ActivationFunctionType
AX = mybir.AxisListType
F32 = mybir.dt.float32
F32R = mybir.dt.float32r
I32 = mybir.dt.int32
BF16 = mybir.dt.bfloat16

P = 128
D = 1024
T = 1024
KT = D // P
HALF = 512
EPS = 1e-6
GH = 4
C = T // P
D_FF = 2816
D_FF2 = 4096
BIG = 3.0e38

VEC_ROWS = [("norm_mix", 8), ("gla_norm", 8), ("pool_scale", 8), ("norm_ffn", 8), ("norm_final", 8),
            ("norm_pre_mix_2", 8), ("norm_post_mix_2", 8), ("norm_pre_mlp_2", 8),
            ("norm_post_mlp_2", 8), ("b_decay_fwd", 4), ("b_decay_bwd", 4), ("conv_w_2", 16),
            ("conv_b_2", 4), ("ml_head_norm_2", 4), ("q_norm_2", 2), ("kv_norm_2", 1)]
VEC = {}
NVEC = 0
for _name, _n in VEC_ROWS:
    VEC[_name] = NVEC
    NVEC += _n

G = 4
F1 = D_FF // P
F2 = D_FF2 // P
G1 = [G] * (F1 // G) + ([F1 % G] if F1 % G else [])
G2 = [G] * (F2 // G)
U_IN = 0
N_IN = 45
U_YA = U_IN + N_IN
U_WO = U_YA + KT
U_F1 = U_WO + KT
N_F1 = 2 * F1 + KT * len(G1)
U_IN2 = U_F1 + N_F1
N_IN2 = 17
U_QKV = U_IN2 + N_IN2
U_WO2 = U_QKV + 16
U_F2 = U_WO2 + KT
N_F2 = F2 + KT * len(G2)
U_END = U_F2 + N_F2

NORMS = [("mix", 8), ("ffn", 8), ("final", 8), ("mix2", 8), ("post_mix", 8),
         ("mlp", 8), ("post_mlp", 8)]
NORM_AT = {}
SQ_BASE = {}
_b = 0
for _i, (_name, _n) in enumerate(NORMS):
    NORM_AT[_name] = _i
    SQ_BASE[_name] = _b
    _b += _n

THREE = {U_IN2 + 4} | {U_QKV + 2 * h for h in range(8)}
LANDED = []
_c = [0, 0]
for _u in range(U_END):
    _c[_u % 2] += 48 if _u in THREE else 16
    LANDED.append(_c[_u % 2])


def par(u):
    return u % 2


def nth(u):
    return u // 2 + 1


class Step:

    def __init__(self, c, s=0, i=0):
        self.c, self.s, self.i = c, s, i

    def __add__(self, k):
        return Step(self.c + k, self.s, self.i)

    def times(self, m, plus=0):
        v = self.c * m + plus
        return self.i * (self.s * m) + v if self.s else v

    @property
    def par(self):
        return self.c % 2

    def nth(self, plus=0):
        v = self.c // 2 + 1 + plus
        return self.i * (self.s // 2) + v if self.s else v

    def landed(self):
        return self.i * (8 * self.s) + LANDED[self.c] if self.s else LANDED[self.c]


SEMS = ("p_norm pt_out w_hi w_split unit_done sq_done sq_added norm_sum norm_mean rstd_ready hi_ready lo_ready "
        "consts_ready x_loaded vec_loaded vec_t xt_tr cols_ready xt_ev x_spilled gla_loaded "
        "qk_loaded v_loaded r_loaded wup_zero z_ready vt_ready sc_ready kdt_ready kv_ready "
        "o_ready o_sum o_stored z_log vtok_ready e_ready sc_fwd kdtok_ready osq_ready r_silu o_rstd o_hi "
        "rmask_ready z_min la_ready b_step dec_ready qk_weighted sc_tile state_step o_norm o_gate "
        "o_lo wpool_loaded u_loaded yb_ready gates_sig merged_hi pool_consts pool_step "
        "pooled_ready merged_lo yb_scaled merged_ready gate_silu act_hi act_full act_lo fin_done "
        "mla_loaded latent_hi rope_sin kr_copied vh_tok p_ready mixa_hi ang_step "
        "latent_lo cs_moved lat_loaded lat_sq lat_sum lat_mean lat_rstd lat_normed q_copied q_a q_rope rs_inv mixa_lo s_stat "
        "vh_t s_ready pt_ready pv_ready gates_loaded conv_loaded mv_loaded om_loaded "
        "f_log mq_stored em_row em_stored em_loaded qk_back w_summed num_copied den_ready hsq_sum conv_silu mv_tok om_sig st_exp h_sq h_rstd mixm_hi ml_consts w_ready "
        "m_step g_step conv_step st_w h_step mixm_lo am_t mv_t st_ready ho_ready "
        "y_scaled x_added up_sq sq_hi sq_lo acc_zero out_t out_ev").split()
PAIRED = ("o_back gab_loaded out_stored r_stored stored unit_out w_landed x_back").split()


def two_block_kernel(nc, A, out):
    ctx = ExitStack()

    def dram(name, shape):
        return nc.dram_tensor(name, shape, F32, kind="Internal").ap()

    x_in = A["x"][0]
    w_in = A["w_in"][0].rearrange("(k p) n -> p k n", p=P)
    w_ya = A["w_branch_gla"][0].rearrange("(k p) n -> p k n", p=P)
    w_out = A["w_out"][0].rearrange("(k p) n -> p k n", p=P)
    w_f1 = A["w_ffn_in"][0].rearrange("(k p) n -> p k n", p=P)
    w_f1o = A["w_ffn_out"][0].rearrange("(k p) n -> p k n", p=P)
    w_in2 = A["w_in_2"][0].rearrange("(k p) n -> p k n", p=P)
    w_uq = A["w_uq_2"][0].rearrange("(k p) n -> p k n", p=P)
    w_ukv = A["w_ukv_2"][0].rearrange("(k p) n -> p k n", p=P)
    w_out2 = A["w_out_2"][0].rearrange("(k p) n -> p k n", p=P)
    w_up = A["w_up_2"][0].rearrange("(k p) n -> p k n", p=P)
    w_down = A["w_down_2"][0].rearrange("(k p) n -> p k n", p=P)

    proj = dram("proj", (N_IN * P, T))
    proj2 = dram("proj2", (N_IN2 * P, T))
    o_d = dram("gla_out", (D, T))
    x_d = dram("x_feature_major", (D, T))
    x2_d = dram("x_block2", (D, T))
    x3_d = dram("x_after_mixer2", (D, T))
    r_d = dram("mlstm_log_weights", (C * 4 + 4, T))
    mq_d = dram("mlstm_q_k", (4 * P, T))

    def tile_of(t, j, n=1):
        return t[j * P:(j + n) * P, :].rearrange("(k p) t -> p k t", p=P)

    with ctx:
        def sb(name, shape, dt=F32, c=ctx):
            return c.enter_context(nc.sbuf_tensor(name, shape, dt))

        S = {n: ctx.enter_context(nc.semaphore(n)) for n in SEMS}
        for n in PAIRED:
            S[n] = [ctx.enter_context(nc.semaphore(f"{n}{i}")) for i in range(2)]
        S["r_bc_loaded"] = [ctx.enter_context(nc.semaphore(f"r_bc_loaded{i}")) for i in range(4)]

        PS = [ctx.enter_context(nc.psum_tensor(f"ps{i}", [P, T], F32)) for i in range(4)]

        acc = sb("acc", [P, KT, T])
        raw = sb("w_raw", [P, 2, KT * P])
        whi = sb("w_hi_t", [P, 2, KT * P], F32R)
        wlo = sb("w_lo_t", [P, 2, KT * P], F32R)
        stage = sb("stage", [P, 2, T])
        ssq = sb("ssq", [P, T])
        rstd = sb("rstd", [P, T])
        ident = sb("ident", [P, P])
        ones = sb("ones", [P, P])
        maskb = sb("maskb", [P, P])
        ident16 = sb("ident16", [P, P], BF16)
        negm16 = sb("negm16", [P, P], BF16)
        cols = sb("cols", [P, NVEC])
        small = sb("small", [P, 64])

        def col(name, k):
            return cols[:, VEC[name] + k:VEC[name] + k + 1]

        with ExitStack() as s:
            vtok = sb("vtok", [P, C, 256], F32, s)
            sct = sb("sct", [P, C, P], F32, s)
            St = sb("states", [P, 2, C, 256], F32, s)
            qi = sb("qi", [P, 2, T], F32, s)
            qs = sb("qs", [P, T], F32, s)
            ks = sb("ks", [P, T], F32, s)
            lt = sb("lt", [P, T], F32, s)
            kdtok = sb("kdtok", [P, C, P], F32, s)
            bt = sb("bt", [P, T], F32, s)
            kd = sb("kd", [P, T], F32, s)
            mn = sb("mn", [P, T], F32, s)
            wup = sb("wup", [32, 2, HALF], F32, s)
            with ExitStack() as s2:
                xin = sb("xin", [P, C, T], F32, s2)
                vrow = sb("vrow", [P, P], F32, s2)
            with ExitStack() as s2:
                h1hi = sb("h1hi", [P, KT, T], F32R, s2)
                h1lo = sb("h1lo", [P, KT, T], F32R, s2)
        s_m2 = ExitStack()
        m2hi = sb("m2hi", [P, KT, T], F32R, s_m2)
        m2lo = sb("m2lo", [P, KT, T], F32R, s_m2)
        with ExitStack() as s:
            oback = sb("oback", [P, KT, T], F32, s)
        with ExitStack() as s:
            m1hi = sb("m1hi", [P, KT, T], F32R, s)
            m1lo = sb("m1lo", [P, KT, T], F32R, s)
            wpool = sb("wpool", [P, 4, 256], F32, s)
        with ExitStack() as s:
            g1hi = sb("g1hi", [P, KT, T], F32R, s)
            g1lo = sb("g1lo", [P, KT, T], F32R, s)
        with ExitStack() as s:
            kT = sb("kT", [P, 8, T], F32, s)
            Vt = sb("Vt", [P, C, 8, 64], F32, s)
            x4 = sb("x4", [P, 4, T], F32, s)
        with ExitStack() as s:
            qk = sb("qk", [P, 4, T], F32, s)
            ering = sb("ering", [P, 4, T], F32, s)
            Wt = sb("Wt", [P, 3, T], F32, s)
            wsum = sb("wsum", [P, T], F32, s)
            vtok2 = sb("vtok2", [P, 2, C, P], F32, s)
        s_m2.close()
        with ExitStack() as s:
            lat_place = sb("lat_place", [P, 3, T], F32, s)
            lat = sb("lat", [P, 3, T], F32, s)
            lat_r = sb("lat_r", [P, 2, T], F32, s)
            lat_s = sb("lat_s", [P, 3, T], F32, s)
            cb = sb("cb", [P, 4, T + 4], F32, s)
        with ExitStack() as s:
            xr = sb("xr", [P, KT, T], F32, s)
            orow = sb("orow", [P, 2, T], F32, s)
        with ExitStack() as s:
            a2hi = sb("a2hi", [P, KT, T], F32R, s)
            a2lo = sb("a2lo", [P, KT, T], F32R, s)
            h3hi = sb("h3hi", [P, KT, T], F32R, s)
            h3lo = sb("h3lo", [P, KT, T], F32R, s)

        gq, gk, gv, gr = acc[:, 0, :], acc[:, 1, :], acc[:, 2:4, :], acc[:, 4:6, :]
        rmask, bm = acc[:, 6, :], acc[:, 7, :]
        bg = small[0:4, 0:2]
        lrT = ssq[0:32, :]
        block = ctx.enter_context(nc.Block())


        def load_unit(sp, u, src, nk=KT, parts=None):
            if u.c >= 2:
                sp.wait_ge(S["w_split"], u.times(1, -1))
            dst = raw[:, u.par, 0:nk * P].rearrange("p (k c) -> p k c", k=nk)
            for (a, b, s_) in parts or [(0, P, src)]:
                sp.dma_start(dst[:, :, a:b], s_).then_inc(S["w_landed"][u.par], 16)

        def split_unit(pool, u, nk=KT):
            n = nk * P
            r, h, lo = raw[:, u.par, 0:n], whi[:, u.par, 0:n], wlo[:, u.par, 0:n]
            pool.wait_ge(S["w_landed"][u.par], u.landed())
            if u.c >= 2:
                pool.wait_ge(S["unit_done"], u.times(1, -1))
            pool.tensor_tensor(h, r, ones[:, 0:1].to_broadcast([P, n]), ALU.mult).then_inc(S["w_hi"], 1)
            pool.wait_ge(S["w_hi"], u.times(1, 1))
            pool.tensor_tensor(lo, r, h.bitcast(F32), ALU.subtract).then_inc(S["w_split"], 1)

        def mm_unit(pe, u, xhi, xlo, nk=KT, wait_k=None, pair=None):
            pe.wait_ge(S["w_split"], u.times(1, 1))
            if pair is not None:
                pe.wait_ge(S["unit_out"][(u.c - 1) % 2], nth(u.c - 1))
            elif u.c >= 2:
                pe.wait_ge(S["unit_out"][u.par], u.nth(-1))
            out = PS[u.par if pair is None else pair]
            for k in range(nk):
                if wait_k:
                    wait_k(k)
                w_h = whi[:, u.par, k * P:(k + 1) * P]
                w_l = wlo[:, u.par, k * P:(k + 1) * P]
                for n, (w, x) in enumerate(((w_h, xhi), (w_h, xlo), (w_l, xhi))):
                    for b in range(2):
                        mm = pe.matmul(out[:, b * HALF:(b + 1) * HALF], w,
                                       x[:, k, b * HALF:(b + 1) * HALF],
                                       start=(k == 0 and n == 0), stop=(k == nk - 1 and n == 2))
            mm.then_inc(S["unit_done"], 1)


        def norm_square(act, name, k, src):
            m = SQ_BASE[name] + k
            if m >= 2:
                act.wait_ge(S["sq_added"], m - 1)
            act.activation(stage[:, m % 2, :], src, ACT.Square).then_inc(S["sq_done"], 1)

        def norm_add(dve, name, k):
            m = SQ_BASE[name] + k
            n = NORM_AT[name]
            dve.wait_ge(S["sq_done"], m + 1)
            if k == 0:
                if n:
                    dve.wait_ge(S["rstd_ready"], n)
                dve.tensor_copy(ssq[:, :], stage[:, m % 2, :]).then_inc(S["sq_added"], 1)
            else:
                dve.wait_ge(S["sq_added"], m)
                dve.tensor_tensor(ssq[:, :], ssq[:, :], stage[:, m % 2, :], ALU.add)\
                   .then_inc(S["sq_added"], 1)

        def norm_sum(pe, name, nk):
            pe.wait_ge(S["sq_added"], SQ_BASE[name] + nk)
            for b in range(2):
                mm = pe.matmul(PS[2][:, b * HALF:(b + 1) * HALF], ones[:, :],
                               ssq[:, b * HALF:(b + 1) * HALF], start=True, stop=True)
            mm.then_inc(S["norm_sum"], 1)

        def norm_mean(dve, name, nk):
            n = NORM_AT[name] + 1
            dve.wait_ge(S["norm_sum"], n)
            dve.tensor_scalar(ssq[:, :], PS[2][:, :], 1.0 / (nk * P), EPS, ALU.mult, ALU.add)\
               .then_inc(S["norm_mean"], 1)
            dve.wait_ge(S["norm_mean"], 2 * n - 1)
            dve.reciprocal(ssq[:, :], ssq[:, :]).then_inc(S["norm_mean"], 1)

        def norm_root(act, name, dst):
            act.wait_ge(S["norm_mean"], 2 * (NORM_AT[name] + 1))
            act.activation(dst, ssq[:, :], ACT.Sqrt).then_inc(S["rstd_ready"], 1)

        def scale_hi(act, k, src, g, hi):
            act.activation(hi[:, k, :], src, ACT.Copy, scale=g).then_inc(S["hi_ready"], 1)

        def scale_lo(dve, at, k, src, g, hi, lo):
            dve.wait_ge(S["hi_ready"], at + k + 1)
            dve.scalar_tensor_tensor(out=lo[:, k, :], in0=src, scalar=g, in1=hi[:, k, :].bitcast(F32),
                                     op0=ALU.mult, op1=ALU.subtract).then_inc(S["lo_ready"], 1)

        OPERAND = {"mix": 0, "ffn": 8, "mix2": 16, "mlp": 24}

        def norm_act(act, name, ready, g=None, hi=None, src=acc, nk=KT, dst=rstd):
            for k in range(nk):
                ready(act, k)
                if hi is not None:
                    scale_hi(act, k, src[:, k, :], col(g, k), hi)
                norm_square(act, name, k, src[:, k, :])
            norm_root(act, name, dst[:, :])

        def norm_dve(dve, name, ready, g=None, hi=None, lo=None, src=acc, nk=KT):
            for k in range(nk):
                if hi is not None:
                    scale_lo(dve, OPERAND[name], k, src[:, k, :], col(g, k), hi, lo)
                norm_add(dve, name, k)
            norm_mean(dve, name, nk)

        def lo_wait(pe, name):
            return lambda k: pe.wait_ge(S["lo_ready"], OPERAND[name] + k + 1)

        def no_wait(eng, k):
            pass

        def stores_before(u, first, before):
            f = first if first % 2 == u.par else first + 1
            return u.nth(-(f // 2 + 1) + before[u.par])

        def store_dve(dve, u, first, before, pair=None):
            dve.wait_ge(S["unit_done"], u.times(1, 1))
            if not (u.s == 0 and stores_before(u, first, before) == 0):
                v = stores_before(u, first, before)
                dve.wait_ge(S["stored"][u.par], v * 16)
            dve.tensor_tensor(stage[:, u.par, :], PS[u.par if pair is None else pair][:, :], rstd[:, :],
                              ALU.mult).then_inc(S["unit_out"][u.par], 1)

        def store_act(act, u, dst):
            act.wait_ge(S["unit_out"][u.par], u.nth())
            act.dma_start(dst, stage[:, u.par, :]).then_inc(S["stored"][u.par], 16)

        ALL_IN = (16 * ((N_IN + 1) // 2), 16 * (N_IN // 2))
        B2 = ((N_IN + 1) // 2, N_IN // 2)
        N0_IN2 = sum((U_IN2 + j) % 2 == 0 for j in range(N_IN2))
        ALL_IN2 = (ALL_IN[0] + 16 * N0_IN2, ALL_IN[1] + 16 * (N_IN2 - N0_IN2))

        def all_stored(eng, counts):
            for i in range(2):
                eng.wait_ge(S["stored"][i], counts[i])

        def ffn_order(groups, per_tile, u0, name):
            order = [("in", 0)]
            for g in range(1, len(groups)):
                order += [("in", g), ("out", g - 1)]
            order.append(("out", len(groups) - 1))
            seg, u = [], u0
            for kind, g in order:
                seg.append((kind, g, u))
                u += per_tile * groups[g] if kind == "in" else KT
            return seg

        SEG1 = ffn_order(G1, 2, U_F1, "f1")
        SEG2 = ffn_order(G2, 1, U_F2, "f2")

        def run_ffn(eng, seg, groups, per_tile, do):
            full = sum(g == G for g in groups)
            loops = (full - 1) // 2
            stride = 2 * (per_tile * G + KT)
            do(eng, seg[0][0], Step(0), Step(seg[0][2]), G)
            with eng.Fori(0, loops) as i:
                for kind, g, u in seg[1:5]:
                    do(eng, kind, Step(g, 2, i), Step(u, stride, i), G)
            for kind, g, u in seg[1 + 4 * loops:]:
                do(eng, kind, Step(g), Step(u), groups[g])

        N_CONST = 9

        def start_pool(pool):
            pool.memset(ident[:, :], 0.0).then_inc(S["consts_ready"], 1)
            pool.memset(ones[:, :], 1.0).then_inc(S["consts_ready"], 1)
            pool.memset(maskb[:, :], 1.0).then_inc(S["consts_ready"], 1)
            pool.memset(negm16[:, :], 0.0).then_inc(S["consts_ready"], 1)
            pool.memset(ident16[:, :], 0.0).then_inc(S["consts_ready"], 1)
            pool.wait_ge(S["consts_ready"], 5)
            pool.affine_select(out=ident[:, :], in_=ident[:, :], compare_op=ALU.not_equal, fill=1.0, base=0,
                               pattern=[[-1, P]], channel_multiplier=1).then_inc(S["consts_ready"], 1)
            pool.affine_select(out=maskb[:, :], in_=maskb[:, :], compare_op=ALU.is_gt, fill=0.0, base=0,
                               pattern=[[-1, P]], channel_multiplier=1).then_inc(S["consts_ready"], 1)
            pool.affine_select(out=negm16[:, :], in_=negm16[:, :], compare_op=ALU.is_ge, fill=-BIG, base=0,
                               pattern=[[-1, P]], channel_multiplier=1).then_inc(S["consts_ready"], 1)
            pool.affine_select(out=ident16[:, :], in_=ident16[:, :], compare_op=ALU.not_equal, fill=1.0, base=0,
                               pattern=[[-1, P]], channel_multiplier=1).then_inc(S["consts_ready"], 1)

        def start_sp(sp):
            for h in range(2):
                sp.dma_start(xin[:, 4 * h:4 * h + 4, :],
                             x_in[4 * h * P:(4 * h + 4) * P, :].rearrange("(c p) d -> p c d", p=P))\
                  .then_inc(S["x_loaded"], 16)
            for name, n in VEC_ROWS:
                v = A[name][0] if len(A[name].shape) > 1 else A[name]
                if len(v.shape) == 2:
                    v = v.rearrange("a n -> (a n)")
                sp.dma_start(vrow[VEC[name]:VEC[name] + n, :], v.rearrange("(k p) -> k p", p=P))\
                  .then_inc(S["vec_loaded"], 16)

        def start_pe(pe):
            pe.wait_ge(S["consts_ready"], N_CONST)
            pe.wait_ge(S["vec_loaded"], 16 * len(VEC_ROWS))
            pe.transpose(PS[2][:, 0:NVEC], vrow[0:NVEC, :], ident[0:NVEC, 0:NVEC]).then_inc(S["vec_t"], 1)
            pe.wait_ge(S["x_loaded"], 32)
            for h in range(2):
                for k in range(KT):
                    n = h * KT + k
                    if n >= 4:
                        pe.wait_ge(S["xt_ev"], n - 3)
                    bank = PS[n % 4 // 2][:, n % 2 * HALF:n % 2 * HALF + HALF]
                    for c in range(4):
                        tr = pe.transpose(bank[:, c * P:(c + 1) * P],
                                          xin[:, 4 * h + c, k * P:(k + 1) * P], ident[:, :])
                    tr.then_inc(S["xt_tr"], 1)

        def start_act(act):
            act.wait_ge(S["vec_t"], 1)
            act.activation(cols[:, :], PS[2][:, 0:NVEC], ACT.Copy).then_inc(S["cols_ready"], 1)
            for h in range(2):
                for k in range(KT):
                    n = h * KT + k
                    act.wait_ge(S["xt_tr"], n + 1)
                    act.activation(acc[:, k, h * HALF:(h + 1) * HALF],
                                   PS[n % 4 // 2][:, n % 2 * HALF:n % 2 * HALF + HALF], ACT.Copy)\
                       .then_inc(S["xt_ev"], 1)
            act.wait_ge(S["xt_ev"], 2 * KT)
            act.dma_start(tile_of(x_d, 0, KT), acc[:, :, :]).then_inc(S["x_spilled"], 16)
            act.wait_ge(S["cols_ready"], 1)

        LR0 = 3072
        REST0 = LR0 + 32

        def in_steps(eng, do):
            for j in range(2):
                do(eng, Step(j), j * P, j)
            with eng.Fori(0, 11) as i:
                for j in range(2):
                    do(eng, Step(2 + j, 2, i), i * (2 * P) + (2 + j) * P, None, i * (2 * P) + (2 + j) * P)
            do(eng, Step(24), LR0, 24)

        def in_sp(sp):
            def do(e, u, c0, j, r0=None):
                load_unit(e, u, w_in[:, :, bass.ds(c0, P)] if j is None else w_in[:, :, c0:c0 + P])
            in_steps(sp, do)

        def in_pool(pool):
            in_steps(pool, lambda e, u, c0, j, r0=None: split_unit(e, u))

        def in_pe(pe):
            def do(e, u, c0, j, r0=None):
                first = j == 0
                mm_unit(e, u, h1hi, h1lo, wait_k=lo_wait(e, "mix") if first else None)
                if first:
                    norm_sum(e, "mix", KT)
            in_steps(pe, do)

        def in_act(act):
            def do(e, u, c0, j, r0=None):
                store_act(e, u, proj[bass.ds(r0, P), :] if j is None else proj[j * P:(j + 1) * P, :])
            in_steps(act, do)

        def in_dve(dve):
            dve.wait_ge(S["rstd_ready"], NORM_AT["mix"] + 1)
            in_steps(dve, lambda e, u, c0, j, r0=None: store_dve(e, u, 0, (0, 0)))

        NORM16 = 1.0 / 16.0
        QSCALE = float(P) ** -0.5
        MID, END = (63, 64), (P - 1, 0)
        Ering = [lt[:, :], mn[:, :]]
        MID0 = 25
        MIDS = (N_IN - MID0) // GH

        def order(d):
            return list(range(C)) if d == 0 else list(range(C - 1, -1, -1))

        def mid_weights(sp, u):
            c0 = REST0 + (u - MID0) * P
            if u < N_IN:
                load_unit(sp, Step(u), w_in[:, :, c0:c0 + P])
            else:
                ya_wo_unit(sp, u - N_IN)

        def gla_sp(sp):
            for u in (MID0, MID0 + 1):
                mid_weights(sp, u)
            sp.wait_ge(S["x_spilled"], 16)
            for i in range(2):
                sp.wait_ge(S["stored"][i], 16 * ((MID0 + 1 - i) // 2))
            sp.dma_start(lrT, proj[24 * P:24 * P + 32, :]).then_inc(S["gla_loaded"], 16)

            def qkv(h):
                if h:
                    sp.wait_ge(S["qk_weighted"], 8 * h)
                sp.dma_start(gq, proj[h * P:(h + 1) * P, :]).then_inc(S["qk_loaded"], 16)
                sp.dma_start(gk, proj[(4 + h) * P:(5 + h) * P, :]).then_inc(S["qk_loaded"], 16)
                if h:
                    sp.wait_ge(S["vt_ready"], 2 * h)
                sp.dma_start(gv, tile_of(proj, 8 + 2 * h, 2)).then_inc(S["v_loaded"], 16)

            def gate(h):
                if h:
                    sp.wait_ge(S["o_gate"], 4 * h)
                sp.dma_start(gr, tile_of(proj, 16 + 2 * h, 2)).then_inc(S["r_loaded"], 16)

            qkv(0)
            gate(0)
            for h in range(GH):
                for i in range(MIDS):
                    u = Step(MID0 + MIDS * h + i)
                    sp.wait_ge(S["unit_out"][u.par], u.nth())
                    sp.dma_start(proj[u.c * P:(u.c + 1) * P, :], stage[:, u.par, :])\
                      .then_inc(S["stored"][u.par], 16)
                    mid_weights(sp, u.c + 2)
                    if i == 2 and h < GH - 1:
                        qkv(h + 1)
                if h < GH - 1:
                    gate(h + 1)

        def mid_pool(pool):
            for u in range(MID0, N_IN):
                split_unit(pool, Step(u))

        def wup_pool(pool):
            pool.memset(wup[:, :, :], 0.0).then_inc(S["wup_zero"], 1)

        def wup_sp(sp):
            sp.wait_ge(S["wup_zero"], 1)
            sp.dma_start(wup[0:16, 0, :], A["w_decay_up_fwd"][0]).then_inc(S["gla_loaded"], 16)
            sp.dma_start(wup[16:32, 1, :], A["w_decay_up_bwd"][0]).then_inc(S["gla_loaded"], 16)

        def gla_pe(pe):
            pe.wait_ge(S["gla_loaded"], 48)
            pe.wait_ge(S["unit_out"][1], MID0 // 2)

            def z(h, d):
                if d == 0 and h:
                    pe.wait_ge(S["o_norm"], 3 * h - 1)
                if d == 1:
                    pe.wait_ge(S["sc_fwd"], h + 1)
                for b in range(2):
                    mm = pe.matmul(PS[3 - 2 * d][:, b * HALF:(b + 1) * HALF], wup[:, d, h * P:(h + 1) * P],
                                   lrT[:, b * HALF:(b + 1) * HALF], start=True, stop=True)
                mm.then_inc(S["z_ready"], 1)

            def turn_v(h):
                pe.wait_ge(S["v_loaded"], 16 * (h + 1))
                if h:
                    pe.wait_ge(S["o_gate"], 4 * h - 1)
                for half in range(2):
                    if half:
                        pe.wait_ge(S["z_min"], 2 * h + 1)
                        pe.wait_ge(S["z_log"], 6 * h + 1)
                    for c in range(4):
                        for e in range(2):
                            tr = pe.transpose(PS[2 + half][:, c * 256 + e * P:c * 256 + (e + 1) * P],
                                              gv[:, e, (4 * half + c) * P:(4 * half + c + 1) * P], ident[:, :])
                    tr.then_inc(S["vt_ready"], 1)

            def scores(h, d):
                n = 2 * h + d
                pe.wait_ge(S["qk_weighted"], 4 * n + 3)
                if d == 0 and h:
                    pe.wait_ge(S["o_gate"], 4 * h - 3)
                if d == 1:
                    pe.wait_ge(S["z_min"], n + 1)
                    pe.wait_ge(S["z_log"], 3 * n + 1)
                for c in range(C):
                    mm = pe.matmul(PS[1][:, c * P:(c + 1) * P], ks[:, c * P:(c + 1) * P],
                                   qs[:, c * P:(c + 1) * P], start=True, stop=True)
                mm.then_inc(S["sc_ready"], 1)

            def turn_k(h, d):
                n = 2 * h + d
                pe.wait_ge(S["qk_weighted"], 4 * n + 4)
                pe.wait_ge(S["vtok_ready"], 2 * h + 2)
                if n:
                    pe.wait_ge(S["state_step"], 7 * n)
                for c in range(C):
                    tr = pe.transpose(PS[2][:, c * P:(c + 1) * P], kd[:, c * P:(c + 1) * P], ident[:, :])
                tr.then_inc(S["kdt_ready"], 1)

            def keys_values(h, d):
                pe.wait_ge(S["kdtok_ready"], 2 * h + d + 1)
                for i, c in enumerate(order(d)[:C - 1]):
                    mm = pe.matmul(PS[3 - i // 4][:, i % 4 * 256:(i % 4 + 1) * 256], kdtok[:, c, :],
                                   vtok[:, c, :], start=True, stop=True)
                    if i == 3:
                        mm.then_inc(S["kv_ready"], 1)
                mm.then_inc(S["kv_ready"], 1)

            def output(h):
                pe.wait_ge(S["sc_tile"], h + 1)
                pe.wait_ge(S["state_step"], 14 * h + 14)
                pe.wait_ge(S["qk_weighted"], 8 * h + 5)
                for e in range(2):
                    for c in range(C):
                        o = PS[1 + e][:, c * P:(c + 1) * P]
                        terms = [(vtok[:, c, e * P:(e + 1) * P], sct[:, c, :])]
                        if c > 0:
                            terms.append((St[:, 0, c, e * P:(e + 1) * P], qi[:, 0, c * P:(c + 1) * P]))
                        if c < C - 1:
                            terms.append((St[:, 1, c, e * P:(e + 1) * P], qi[:, 1, c * P:(c + 1) * P]))
                        for i, (w, x) in enumerate(terms):
                            mm = pe.matmul(o, w, x, start=(i == 0), stop=(i == len(terms) - 1))
                    mm.then_inc(S["o_ready"], 1)

            def square_sum(h):
                pe.wait_ge(S["o_norm"], 3 * h + 1)
                for b in range(2):
                    mm = pe.matmul(PS[3][:, b * HALF:(b + 1) * HALF], ones[:, :],
                                   mn[:, b * HALF:(b + 1) * HALF], start=True, stop=True)
                mm.then_inc(S["o_sum"], 1)

            def mid_unit(h, i):
                mm_unit(pe, Step(MID0 + MIDS * h + i), h1hi, h1lo, pair=0)

            for h in range(GH):
                z(h, 0)
                mid_unit(h, 0)
                turn_v(h)
                scores(h, 0)
                turn_k(h, 0)
                z(h, 1)
                keys_values(h, 0)
                mid_unit(h, 1)
                mid_unit(h, 2)
                scores(h, 1)
                turn_k(h, 1)
                keys_values(h, 1)
                mid_unit(h, 3)
                output(h)
                mid_unit(h, 4)
                square_sum(h)

        def gla_act(act):
            def store_o(h):
                for e in range(2):
                    act.wait_ge(S["o_gate"], 2 * (2 * h + e + 1))
                    act.dma_start(o_d[(2 * h + e) * P:(2 * h + e + 1) * P, :], (kd if e == 0 else bt)[:, :])\
                       .then_inc(S["o_stored"], 16)

            for h in range(GH):
                for d in range(2):
                    n = 2 * h + d
                    bias = col("b_decay_bwd" if d else "b_decay_fwd", h)
                    act.wait_ge(S["z_ready"], n + 1)
                    if n:
                        act.wait_ge(S["qk_weighted"], 4 * n - 1)
                    act.activation(lt[:, :], PS[3 - 2 * d][:, :], ACT.Abs, bias=bias).then_inc(S["z_log"], 1)
                    act.wait_ge(S["z_log"], 3 * n + 1)
                    act.activation(lt[:, :], lt[:, :], ACT.Exp, scale=-1.0).then_inc(S["z_log"], 1)
                    act.wait_ge(S["z_log"], 3 * n + 2)
                    act.activation(lt[:, :], lt[:, :], ACT.Ln, bias=1.0).then_inc(S["z_log"], 1)
                    if d == 0 and h:
                        store_o(h - 1)
                    for i, (ready, src, scale) in enumerate(
                            ((1, bt, NORM16), (2, bm, NORM16), (2, bm, -NORM16), (3, bm, NORM16))):
                        m = 4 * n + i
                        act.wait_ge(S["b_step"], 3 * n + ready)
                        if m >= 2:
                            act.wait_ge(S["qk_weighted"], m - 1)
                        act.activation(Ering[m % 2], src[:, :], ACT.Exp, scale=scale).then_inc(S["e_ready"], 1)
                    if d == 0:
                        for half in range(2):
                            act.wait_ge(S["vt_ready"], 2 * h + half + 1)
                            if h:
                                act.wait_ge(S["o_ready"], 2 * h)
                            act.activation(vtok[:, 4 * half:4 * half + 4, :],
                                           PS[2 + half][:, :].rearrange("p (c e) -> p c e", c=4), ACT.Copy)\
                               .then_inc(S["vtok_ready"], 1)
                    if d == 0:
                        act.wait_ge(S["sc_ready"], n + 1)
                        if h:
                            act.wait_ge(S["o_ready"], 2 * h)
                        act.activation(sct[:, :, :], PS[1][:, :].rearrange("p (c s) -> p c s", c=C), ACT.Copy)\
                           .then_inc(S["sc_fwd"], 1)
                    act.wait_ge(S["kdt_ready"], n + 1)
                    if n:
                        act.wait_ge(S["kv_ready"], 2 * n)
                    act.activation(kdtok[:, :, :], PS[2][:, :].rearrange("p (c s) -> p c s", c=C), ACT.Copy)\
                       .then_inc(S["kdtok_ready"], 1)
                for e in range(2):
                    act.wait_ge(S["o_ready"], 2 * h + e + 1)
                    act.activation((qs if e == 0 else ks)[:, :], PS[1 + e][:, :], ACT.Square)\
                       .then_inc(S["osq_ready"], 1)
                act.wait_ge(S["r_loaded"], 16 * (h + 1))
                act.activation(gr, gr, ACT.Silu).then_inc(S["r_silu"], 1)
                act.wait_ge(S["o_norm"], 3 * h + 3)
                act.activation(mn[:, :], mn[:, :], ACT.Sqrt).then_inc(S["o_rstd"], 1)
            store_o(GH - 1)

        def gla_dve(dve):
            dve.wait_ge(S["x_spilled"], 16)
            dve.memset(rmask, 1.0).then_inc(S["rmask_ready"], 1)
            dve.wait_ge(S["rmask_ready"], 1)
            r3 = rmask.rearrange("p (c t) -> p c t", c=C)
            dve.memset(r3[:, :, 0:1], 0.0).then_inc(S["rmask_ready"], 1)
            dve.wait_ge(S["rmask_ready"], 2)
            dve.wait_ge(S["cols_ready"], 1)

            def evacuate(h, i):
                store_dve(dve, Step(MID0 + MIDS * h + i), 0, (0, 0), pair=0)

            for h in range(GH):
                for d in range(2):
                    n = 2 * h + d
                    bias = col("b_decay_bwd" if d else "b_decay_fwd", h)
                    dve.wait_ge(S["z_log"], 3 * n + 1)
                    if n:
                        dve.wait_ge(S["qk_weighted"], 4 * n)
                    if h and d == 0:
                        dve.wait_ge(S["o_gate"], 4 * h)
                    dve.tensor_scalar(mn[:, :], PS[3 - 2 * d][:, :], bias, 0.0, ALU.add, ALU.min)\
                       .then_inc(S["z_min"], 1)
                    dve.wait_ge(S["z_log"], 3 * n + 3)
                    dve.wait_ge(S["z_min"], n + 1)
                    dve.tensor_tensor(mn[:, :], mn[:, :], lt[:, :], ALU.subtract).then_inc(S["la_ready"], 1)
                    dve.wait_ge(S["la_ready"], n + 1)
                    if n:
                        dve.wait_ge(S["e_ready"], 4 * n)
                    if h and d == 0:
                        dve.wait_ge(S["o_stored"], 32 * h)
                    st = slice(None) if d == 0 else slice(None, None, -1)
                    dve.tensor_tensor_scan(bt[:, st], rmask, mn[:, st], 0.0, ALU.mult, ALU.add)\
                       .then_inc(S["b_step"], 1)
                    dve.wait_ge(S["b_step"], 3 * n + 1)
                    b3 = bt[:, :].rearrange("p (c t) -> p c t", c=C)
                    bm3 = bm.rearrange("p (c t) -> p c t", c=C)
                    dve.tensor_tensor(bm3, b3, b3[:, :, MID[d]:MID[d] + 1].to_broadcast([P, C, P]),
                                      ALU.subtract).then_inc(S["b_step"], 1)
                    if d == 0:
                        dve.wait_ge(S["qk_loaded"], 32 * (h + 1))
                    if d == 1:
                        evacuate(h, 1)
                    m = 4 * n
                    dve.wait_ge(S["e_ready"], m + 1)
                    e3 = Ering[0].rearrange("p (c t) -> p c t", c=C)
                    dve.tensor_copy(small[:, 40:40 + C].rearrange("p (c o) -> p c o", o=1),
                                    e3[:, :, END[d]:END[d] + 1]).then_inc(S["dec_ready"], 1)
                    if h:
                        dve.wait_ge(S["o_ready"], 2 * h)
                    dve.scalar_tensor_tensor(out=qi[:, d, :], in0=gq, scalar=QSCALE, in1=Ering[0],
                                             op0=ALU.mult, op1=ALU.mult).then_inc(S["qk_weighted"], 1)
                    dve.wait_ge(S["e_ready"], m + 2)
                    if n:
                        dve.wait_ge(S["sc_ready"], n)
                    if h and d == 0:
                        dve.wait_ge(S["o_norm"], 3 * h - 2)
                    dve.scalar_tensor_tensor(out=qs[:, :], in0=gq, scalar=QSCALE, in1=Ering[1],
                                             op0=ALU.mult, op1=ALU.mult).then_inc(S["qk_weighted"], 1)
                    dve.wait_ge(S["e_ready"], m + 3)
                    dve.tensor_tensor(bm3, b3[:, :, END[d]:END[d] + 1].to_broadcast([P, C, P]), b3,
                                      ALU.subtract).then_inc(S["b_step"], 1)
                    dve.tensor_tensor(ks[:, :], gk, Ering[0], ALU.mult).then_inc(S["qk_weighted"], 1)
                    if d == 0:
                        evacuate(h, 0)
                    dve.wait_ge(S["e_ready"], m + 4)
                    if n:
                        dve.wait_ge(S["kdt_ready"], n)
                    dve.tensor_tensor(kd[:, :], gk, Ering[1], ALU.mult).then_inc(S["qk_weighted"], 1)
                    if d == 1:
                        evacuate(h, 2)
                    if d == 1:
                        dve.wait_ge(S["sc_ready"], n + 1)
                        dve.wait_ge(S["sc_fwd"], h + 1)
                        dve.copy_predicated(
                            sct[:, :, :],
                            maskb[:, :].bitcast(I32).rearrange("p (o s) -> p o s", o=1).to_broadcast([P, C, P]),
                            PS[1][:, :].rearrange("p (c s) -> p c s", c=C)).then_inc(S["sc_tile"], 1)
                    od = order(d)
                    dve.wait_ge(S["dec_ready"], n + 1)
                    for i in range(C - 1):
                        if i == 0:
                            dve.wait_ge(S["kv_ready"], 2 * n + 1)
                        if i == 4:
                            dve.wait_ge(S["kv_ready"], 2 * n + 2)
                        kv = PS[3 - i // 4][:, i % 4 * 256:(i % 4 + 1) * 256]
                        if i == 0:
                            ins = dve.tensor_copy(St[:, d, od[1], :], kv)
                        else:
                            dve.wait_ge(S["state_step"], (C - 1) * n + i)
                            ins = dve.scalar_tensor_tensor(
                                out=St[:, d, od[i + 1], :], in0=St[:, d, od[i], :],
                                scalar=small[:, 40 + od[i]:41 + od[i]], in1=kv, op0=ALU.mult, op1=ALU.add)
                        ins.then_inc(S["state_step"], 1)
                evacuate(h, 3)
                dve.wait_ge(S["osq_ready"], 2 * h + 2)
                dve.tensor_tensor(mn[:, :], qs[:, :], ks[:, :], ALU.add).then_inc(S["o_norm"], 1)
                evacuate(h, 4)
                dve.wait_ge(S["o_sum"], h + 1)
                dve.tensor_scalar(mn[:, :], PS[3][:, :], 1.0 / 256, EPS, ALU.mult, ALU.add)\
                   .then_inc(S["o_norm"], 1)
                dve.wait_ge(S["o_norm"], 3 * h + 2)
                dve.reciprocal(mn[:, :], mn[:, :]).then_inc(S["o_norm"], 1)
                dve.wait_ge(S["o_rstd"], h + 1)
                dve.wait_ge(S["r_silu"], h + 1)
                dve.wait_ge(S["kdt_ready"], 2 * h + 2)
                for e in range(2):
                    t = (kd if e == 0 else bt)[:, :]
                    dve.scalar_tensor_tensor(out=t, in0=PS[1 + e][:, :], scalar=col("gla_norm", 2 * h + e),
                                             in1=mn[:, :], op0=ALU.mult, op1=ALU.mult)\
                       .then_inc(S["o_gate"], 1)
                    dve.wait_ge(S["o_gate"], 2 * (2 * h + e + 1) - 1)
                    dve.tensor_tensor(t, t, gr[:, e, :], ALU.mult).then_inc(S["o_gate"], 1)

        ub, csb, pooled = acc[:, 0, :], acc[:, 1:3, :].rearrange("p a t -> p (a t)"), acc[:, 3, :]
        gab = [(acc[:, 4, :], acc[:, 6, :]), (acc[:, 5, :], acc[:, 7, :])]
        ones_row = ssq
        Z0 = 8

        def ya_wo_unit(sp, j):
            w = w_ya if j < KT else w_out
            load_unit(sp, Step(U_YA + j), w[:, :, j % KT * P:(j % KT + 1) * P])

        def merge_sp(sp):
            sp.wait_ge(S["o_stored"], 32 * (GH - 1))
            sp.wait_ge(S["unit_done"], N_IN)
            sp.wait_ge(S["z_ready"], 2 * GH)
            sp.dma_start(oback[:, 0:6, :], tile_of(o_d, 0, 6)).then_inc(S["o_back"][0], 16)
            sp.wait_ge(S["o_gate"], 4 * GH)
            all_stored(sp, ALL_IN)
            sp.dma_start(wpool[:, :, :], A["w_pool_group"][0].rearrange("g c d -> c g d"))\
              .then_inc(S["wpool_loaded"], 16)
            for j in range(KT):
                g = j // 2
                if j % 2 == 0:
                    if g:
                        sp.wait_ge(S["pooled_ready"], g)
                    sp.dma_start(ub, proj[(25 + g) * P:(26 + g) * P, :]).then_inc(S["u_loaded"], 16)
                if j >= 2:
                    sp.wait_ge(S["merged_ready"], j - 1)
                a, b = gab[j % 2]
                sp.dma_start(a, proj[(29 + j) * P:(30 + j) * P, :]).then_inc(S["gab_loaded"][j % 2], 16)
                sp.dma_start(b, proj[(37 + j) * P:(38 + j) * P, :]).then_inc(S["gab_loaded"][j % 2], 16)
                if j == 0:
                    sp.wait_ge(S["o_stored"], 32 * GH)
                    sp.dma_start(oback[:, 6:8, :], tile_of(o_d, 6, 2)).then_inc(S["o_back"][1], 16)
                ya_wo_unit(sp, j + 2)

        def merge_pe(pe):
            pe.wait_ge(S["wpool_loaded"], 16)
            pe.wait_ge(S["o_gate"], 4 * GH)
            for j in range(KT):
                mm_unit(pe, Step(U_YA + j), m2hi, m2lo,
                        wait_k=(lambda k: pe.wait_ge(S["o_lo"], k + 1)) if j == 0 else None)
                pe.wait_ge(S["pooled_ready"], j // 2 + 1)
                if j:
                    pe.wait_ge(S["yb_scaled"], j)
                for b in range(2):
                    mm = pe.matmul(PS[2][:, b * HALF:(b + 1) * HALF], wpool[:, j // 2, j % 2 * P:(j % 2 + 1) * P],
                                   pooled[:, b * HALF:(b + 1) * HALF], start=True, stop=True)
                mm.then_inc(S["yb_ready"], 1)

        def merge_act(act):
            act.wait_ge(S["o_ready"], 2 * GH)
            for k in range(KT):
                act.wait_ge(S["o_back"][k // 6], 16)
                act.activation(m2hi[:, k, :], oback[:, k, :], ACT.Copy).then_inc(S["o_hi"], 1)
            for j in range(KT):
                a, b = gab[j % 2]
                act.wait_ge(S["gab_loaded"][j % 2], 32 * (j // 2 + 1))
                act.activation(a, a, ACT.Sigmoid).then_inc(S["gates_sig"], 1)
                act.activation(b, b, ACT.Sigmoid).then_inc(S["gates_sig"], 1)
                act.wait_ge(S["merged_ready"], j + 1)
                act.activation(m1hi[:, j, :], stage[:, j % 2, :], ACT.Copy).then_inc(S["merged_hi"], 1)

        def merge_dve(dve):
            dve.wait_ge(S["o_stored"], 32 * GH)
            for k in range(KT):
                dve.wait_ge(S["o_hi"], k + 1)
                dve.tensor_tensor(m2lo[:, k, :], oback[:, k, :], m2hi[:, k, :].bitcast(F32), ALU.subtract)\
                   .then_inc(S["o_lo"], 1)
            all_stored(dve, ALL_IN)
            dve.wait_ge(S["z_ready"], 2 * GH)
            dve.memset(ones_row[:, :], 1.0).then_inc(S["pool_consts"], 1)
            dve.memset(csb[:, 0:Z0 + 1], 0.0).then_inc(S["pool_consts"], 1)
            dve.wait_ge(S["pool_consts"], 1)

            def pool(g):
                w = 2 << g
                h = w // 2
                dve.wait_ge(S["u_loaded"], 16 * (g + 1))
                dve.tensor_tensor_scan(csb[:, Z0 + 1:Z0 + 1 + T], ones_row[:, :], ub, 0.0, ALU.mult, ALU.add)\
                   .then_inc(S["pool_step"], 1)
                dve.wait_ge(S["pool_step"], 3 * g + 1)
                dve.tensor_copy(csb[:, Z0 + 1 + T:Z0 + 8 + T], csb[:, Z0 + T:Z0 + T + 1].to_broadcast([P, 7]))\
                   .then_inc(S["pool_step"], 1)
                dve.wait_ge(S["pool_step"], 3 * g + 2)
                dve.wait_ge(S["pool_consts"], 2)
                if g:
                    dve.wait_ge(S["yb_ready"], 2 * g)
                dve.tensor_tensor(pooled, csb[:, Z0 + h:Z0 + h + T], csb[:, Z0 - h:Z0 - h + T], ALU.subtract)\
                   .then_inc(S["pool_step"], 1)
                dve.wait_ge(S["pool_step"], 3 * g + 3)
                edges = [(t, t + h) for t in range(h)] + [(t, T - t + h) for t in range(T - h + 1, T)]
                dve.scalar_tensor_tensor(out=pooled[:, h:T - h + 1], in0=pooled[:, h:T - h + 1], scalar=1.0 / w,
                                         in1=ub[:, h:T - h + 1], op0=ALU.mult, op1=ALU.subtract)
                for n, (t, count) in enumerate(edges):
                    ins = dve.scalar_tensor_tensor(out=pooled[:, t:t + 1], in0=pooled[:, t:t + 1],
                                                   scalar=1.0 / count, in1=ub[:, t:t + 1],
                                                   op0=ALU.mult, op1=ALU.subtract)
                ins.then_inc(S["pooled_ready"], 1)

            def split_lo(j):
                dve.wait_ge(S["merged_hi"], j + 1)
                dve.tensor_tensor(m1lo[:, j, :], stage[:, j % 2, :], m1hi[:, j, :].bitcast(F32), ALU.subtract)\
                   .then_inc(S["merged_lo"], 1)

            for j in range(KT):
                a, b = gab[j % 2]
                u = Step(U_YA + j)
                if j % 2 == 0:
                    pool(j // 2)
                if j:
                    split_lo(j - 1)
                dve.wait_ge(S["yb_ready"], j + 1)
                dve.wait_ge(S["gates_sig"], 2 * j + 2)
                dve.scalar_tensor_tensor(out=b, in0=PS[2][:, :], scalar=col("pool_scale", j), in1=b,
                                         op0=ALU.mult, op1=ALU.mult).then_inc(S["yb_scaled"], 1)
                dve.wait_ge(S["unit_done"], u.times(1, 1))
                dve.wait_ge(S["gates_sig"], 2 * j + 1)
                dve.tensor_tensor(a, PS[u.par][:, :], a, ALU.mult).then_inc(S["unit_out"][u.par], 1)
                dve.wait_ge(S["unit_out"][u.par], u.nth())
                dve.wait_ge(S["yb_scaled"], j + 1)
                dve.tensor_tensor(stage[:, j % 2, :], a, b, ALU.add).then_inc(S["merged_ready"], 1)
            split_lo(KT - 1)

        def wo_sp(sp):
            sp.wait_ge(S["merged_ready"], KT)
            sp.wait_ge(S["pooled_ready"], 4)
            sp.wait_ge(S["yb_ready"], KT)
            for i in range(2):
                sp.dma_start(acc[:, 4 * i:4 * i + 4, :], tile_of(x_d, 4 * i, 4)).then_inc(S["x_back"][i], 16)
            for j in range(KT + 2, 2 * KT):
                ya_wo_unit(sp, j)

        def wo_pe(pe):
            for j in range(KT):
                mm_unit(pe, Step(U_WO + j), m1hi, m1lo,
                        wait_k=(lambda k: pe.wait_ge(S["merged_lo"], k + 1)) if j == 0 else None)

        def add_dve(dve, u, j, ready=None):
            dve.wait_ge(S["unit_done"], u.times(1, 1))
            dve.tensor_tensor(acc[:, j, :], PS[u.par][:, :], acc[:, j, :], ALU.add)\
               .then_inc(S["unit_out"][u.par], 1)

        def wo_dve(dve):
            for j in range(KT):
                if j % 4 == 0:
                    dve.wait_ge(S["x_back"][j // 4], 16)
                add_dve(dve, Step(U_WO + j), j)

        def after_unit(u0):
            def ready(eng, k):
                u = Step(u0 + k)
                eng.wait_ge(S["unit_out"][u.par], u.nth())
            return ready

        def f1_count(g):
            return g.times(G)

        def f1_sp(sp):
            def do(e, kind, g, u, size):
                for t in range(size if kind == "in" else 0):
                    c0 = g.times(G * P, t * P)
                    load_unit(e, u + 2 * t, w_f1[:, :, bass.ds(c0, P)])
                    c1 = g.times(G * P, D_FF + t * P)
                    load_unit(e, u + (2 * t + 1), w_f1[:, :, bass.ds(c1, P)])
                for j in range(KT if kind == "out" else 0):
                    load_unit(e, u + j, w_f1o[:, bass.ds(g.times(G), size), j * P:(j + 1) * P], size)
            run_ffn(sp, SEG1, G1, 2, do)

        def f1_pool(pool):
            def do(e, kind, g, u, size):
                for t in range(2 * size if kind == "in" else KT):
                    split_unit(e, u + t, KT if kind == "in" else size)
            run_ffn(pool, SEG1, G1, 2, do)

        def f1_pe(pe):
            first = [True]

            def do(e, kind, g, u, size):
                if kind == "in":
                    for t in range(2 * size):
                        mm_unit(e, u + t, m2hi, m2lo, wait_k=lo_wait(e, "ffn") if first[0] else None)
                        if first[0]:
                            norm_sum(e, "ffn", KT)
                        first[0] = False
                else:
                    e.wait_ge(S["act_lo"], g.times(G, size))
                    s0 = G * g.par
                    for j in range(KT):
                        mm_unit(e, u + j, m1hi[:, s0:s0 + size, :], m1lo[:, s0:s0 + size, :], size)
            run_ffn(pe, SEG1, G1, 2, do)

        def f1_act(act):
            def do(e, kind, g, u, size):
                for t in range(size if kind == "in" else 0):
                    ug = u + 2 * t
                    e.wait_ge(S["unit_out"][ug.par], ug.nth())
                    e.activation(stage[:, 0, :], stage[:, 0, :], ACT.Silu).then_inc(S["gate_silu"], 1)
                    e.wait_ge(S["act_full"], g.times(G, t + 1))
                    e.activation(m1hi[:, G * g.par + t, :], ssq[:, :], ACT.Copy).then_inc(S["act_hi"], 1)
            run_ffn(act, SEG1, G1, 2, do)

        def f1_dve(dve):
            def do(e, kind, g, u, size):
                if kind == "out":
                    for j in range(KT):
                        add_dve(e, u + j, j)
                    return
                for t in range(size):
                    n = g.times(G, t + 1)
                    ug, uu = u + 2 * t, u + (2 * t + 1)
                    e.wait_ge(S["unit_done"], ug.times(1, 1))
                    e.tensor_tensor(stage[:, 0, :], PS[ug.par][:, :], rstd[:, :], ALU.mult)\
                     .then_inc(S["unit_out"][ug.par], 1)
                    e.wait_ge(S["unit_out"][ug.par], ug.nth())
                    e.wait_ge(S["unit_done"], uu.times(1, 1))
                    e.tensor_tensor(stage[:, 1, :], PS[uu.par][:, :], rstd[:, :], ALU.mult)\
                     .then_inc(S["unit_out"][uu.par], 1)
                    e.wait_ge(S["unit_out"][uu.par], uu.nth())
                    e.wait_ge(S["gate_silu"], n)
                    e.tensor_tensor(ssq[:, :], stage[:, 0, :], stage[:, 1, :], ALU.mult)\
                     .then_inc(S["act_full"], 1)
                    e.wait_ge(S["act_hi"], n)
                    e.wait_ge(S["act_full"], n)
                    e.tensor_tensor(m1lo[:, G * g.par + t, :], ssq[:, :],
                                    m1hi[:, G * g.par + t, :].bitcast(F32), ALU.subtract)\
                     .then_inc(S["act_lo"], 1)
            dve.wait_ge(S["rstd_ready"], NORM_AT["ffn"] + 1)
            run_ffn(dve, SEG1, G1, 2, do)

        def fin_dve(dve):
            dve.wait_ge(S["rstd_ready"], NORM_AT["final"] + 1)
            for k in range(KT):
                dve.scalar_tensor_tensor(out=acc[:, k, :], in0=acc[:, k, :], scalar=col("norm_final", k),
                                         in1=rstd[:, :], op0=ALU.mult, op1=ALU.mult)\
                   .then_inc(S["fin_done"], 1)

        def spill2_act(act):
            act.wait_ge(S["fin_done"], KT)
            act.dma_start(tile_of(x2_d, 0, KT), acc[:, :, :]).then_inc(S["x_spilled"], 16)

        KR0 = 1928
        IN2_COLS = [j * P for j in range(12)] + [1536, 1544, 1672, 1800]
        IN2_ORDER = [12, 13, 14, 15, 16] + list(range(12))

        def in2_sp(sp):
            for j, t in enumerate(IN2_ORDER):
                if t < 16:
                    load_unit(sp, Step(U_IN2 + j), w_in2[:, :, IN2_COLS[t]:IN2_COLS[t] + P])
                else:
                    load_unit(sp, Step(U_IN2 + j), None, parts=[
                        (0, 96, w_in2[:, :, KR0 - 64:KR0 + 32]), (96, 112, w_in2[:, :, KR0 + 16:KR0 + 32]),
                        (112, 128, w_in2[:, :, KR0:KR0 + 16])])
                if j == 4:
                    gates_sp(sp)
                if j == 8:
                    for i in range(3, 5):
                        sp.wait_ge(S["stored"][(U_IN2 + i) % 2], STORED2(i))
                    sp.dma_start(lat[:, :, :], tile_of(proj2, 13, 3)).then_inc(S["lat_loaded"], 16)
                    sp.dma_start(KR, proj2[16 * P + 64:17 * P, :]).then_inc(S["lat_loaded"], 16)
                if j == 12:
                    for i in range(7, 9):
                        sp.wait_ge(S["stored"][(U_IN2 + i) % 2], STORED2(i))
                    sp.dma_start(cb[:, :, 3:3 + T], tile_of(proj2, 0, 4)).then_inc(S["conv_loaded"], 16)
                if 8 <= j < 12:
                    rows_sp(sp, 2 * (j - 8))
                if j == 12:
                    sp.wait_ge(S["em_row"], 1)
                    sp.dma_start(r_d[C * 4:C * 4 + 4, :], emrow).then_inc(S["em_stored"], 16)

        def mq_sp(sp):
            sp.wait_ge(S["conv_silu"], 4)
            sp.dma_start(tile_of(mq_d, 0, 4), cq).then_inc(S["mq_stored"], 16)

        def STORED2(j):
            return ALL_IN[(U_IN2 + j) % 2] + 16 * (j // 2 + 1)

        def in2_pool(pool):
            for j in range(N_IN2):
                split_unit(pool, Step(U_IN2 + j))
                if j == 0:
                    pool.wait_ge(S["unit_done"], U_IN2)
                    pool.memset(cb[:, :, 0:3], 0.0).then_inc(S["ml_consts"], 1)

        def in2_pe(pe):
            for j in range(N_IN2):
                mm_unit(pe, Step(U_IN2 + j), g1hi, g1lo, wait_k=lo_wait(pe, "mix2") if j == 0 else None)
                if j == 0:
                    norm_sum(pe, "mix2", KT)
                if j == 9:
                    pe.wait_ge(S["rstd_ready"], NORM_AT["mix2"] + 1)
                    for k, (pair, first, last) in enumerate(((3, 1, 0), (3, 0, 1), (2, 1, 1))):
                        pe.wait_ge(S["lat_sq"], k + 1)
                        for b in range(2):
                            mm = pe.matmul(PS[pair][:, b * HALF:(b + 1) * HALF], ones[:, :],
                                           lat_s[:, k, b * HALF:(b + 1) * HALF], start=bool(first),
                                           stop=bool(last))
                        if last:
                            mm.then_inc(S["lat_sum"], 1)
                if j == 12:
                    pe.wait_ge(S["lat_mean"], 3)
                    pe.wait_ge(S["g_step"], 3 * C - 1)
                    pe.wait_ge(S["rstd_ready"], NORM_AT["mix2"] + 1)
                    for i in range(C):
                        tr = pe.transpose(PS[2][:, 4 * i:4 * i + 4], arow[:, i * P:(i + 1) * P],
                                          ident[0:4, 0:4])
                    tr.then_inc(S["am_t"], 1)

        def in2_act(act):
            for j in range(N_IN2):
                t = IN2_ORDER[j]
                store_act(act, Step(U_IN2 + j), proj2[t * P:(t + 1) * P, :])
                if j == 2:
                    gates_act(act)
                if j == 4:
                    act.wait_ge(S["m_step"], 5)
                    act.activation(emrow, mrow, ACT.Exp, scale=-1.0).then_inc(S["em_row"], 1)
                if j == 8:
                    act.wait_ge(S["lat_loaded"], 32)
                    for k in range(3):
                        act.activation(lat_s[:, k, :], lat[:, k, :], ACT.Square).then_inc(S["lat_sq"], 1)
                if j == 9:
                    act.wait_ge(S["ang_step"], 10)
                    act.activation(CS, CSQ, ACT.Sin).then_inc(S["rope_sin"], 1)
                if j == 10:
                    for i in range(2):
                        act.wait_ge(S["lat_mean"], 2 * i + 2)
                        act.activation(lat_r[:, i, :], lat_r[:, i, :], ACT.Sqrt).then_inc(S["lat_rstd"], 1)
                if j == 11:
                    for k in range(3):
                        act.wait_ge(S["lat_normed"], k + 1)
                        gain = col("q_norm_2", k) if k < 2 else col("kv_norm_2", 0)
                        act.activation(m2hi[:, k, :], lat[:, k, :], ACT.Copy, scale=gain)\
                           .then_inc(S["latent_hi"], 1)
                if 13 <= j < 17:
                    t = j - 13
                    act.wait_ge(S["conv_step"], 4 * t + 4)
                    act.activation(cq[:, t, :], cq[:, t, :], ACT.Silu).then_inc(S["conv_silu"], 1)
                if j == 14:
                    act.wait_ge(S["am_t"], 1)
                    act.activation(acol, PS[2][:, 0:32], ACT.Copy)

        def in2_dve(dve):
            dve.wait_ge(S["rstd_ready"], NORM_AT["mix2"] + 1)
            for j in range(N_IN2):
                store_dve(dve, Step(U_IN2 + j), U_IN2, B2)
                if j == 3:
                    gates_dve(dve)
                if 4 <= j < 8:
                    rows_dve(dve, 2 * (j - 4))
                    rows_dve(dve, 2 * (j - 4) + 1)
                if j == 8:
                    angles(dve, 0)
                if j == 9:
                    angles(dve, 1)
                if j == 10:
                    lat_means(dve)
                    rope_key(dve)
                if j == 11:
                    for k in range(3):
                        dve.wait_ge(S["lat_rstd"], k // 2 + 1)
                        dve.tensor_tensor(lat[:, k, :], lat[:, k, :], lat_r[:, k // 2, :], ALU.mult)\
                           .then_inc(S["lat_normed"], 1)
                if j == 12:
                    for k in range(3):
                        gain = col("q_norm_2", k) if k < 2 else col("kv_norm_2", 0)
                        dve.wait_ge(S["latent_hi"], k + 1)
                        dve.scalar_tensor_tensor(out=m2lo[:, k, :], in0=lat[:, k, :], scalar=gain,
                                                 in1=m2hi[:, k, :].bitcast(F32), op0=ALU.mult,
                                                 op1=ALU.subtract).then_inc(S["latent_lo"], 1)
                if 12 <= j < 16:
                    conv_dve(dve, j - 12)

        ig, lf, fz, mrow = acc[0:4, 0, :], acc[0:4, 1, :], acc[0:4, 2, :], acc[0:4, 3, :]
        grow, arow, emrow, on4 = acc[0:4, 4, :], acc[0:4, 7, :], acc[32:36, 7, :], ssq[0:4, :]
        rrow = [acc[0:4, 5, :], acc[0:4, 6, :]]
        acol = small[:, 0:32]
        cq = acc[:, 3:7, :]
        RP = slice(64, 128)
        NOPE, RO, SW = slice(0, 64), slice(64, 96), slice(96, 128)
        CS, CSQ, KR, KROPE = acc[RP, 0, :], acc[RP, 1, :], acc[RP, 2, :], acc[RO, 7, :]
        ptab = small[:, 36:39]
        MAGIC = 12582912.0
        PI = 3.1415925
        TWO_PI = (6.28125, 0.0019350051879882812, 3.019915981956753e-07)

        def angles(dve, part):
            if part == 0:
                dve.wait_ge(S["mla_loaded"], 32)
                dve.tensor_copy(CS, CSQ.bitcast(I32)).then_inc(S["ang_step"], 1)
                dve.wait_ge(S["ang_step"], 1)
                dve.tensor_scalar(CS, CS, ptab[RP, 0:1], None, ALU.mult).then_inc(S["ang_step"], 1)
                dve.wait_ge(S["ang_step"], 2)
                dve.tensor_scalar(CSQ, CS, ptab[RP, 1:2], 0.15915494309189535, ALU.add, ALU.mult)\
                   .then_inc(S["ang_step"], 1)
                dve.wait_ge(S["ang_step"], 3)
                dve.tensor_scalar(CSQ, CSQ, MAGIC, None, ALU.add).then_inc(S["ang_step"], 1)
                dve.wait_ge(S["ang_step"], 4)
                dve.tensor_scalar(CSQ, CSQ, MAGIC, None, ALU.subtract).then_inc(S["ang_step"], 1)
                return
            for i, part in enumerate(TWO_PI):
                dve.wait_ge(S["ang_step"], 3 + i + 2)
                dve.scalar_tensor_tensor(out=CS, in0=CSQ, scalar=-part, in1=CS,
                                         op0=ALU.mult, op1=ALU.add).then_inc(S["ang_step"], 1)
            dve.wait_ge(S["ang_step"], 8)
            dve.tensor_scalar(CSQ, CS, ptab[RP, 1:2], PI, ALU.add, ALU.min).then_inc(S["ang_step"], 1)
            dve.wait_ge(S["ang_step"], 9)
            dve.tensor_scalar(CSQ, CSQ, -PI, None, ALU.max).then_inc(S["ang_step"], 1)

        def lat_means(dve):
            for i, n in enumerate((2, 1)):
                dve.wait_ge(S["lat_sum"], i + 1)
                dve.tensor_scalar(lat_r[:, i, :], PS[3 - i][:, :], 1.0 / (n * P), EPS, ALU.mult, ALU.add)\
                   .then_inc(S["lat_mean"], 1)
                dve.wait_ge(S["lat_mean"], 2 * i + 1)
                dve.reciprocal(lat_r[:, i, :], lat_r[:, i, :]).then_inc(S["lat_mean"], 1)

        def rope_key(dve):
            dve.wait_ge(S["rope_sin"], 1)
            dve.tensor_scalar(CS, CS, ptab[RP, 2:3], None, ALU.mult).then_inc(S["ang_step"], 1)
            dve.wait_ge(S["ang_step"], 11)
            dve.wait_ge(S["lat_loaded"], 32)
            dve.tensor_tensor(KROPE, acc[RO, 2, :], acc[RO, 0, :], ALU.mult).then_inc(S["ang_step"], 1)
            dve.tensor_tensor(acc[RO, 1, :], acc[SW, 2, :], acc[SW, 0, :], ALU.mult).then_inc(S["ang_step"], 1)
            dve.wait_ge(S["ang_step"], 13)
            dve.tensor_tensor(KROPE, KROPE, acc[RO, 1, :], ALU.add).then_inc(S["ang_step"], 1)

        def gates_sp(sp):
            sp.wait_ge(S["x_spilled"], 32)
            sp.wait_ge(S["stored"][U_IN2 % 2], STORED2(0))
            sp.dma_start(CSQ.bitcast(I32), A["positions_2"].to_broadcast([64, T])).then_inc(S["mla_loaded"], 16)
            sp.dma_start(ptab, A["rope_table"]).then_inc(S["mla_loaded"], 16)
            sp.dma_start(ig, proj2[12 * P:12 * P + 4, :]).then_inc(S["gates_loaded"], 16)
            sp.dma_start(fz, proj2[12 * P + 4:12 * P + 8, :]).then_inc(S["gates_loaded"], 16)
            sp.dma_start(small[0:4, 60:61], A["b_gates_2"][:, 0:4].rearrange("a h -> h a"))\
              .then_inc(S["gates_loaded"], 16)
            sp.dma_start(small[0:4, 61:62], A["b_gates_2"][:, 4:8].rearrange("a h -> h a"))\
              .then_inc(S["gates_loaded"], 16)

        def rows_sp(sp, first):
            for J in (first, first + 1):
                sp.wait_ge(S["g_step"], 3 * J + 3)
                sp.dma_start(r_d[J * 4:J * 4 + 4, J * P:T], rrow[J % 2][:, J * P:T])\
                  .then_inc(S["r_stored"][J % 2], 16)

        def gates_act(act):
            act.wait_ge(S["gates_loaded"], 64)
            bf = small[0:4, 61:62]
            act.activation(lf, fz, ACT.Abs, bias=bf).then_inc(S["f_log"], 1)
            act.wait_ge(S["f_log"], 1)
            act.activation(lf, lf, ACT.Exp, scale=-1.0).then_inc(S["f_log"], 1)
            act.wait_ge(S["f_log"], 2)
            act.activation(lf, lf, ACT.Ln, bias=1.0).then_inc(S["f_log"], 1)

        def gates_dve(dve):
            dve.wait_ge(S["gates_loaded"], 64)
            bi, bf = small[0:4, 60:61], small[0:4, 61:62]
            dve.memset(on4, 1.0).then_inc(S["m_step"], 1)
            dve.tensor_scalar(ig, ig, bi, None, ALU.add).then_inc(S["m_step"], 1)
            dve.wait_ge(S["f_log"], 1)
            dve.tensor_scalar(fz, fz, bf, 0.0, ALU.add, ALU.min).then_inc(S["m_step"], 1)
            dve.wait_ge(S["f_log"], 3)
            dve.wait_ge(S["m_step"], 3)
            dve.tensor_tensor(lf, fz, lf, ALU.subtract).then_inc(S["m_step"], 1)
            dve.wait_ge(S["m_step"], 4)
            dve.wait_ge(S["m_step"], 2)
            dve.tensor_tensor_scan(mrow, lf, ig, 0.0, ALU.add, ALU.max).then_inc(S["m_step"], 1)

        def rows_dve(dve, J):
            dve.wait_ge(S["m_step"], 5)
            s = slice(J * P, T)
            b = slice(J * P, (J + 1) * P)
            if J:
                dve.wait_ge(S["g_step"], 3 * J)
            dve.tensor_tensor_scan(grow[:, s], on4[:, s], lf[:, s], 0.0, ALU.mult, ALU.add)\
               .then_inc(S["g_step"], 1)
            dve.wait_ge(S["g_step"], 3 * J + 1)
            dve.tensor_tensor(arow[:, b], ig[:, b], grow[:, b], ALU.subtract).then_inc(S["g_step"], 1)
            if J >= 2:
                dve.wait_ge(S["r_stored"][J % 2], 16 * (J // 2))
            dve.tensor_tensor(rrow[J % 2][:, s], grow[:, s], mrow[:, s], ALU.subtract)\
               .then_inc(S["g_step"], 1)

        def conv_dve(dve, t):
            dve.wait_ge(S["ml_consts"], 1)
            dve.wait_ge(S["conv_loaded"], 16)
            dve.wait_ge(S["em_stored"], 16)
            for i in range(2):
                dve.wait_ge(S["r_stored"][i], 16 * C // 2)
            dve.tensor_scalar(cq[:, t, :], cb[:, t, 3:3 + T], col("conv_w_2", 12 + t), col("conv_b_2", t),
                              ALU.mult, ALU.add).then_inc(S["conv_step"], 1)
            for k in range(3):
                dve.wait_ge(S["conv_step"], 4 * t + k + 1)
                dve.scalar_tensor_tensor(out=cq[:, t, :], in0=cb[:, t, k:k + T],
                                         scalar=col("conv_w_2", 4 * k + t), in1=cq[:, t, :],
                                         op0=ALU.mult, op1=ALU.add).then_inc(S["conv_step"], 1)

        ROT, VTH = x4[:, 0, :], x4[:, 3, :]
        QK_SCALE = 96.0 ** -0.5
        qT = acc
        NQ = [(h, i) for h in range(8) for i in range(C)]

        def mla_sp(sp):
            for h in range(8):
                q0 = h * 96
                load_unit(sp, Step(U_QKV + 2 * h), None, 2, parts=[
                    (0, 96, w_uq[:, :, q0:q0 + 96]), (96, 112, w_uq[:, :, q0 + 80:q0 + 96]),
                    (112, 128, w_uq[:, :, q0 + 64:q0 + 80])])
                load_unit(sp, Step(U_QKV + 2 * h + 1), w_ukv[:, :, h * P:(h + 1) * P], 1)
                if h == 0:
                    mq_sp(sp)

        def mla_pool(pool):
            for h in range(8):
                split_unit(pool, Step(U_QKV + 2 * h), 2)
                split_unit(pool, Step(U_QKV + 2 * h + 1), 1)

        def vt_act(act, h):
            act.wait_ge(S["vh_t"], h + 1)
            act.activation(Vt[:, :, h, :], PS[3][:, 0:HALF].rearrange("p (c e) -> p c e", c=C), ACT.Copy)\
               .then_inc(S["vh_tok"], 1)

        def mla_act(act):
            act.wait_ge(S["unit_done"], U_QKV)
            act.wait_ge(S["ang_step"], 14)
            act.wait_ge(S["cs_moved"], 1)
            for h in range(8):
                uq, uk = Step(U_QKV + 2 * h), Step(U_QKV + 2 * h + 1)
                if h == 3:
                    act.wait_ge(S["mq_stored"], 16)
                act.wait_ge(S["unit_done"], uq.times(1, 1))
                act.activation(qT[NOPE, h, :], PS[uq.par][NOPE, :], ACT.Copy).then_inc(S["q_copied"], 1)
                act.wait_ge(S["unit_done"], uk.times(1, 1))
                act.activation(kT[NOPE, h, :], PS[uk.par][NOPE, :], ACT.Copy)
                if h:
                    act.wait_ge(S["vh_t"], h)
                act.activation(VTH[RP, :], PS[uk.par][RP, :], ACT.Copy).then_inc(S["unit_out"][uk.par], 1)
                act.activation(kT[RO, h, :], KROPE, ACT.Copy).then_inc(S["kr_copied"], 1)
                if h:
                    vt_act(act, h - 1)
            vt_act(act, 7)
            for n, (h, i) in enumerate(NQ):
                N = (i + 1) * P
                act.wait_ge(S["s_stat"], 2 * n + 2)
                if n >= 2:
                    act.wait_ge(S["pt_ready"], n - 1)
                act.activation(x4[:, n % 2, 0:N], PS[n % 2][:, 0:N], ACT.Exp, bias=sm(n, 1), scale=QK_SCALE,
                               accum_out=sm(n, 2)).then_inc(S["p_ready"], 1)
                if n:
                    pt_copy(act, n - 1)
                if n and (n - 1) % 16 == 15:
                    mixa(act, (n - 1) // 16)
            pt_copy(act, 63)
            mixa(act, 3)

        def sm(n, what):
            c = 40 + 5 * (n % 2) + what
            return small[:, c:c + 1]

        def pt_copy(act, n):
            N = (n % C + 1) * P
            act.wait_ge(S["pt_ready"], n + 1)
            if n:
                act.wait_ge(S["pv_ready"], n)
            act.activation(x4[:, 2, 0:N], PS[2][:, 0:N], ACT.Copy).then_inc(S["pt_out"], 1)

        def mixa(act, pair):
            act.wait_ge(S["pv_ready"], 16 * (pair + 1))
            act.activation(m2hi[:, 4 + pair, :], PS[3][:, :], ACT.Copy).then_inc(S["mixa_hi"], 1)

        def mla_dve(dve):
            dve.wait_ge(S["unit_done"], U_QKV)
            dve.wait_ge(S["ang_step"], 11)
            dve.tensor_copy(ROT[RP, :], CS).then_inc(S["cs_moved"], 1)
            dve.wait_ge(S["cs_moved"], 1)
            for h in range(8):
                uq = Step(U_QKV + 2 * h)
                q = PS[uq.par]
                dve.wait_ge(S["q_copied"], h + 1)
                if h:
                    dve.wait_ge(S["q_rope"], h)
                if h == 7:
                    dve.wait_ge(S["kr_copied"], 8)
                dve.tensor_tensor(qT[RO, h, :], q[RO, :], ROT[RO, :], ALU.mult).then_inc(S["q_a"], 1)
                dve.tensor_tensor(x4[RO, 1, :], q[SW, :], ROT[SW, :], ALU.mult).then_inc(S["unit_out"][uq.par], 1)
                dve.wait_ge(S["unit_out"][uq.par], uq.nth())
                dve.wait_ge(S["q_a"], h + 1)
                dve.tensor_tensor(qT[RO, h, :], qT[RO, h, :], x4[RO, 1, :], ALU.add).then_inc(S["q_rope"], 1)

            def normalise(n):
                N = (n % C + 1) * P
                dve.wait_ge(S["p_ready"], n + 1)
                dve.reciprocal(sm(n, 3), sm(n, 2)).then_inc(S["rs_inv"], 1)
                dve.wait_ge(S["rs_inv"], n + 1)
                dve.tensor_scalar(x4[:, n % 2, 0:N], x4[:, n % 2, 0:N], sm(n, 3), None, ALU.mult)\
                   .then_inc(S["p_norm"], 1)

            def mixa_low(pair):
                dve.wait_ge(S["mixa_hi"], pair + 1)
                dve.tensor_tensor(m2lo[:, 4 + pair, :], PS[3][:, :], m2hi[:, 4 + pair, :].bitcast(F32),
                                  ALU.subtract).then_inc(S["mixa_lo"], 1)

            for n, (h, i) in enumerate(NQ):
                N = (i + 1) * P
                dve.wait_ge(S["s_ready"], n + 1)
                dve.tensor_reduce(sm(n, 0), PS[n % 2][:, 0:N], AX.X, ALU.max).then_inc(S["s_stat"], 1)
                dve.wait_ge(S["s_stat"], 2 * n + 1)
                dve.tensor_scalar(sm(n, 1), sm(n, 0), -QK_SCALE, None, ALU.mult).then_inc(S["s_stat"], 1)
                normalise(n)
                if n and (n - 1) % 16 == 15:
                    mixa_low((n - 1) // 16)
            mixa_low(3)

        def mla_pe(pe):
            def turn_values(h):
                uk = Step(U_QKV + 2 * h + 1)
                pe.wait_ge(S["unit_out"][uk.par], uk.nth())
                if h:
                    pe.wait_ge(S["vh_tok"], h)
                else:
                    pe.wait_ge(S["lat_mean"], 1)
                for c in range(C):
                    tr = pe.transpose(PS[3][:, c * 64:(c + 1) * 64], VTH[RP, c * P:(c + 1) * P],
                                      ident[RP, RP])
                tr.then_inc(S["vh_t"], 1)

            pe.wait_ge(S["latent_lo"], 3)
            for h in range(8):
                mm_unit(pe, Step(U_QKV + 2 * h), m2hi, m2lo, 2)
                if h:
                    turn_values(h - 1)
                mm_unit(pe, Step(U_QKV + 2 * h + 1), m2hi[:, 2:3, :], m2lo[:, 2:3, :], 1)
            turn_values(7)
            pe.wait_ge(S["q_rope"], 8)
            pe.wait_ge(S["kr_copied"], 8)
            pe.wait_ge(S["vh_tok"], 8)

            def scores(n):
                h, i = NQ[n]
                N = (i + 1) * P
                if n >= 2:
                    pe.wait_ge(S["p_ready"], n - 1)
                for b in range(0, N, HALF):
                    w = min(HALF, N - b)
                    last = b + w == N
                    mm = pe.matmul(PS[n % 2][:, b:b + w], qT[0:96, h, i * P:(i + 1) * P],
                                   kT[0:96, h, b:b + w], start=True, stop=True)
                mm = pe.matmul(PS[n % 2][:, N - P:N], ident16[:, :], negm16[:, :], start=False, stop=True,
                               skip_group_check=True)
                mm.then_inc(S["s_ready"], 1)

            def turn(n):
                pe.wait_ge(S["p_norm"], n + 1)
                if n:
                    pe.wait_ge(S["pt_out"], n)
                for j in range(n % C + 1):
                    tr = pe.transpose(PS[2][:, j * P:(j + 1) * P], x4[:, n % 2, j * P:(j + 1) * P], ident[:, :])
                tr.then_inc(S["pt_ready"], 1)

            def values(n):
                h, i = NQ[n]
                if n % 16 == 0 and n:
                    pe.wait_ge(S["mixa_lo"], n // 16)
                pe.wait_ge(S["pt_out"], n + 1)
                o = PS[3][h % 2 * 64:h % 2 * 64 + 64, i * P:(i + 1) * P]
                for j in range(i + 1):
                    mm = pe.matmul(o, Vt[:, j, h, :], x4[:, 2, j * P:(j + 1) * P], start=(j == 0), stop=(j == i))
                mm.then_inc(S["pv_ready"], 1)

            scores(0)
            scores(1)
            for n in range(64):
                turn(n)
                if n + 2 < 64:
                    scores(n + 2)
                values(n)

        NS = 4 * C
        hn, t1, sqb, vTm = acc[:, 0, :], acc[:, 1, :], acc[:, 2, :], acc[:, 3, :]
        omT, emT = [acc[:, 4, :], acc[:, 5, :]], [acc[:, 6, :], acc[:, 7, :]]
        HS = 8

        def em_om_sp(sp, h):
            if h >= 2:
                sp.wait_ge(S["h_step"], HS * (h - 1))
            sp.dma_start(emT[h % 2], r_d[4 * C + h:4 * C + h + 1, :].to_broadcast([P, T]))\
              .then_inc(S["em_loaded"], 16)
            sp.dma_start(omT[h % 2], proj2[(8 + h) * P:(9 + h) * P, :]).then_inc(S["om_loaded"], 16)

        def mlstm_sp(sp):
            sp.wait_ge(S["mixa_lo"], 4)
            sp.dma_start(qk[:, :, :], tile_of(mq_d, 0, 4)).then_inc(S["qk_back"], 16)
            sp.dma_start(vTm, proj2[4 * P:5 * P, :]).then_inc(S["mv_loaded"], 16)
            for n in range(NS):
                h, J = n // C, n % C
                if n >= 4:
                    sp.wait_ge(S["st_w"], n - 3)
                sp.dma_start(ering[:, n % 4, J * P:T],
                             r_d[J * 4 + h:J * 4 + h + 1, J * P:T].to_broadcast([P, T - J * P]))\
                  .then_inc(S["r_bc_loaded"][n % 4], 16)
                if J == 2 and h < 3:
                    sp.wait_ge(S["mv_t"], h + 1)
                    sp.dma_start(vTm, proj2[(5 + h) * P:(6 + h) * P, :]).then_inc(S["mv_loaded"], 16)
                if n == 2:
                    em_om_sp(sp, 0)
                if J == 7 and h < 3:
                    em_om_sp(sp, h + 1)

        def vtok_act(act, h):
            act.wait_ge(S["mv_t"], h + 1)
            if h >= 2:
                act.wait_ge(S["ho_ready"], C * (h - 1))
            act.activation(vtok2[:, h % 2, :, :], PS[3][:, :].rearrange("p (c e) -> p c e", c=C), ACT.Copy)\
               .then_inc(S["mv_tok"], 1)

        def gate_act(act, h):
            act.wait_ge(S["om_loaded"], 16 * (h + 1))
            act.activation(omT[h % 2], omT[h % 2], ACT.Sigmoid).then_inc(S["om_sig"], 1)

        def num_act(act, h):
            act.wait_ge(S["ho_ready"], C * (h + 1))
            act.activation(hn, PS[2][:, :], ACT.Copy).then_inc(S["num_copied"], 1)

        def square_act(act, h):
            act.wait_ge(S["h_step"], HS * h + 4)
            act.activation(sqb, hn, ACT.Square).then_inc(S["h_sq"], 1)

        def root_act(act, h):
            act.wait_ge(S["h_step"], HS * h + 6)
            act.activation(t1, t1, ACT.Sqrt).then_inc(S["h_rstd"], 1)

        def high_act(act, h):
            act.wait_ge(S["h_step"], HS * h + 8)
            act.activation(m2hi[:, h, :], hn, ACT.Copy).then_inc(S["mixm_hi"], 1)

        def mlstm_act(act):
            vtok_act(act, 0)
            for n in range(NS):
                h, J = n // C, n % C
                act.wait_ge(S["r_bc_loaded"][n % 4], 16 * (n // 4 + 1))
                act.activation(ering[:, n % 4, J * P:T], ering[:, n % 4, J * P:T], ACT.Exp,
                               bias=acol[:, 4 * J + h:4 * J + h + 1]).then_inc(S["st_exp"], 1)
                if h and J == 0:
                    num_act(act, h - 1)
                if J == 2:
                    gate_act(act, h)
                if h and J == 3:
                    square_act(act, h - 1)
                if h and J == 5:
                    root_act(act, h - 1)
                if J == 6 and h < 3:
                    vtok_act(act, h + 1)
                if h and J == 6:
                    high_act(act, h - 1)
            for part in (num_act, square_act, root_act, high_act):
                part(act, 3)

        def mlstm_pool(pool):
            for n in range(NS):
                h, J = n // C, n % C
                pool.wait_ge(S["st_w"], n + 1)
                blk = Wt[:, n % 3, J * P:(J + 1) * P]
                pool.affine_select(out=blk, in_=blk, compare_op=ALU.is_ge, fill=0.0, base=0,
                                   pattern=[[1, P]], channel_multiplier=-1).then_inc(S["w_ready"], 1)
                pool.wait_ge(S["w_ready"], n + 1)
                if J == 0:
                    if h:
                        pool.wait_ge(S["den_ready"], h)
                    pool.tensor_tensor(wsum[:, :], Wt[:, n % 3, :], ones[:, 0:1].to_broadcast([P, T]), ALU.mult)\
                        .then_inc(S["w_summed"], 1)
                else:
                    pool.wait_ge(S["w_summed"], n)
                    pool.tensor_tensor(wsum[:, J * P:T], wsum[:, J * P:T], Wt[:, n % 3, J * P:T], ALU.add)\
                        .then_inc(S["w_summed"], 1)

        def outputs(dve, h, first, last):
            for step in range(first, last + 1):
                if step > 1:
                    dve.wait_ge(S["h_step"], HS * h + step - 1)
                if step == 1:
                    dve.wait_ge(S["den_ready"], h + 1)
                    dve.wait_ge(S["em_loaded"], 16 * (h + 1))
                    ins = dve.scalar_tensor_tensor(out=t1, in0=PS[3][:, :], scalar=-1.0, in1=emT[h % 2],
                                                   op0=ALU.mult, op1=ALU.max)
                if step == 2:
                    ins = dve.tensor_tensor(t1, PS[3][:, :], t1, ALU.max)
                if step == 3 or step == 6:
                    ins = dve.reciprocal(t1, t1)
                if step == 4:
                    dve.wait_ge(S["num_copied"], h + 1)
                    ins = dve.tensor_tensor(hn, hn, t1, ALU.mult)
                if step == 5:
                    dve.wait_ge(S["hsq_sum"], h + 1)
                    ins = dve.tensor_scalar(t1, PS[3][:, :], 1.0 / P, EPS, ALU.mult, ALU.add)
                if step == 7:
                    dve.wait_ge(S["h_rstd"], h + 1)
                    ins = dve.tensor_tensor(hn, hn, t1, ALU.mult)
                if step == 8:
                    dve.wait_ge(S["om_sig"], h + 1)
                    ins = dve.scalar_tensor_tensor(out=hn, in0=hn, scalar=col("ml_head_norm_2", h),
                                                   in1=omT[h % 2], op0=ALU.mult, op1=ALU.mult)
                ins.then_inc(S["h_step"], 1)

        def low_dve(dve, h):
            dve.wait_ge(S["mixm_hi"], h + 1)
            dve.tensor_tensor(m2lo[:, h, :], hn, m2hi[:, h, :].bitcast(F32), ALU.subtract)\
               .then_inc(S["mixm_lo"], 1)

        def mlstm_dve(dve):
            for n in range(NS):
                h, J = n // C, n % C
                s = slice(J * P, T)
                dve.wait_ge(S["st_exp"], n + 1)
                dve.wait_ge(S["st_ready"], n + 1)
                if n >= 3:
                    dve.wait_ge(S["ho_ready"], n - 2)
                    dve.wait_ge(S["w_summed"], n - 2)
                dve.scalar_tensor_tensor(out=Wt[:, n % 3, s], in0=PS[n % 2][:, s], scalar=0.125,
                                         in1=ering[:, n % 4, s], op0=ALU.mult, op1=ALU.mult)\
                   .then_inc(S["st_w"], 1)
                if h and J == 0:
                    outputs(dve, h - 1, 1, 2)
                if h and J == 1:
                    outputs(dve, h - 1, 3, 4)
                if h and J == 4:
                    outputs(dve, h - 1, 5, 6)
                if h and J == 5:
                    outputs(dve, h - 1, 7, 8)
                if h and J == 6:
                    low_dve(dve, h - 1)
            outputs(dve, 3, 1, 8)
            low_dve(dve, 3)

        def mlstm_pe(pe):
            def turn_v(h):
                pe.wait_ge(S["mv_loaded"], 16 * (h + 1))
                if h >= 2:
                    pe.wait_ge(S["h_step"], HS * (h - 2) + 5)
                for c in range(C):
                    tr = pe.transpose(PS[3][:, c * P:(c + 1) * P], vTm[:, c * P:(c + 1) * P], ident[:, :])
                tr.then_inc(S["mv_t"], 1)

            def scores(n):
                h, J = n // C, n % C
                hp = slice(h % 2 * 64, h % 2 * 64 + 64)
                if n >= 2:
                    pe.wait_ge(S["st_w"], n - 1)
                for a, b in ((J * P, HALF), (max(J * P, HALF), T)):
                    if a < b:
                        mm = pe.matmul(PS[n % 2][:, a:b], qk[hp, 2 + h // 2, J * P:(J + 1) * P],
                                       qk[hp, h // 2, a:b], start=True, stop=True)
                mm.then_inc(S["st_ready"], 1)

            def numerator(n):
                h, J = n // C, n % C
                pe.wait_ge(S["w_ready"], n + 1)
                if J == 0:
                    pe.wait_ge(S["mv_tok"], h + 1)
                    if h:
                        pe.wait_ge(S["num_copied"], h)
                for a, b in ((J * P, HALF), (max(J * P, HALF), T)):
                    if a < b:
                        mm = pe.matmul(PS[2][:, a:b], vtok2[:, h % 2, J, :], Wt[:, n % 3, a:b],
                                       start=(J == 0), stop=(J == b // P - 1), skip_group_check=True)
                mm.then_inc(S["ho_ready"], 1)

            def denominator(h):
                pe.wait_ge(S["w_summed"], C * (h + 1))
                pe.wait_ge(S["mv_tok"], min(h + 2, 4))
                if h == 3:
                    pe.wait_ge(S["h_step"], HS * 2 + 5)
                for b in range(2):
                    mm = pe.matmul(PS[3][:, b * HALF:(b + 1) * HALF], ones[:, :],
                                   wsum[:, b * HALF:(b + 1) * HALF], start=True, stop=True)
                mm.then_inc(S["den_ready"], 1)

            def square_sum(h):
                pe.wait_ge(S["h_sq"], h + 1)
                for b in range(2):
                    mm = pe.matmul(PS[3][:, b * HALF:(b + 1) * HALF], ones[:, :],
                                   sqb[:, b * HALF:(b + 1) * HALF], start=True, stop=True)
                mm.then_inc(S["hsq_sum"], 1)

            turn_v(0)
            pe.wait_ge(S["qk_back"], 16)
            scores(0)
            scores(1)
            for n in range(NS):
                h, J = n // C, n % C
                if h and J == 3:
                    square_sum(h - 1)
                if J == 5 and h < 3:
                    turn_v(h + 1)
                numerator(n)
                if n + 2 < NS:
                    scores(n + 2)
                if J == C - 1:
                    denominator(h)
            square_sum(3)

        def wo2_sp(sp):
            for j in range(2, KT):
                load_unit(sp, Step(U_WO2 + j), w_out2[:, :, j * P:(j + 1) * P])
            last = Step(U_WO2 + KT - 1)
            sp.wait_ge(S["unit_done"], last.times(1, 1))
            for i in range(2):
                sp.dma_start(xr[:, 4 * i:4 * i + 4, :], tile_of(x2_d, 4 * i, 4)).then_inc(S["x_back"][i], 16)

        def wo2_pe(pe):
            for j in range(KT):
                if j == 0:
                    pe.wait_ge(S["mixm_lo"], 4)
                mm_unit(pe, Step(U_WO2 + j), m2hi, m2lo)
            norm_sum(pe, "post_mix", KT)

        def wo2_dve(dve):
            for j in range(KT):
                u = Step(U_WO2 + j)
                dve.wait_ge(S["unit_done"], u.times(1, 1))
                dve.tensor_copy(acc[:, j, :], PS[u.par][:, :]).then_inc(S["unit_out"][u.par], 1)
            norm_dve(dve, "post_mix", no_wait)
            dve.wait_ge(S["rstd_ready"], NORM_AT["post_mix"] + 1)
            for k in range(KT):
                dve.scalar_tensor_tensor(out=acc[:, k, :], in0=acc[:, k, :], scalar=col("norm_post_mix_2", k),
                                         in1=rstd[:, :], op0=ALU.mult, op1=ALU.mult)\
                   .then_inc(S["y_scaled"], 1)
                dve.wait_ge(S["y_scaled"], k + 1)
                dve.wait_ge(S["x_back"][k // 4], 32)
                dve.tensor_tensor(acc[:, k, :], acc[:, k, :], xr[:, k, :], ALU.add).then_inc(S["x_added"], 1)

        def spill3_act(act):
            act.wait_ge(S["x_added"], KT)
            act.dma_start(tile_of(x3_d, 0, KT), acc[:, :, :]).then_inc(S["x_spilled"], 16)

        def f2_sp(sp):
            def do(e, kind, g, u, size):
                for t in range(size if kind == "in" else 0):
                    if u.s == 0 and g.c == 0 and t < 2:
                        continue
                    load_unit(e, u + t, w_up[:, :, bass.ds(g.times(G * P, t * P), P)])
                for j in range(KT if kind == "out" else 0):
                    load_unit(e, u + j, w_down[:, bass.ds(g.times(G), size), j * P:(j + 1) * P], size)
            run_ffn(sp, SEG2, G2, 1, do)

        def f2_pool(pool):
            def do(e, kind, g, u, size):
                for t in range(size if kind == "in" else KT):
                    split_unit(e, u + t, KT if kind == "in" else size)
            run_ffn(pool, SEG2, G2, 1, do)

        def f2_pe(pe):
            first = [True]

            def do(e, kind, g, u, size):
                if kind == "in":
                    for t in range(size):
                        mm_unit(e, u + t, h3hi, h3lo, wait_k=lo_wait(e, "mlp") if first[0] else None)
                        if first[0]:
                            norm_sum(e, "mlp", KT)
                        first[0] = False
                else:
                    e.wait_ge(S["sq_lo"], g.times(G, size))
                    s0 = G * g.par
                    for j in range(KT):
                        mm_unit(e, u + j, a2hi[:, s0:s0 + size, :], a2lo[:, s0:s0 + size, :], size)
            run_ffn(pe, SEG2, G2, 1, do)

        def f2_act(act):
            def do(e, kind, g, u, size):
                for t in range(size if kind == "in" else 0):
                    n = g.times(G, t + 1)
                    ut = u + t
                    e.wait_ge(S["unit_out"][ut.par], ut.nth())
                    e.activation(stage[:, 1, :], stage[:, 0, :], ACT.Square).then_inc(S["up_sq"], 1)
                    e.wait_ge(S["up_sq"], n)
                    e.activation(a2hi[:, G * g.par + t, :], stage[:, 1, :], ACT.Copy).then_inc(S["sq_hi"], 1)
            run_ffn(act, SEG2, G2, 1, do)

        def f2_dve(dve):
            def do(e, kind, g, u, size):
                if kind == "out":
                    for j in range(KT):
                        if u.s == 0 and g.c == 0:
                            raise ValueError("the first down segment is in the loop")
                        add_dve(e, u + j, j)
                    return
                for t in range(size):
                    n = g.times(G, t + 1)
                    ut = u + t
                    e.wait_ge(S["unit_done"], ut.times(1, 1))
                    e.scalar_tensor_tensor(out=stage[:, 0, :], in0=PS[ut.par][:, :], scalar=0.0,
                                           in1=rstd[:, :], op0=ALU.max, op1=ALU.mult)\
                     .then_inc(S["unit_out"][ut.par], 1)
                    e.wait_ge(S["sq_hi"], n)
                    e.tensor_tensor(a2lo[:, G * g.par + t, :], stage[:, 1, :],
                                    a2hi[:, G * g.par + t, :].bitcast(F32), ALU.subtract)\
                     .then_inc(S["sq_lo"], 1)
            dve.wait_ge(S["rstd_ready"], NORM_AT["mlp"] + 1)
            dve.wait_ge(S["x_spilled"], 48)
            dve.memset(acc[:, :, :], 0.0).then_inc(S["acc_zero"], 1)
            dve.wait_ge(S["acc_zero"], 1)
            run_ffn(dve, SEG2, G2, 1, do)

        def end_sp(sp):
            sp.wait_ge(S["unit_done"], U_END)
            for i in range(2):
                sp.dma_start(xr[:, 4 * i:4 * i + 4, :], tile_of(x3_d, 4 * i, 4)).then_inc(S["x_back"][i], 16)
            for c in range(C):
                sp.wait_ge(S["out_ev"], c + 1)
                sp.dma_start(out[0, c * P:(c + 1) * P, :], orow[:, c % 2, :]).then_inc(S["out_stored"][c % 2], 16)
            for i in range(2):
                sp.wait_ge(S["out_stored"][i], 16 * C // 2)

        def end_dve(dve):
            norm_dve(dve, "post_mlp", no_wait)
            dve.wait_ge(S["rstd_ready"], NORM_AT["post_mlp"] + 1)
            for k in range(KT):
                dve.scalar_tensor_tensor(out=acc[:, k, :], in0=acc[:, k, :], scalar=col("norm_post_mlp_2", k),
                                         in1=rstd[:, :], op0=ALU.mult, op1=ALU.mult)\
                   .then_inc(S["y_scaled"], 1)
                dve.wait_ge(S["y_scaled"], KT + k + 1)
                dve.wait_ge(S["x_back"][k // 4], 48)
                dve.tensor_tensor(acc[:, k, :], acc[:, k, :], xr[:, k, :], ALU.add).then_inc(S["x_added"], 1)

        def end_pe(pe):
            norm_sum(pe, "post_mlp", KT)
            pe.wait_ge(S["x_added"], KT + 8)
            for c in range(C):
                if c >= 2:
                    pe.wait_ge(S["out_ev"], c - 1)
                for k in range(KT):
                    tr = pe.transpose(PS[c % 2][:, k * P:(k + 1) * P], acc[:, k, c * P:(c + 1) * P], ident[:, :])
                tr.then_inc(S["out_t"], 1)

        def end_act(act):
            for c in range(C):
                act.wait_ge(S["out_t"], c + 1)
                if c >= 2:
                    act.wait_ge(S["out_stored"][c % 2], 16 * (c // 2))
                act.activation(orow[:, c % 2, :], PS[c % 2][:, :], ACT.Copy).then_inc(S["out_ev"], 1)

        @block.sync
        def _(sp):
            start_sp(sp)
            wup_sp(sp)
            in_sp(sp)
            gla_sp(sp)
            merge_sp(sp)
            wo_sp(sp)
            f1_sp(sp)
            in2_sp(sp)
            mla_sp(sp)
            all_stored(sp, ALL_IN2)
            for j in range(2):
                load_unit(sp, Step(U_WO2 + j), w_out2[:, :, j * P:(j + 1) * P])
            mlstm_sp(sp)
            wo2_sp(sp)
            for t in range(2):
                load_unit(sp, Step(U_F2 + t), w_up[:, :, t * P:(t + 1) * P])
            f2_sp(sp)
            end_sp(sp)

        @block.gpsimd
        def _(pool):
            start_pool(pool)
            wup_pool(pool)
            in_pool(pool)
            mid_pool(pool)
            for j in range(2 * KT):
                split_unit(pool, Step(U_YA + j))
            f1_pool(pool)
            in2_pool(pool)
            mla_pool(pool)
            for j in range(2):
                split_unit(pool, Step(U_WO2 + j))
            mlstm_pool(pool)
            for j in range(2, KT):
                split_unit(pool, Step(U_WO2 + j))
            f2_pool(pool)

        @block.scalar
        def _(act):
            start_act(act)
            norm_act(act, "mix", no_wait, "norm_mix", h1hi)
            in_act(act)
            gla_act(act)
            merge_act(act)
            norm_act(act, "ffn", after_unit(U_WO), "norm_ffn", m2hi)
            f1_act(act)
            norm_act(act, "final", after_unit(U_IN2 - KT))
            norm_act(act, "mix2", lambda e, k: e.wait_ge(S["fin_done"], k + 1), "norm_pre_mix_2", g1hi)
            spill2_act(act)
            in2_act(act)
            mla_act(act)
            mlstm_act(act)
            norm_act(act, "post_mix", after_unit(U_WO2))
            norm_act(act, "mlp", lambda e, k: e.wait_ge(S["x_added"], k + 1), "norm_pre_mlp_2", h3hi)
            spill3_act(act)
            f2_act(act)
            norm_act(act, "post_mlp", after_unit(U_END - KT))
            end_act(act)

        @block.tensor
        def _(pe):
            start_pe(pe)
            in_pe(pe)
            gla_pe(pe)
            merge_pe(pe)
            wo_pe(pe)
            f1_pe(pe)
            norm_sum(pe, "final", KT)
            in2_pe(pe)
            mla_pe(pe)
            mlstm_pe(pe)
            wo2_pe(pe)
            f2_pe(pe)
            end_pe(pe)

        @block.vector
        def _(dve):
            norm_dve(dve, "mix", no_wait, "norm_mix", h1hi, h1lo)
            in_dve(dve)
            gla_dve(dve)
            merge_dve(dve)
            wo_dve(dve)
            norm_dve(dve, "ffn", no_wait, "norm_ffn", m2hi, m2lo)
            f1_dve(dve)
            norm_dve(dve, "final", no_wait)
            fin_dve(dve)
            norm_dve(dve, "mix2", no_wait, "norm_pre_mix_2", g1hi, g1lo)
            in2_dve(dve)
            mla_dve(dve)
            mlstm_dve(dve)
            wo2_dve(dve)
            norm_dve(dve, "mlp", no_wait, "norm_pre_mlp_2", h3hi, h3lo)
            f2_dve(dve)
            end_dve(dve)


OUTS = [((1, T, D), "float32")]


def rope_table():
    import numpy as np
    inv = (1.0 / (10000.0 ** (np.arange(0, 32, 2, dtype=np.float32) / 32))).astype(np.float32)
    t = np.zeros((P, 3), np.float32)
    t[:, 2] = 1.0
    for q in range(4):
        r = slice(64 + 16 * q, 80 + 16 * q)
        t[r, 0] = inv
        t[r, 1] = np.pi / 2 if q < 2 else 0.0
        t[r, 2] = -1.0 if q == 2 else 1.0
    return t


def kernel(**inputs):
    import numpy as np
    import concourse.bacc as bacc
    from concourse.bass_utils import run_bass_kernel_spmd

    nc = bacc.Bacc("TRN2", target_bir_lowering=False, num_devices=1)
    arrays, aps = {}, {}
    for name, a in {**inputs, "rope_table": rope_table()}.items():
        a = np.ascontiguousarray(a)
        arrays[f"in_{name}"] = a
        aps[name] = nc.dram_tensor(f"in_{name}", a.shape, mybir.dt.from_np(a.dtype), kind="ExternalInput").ap()
    shape, dtype = OUTS[0]
    out = nc.dram_tensor("out_0", shape, mybir.dt.from_np(np.dtype(dtype)), kind="ExternalOutput").ap()
    two_block_kernel(nc, aps, out)
    r = run_bass_kernel_spmd(nc, [arrays], core_ids=[0])
    return r.results[0]["out_0"]
```

```python
from contextlib import ExitStack

import concourse.bass as bass
from concourse import mybir

ALU = mybir.AluOpType
ACT = mybir.ActivationFunctionType
AX = mybir.AxisListType
F32 = mybir.dt.float32
F32R = mybir.dt.float32r
I32 = mybir.dt.int32
BF16 = mybir.dt.bfloat16

P = 128
D = 1024
T = 1024
KT = D // P
HALF = 512
EPS = 1e-6
GH = 4
C = T // P
D_FF = 2816
D_FF2 = 4096
BIG = 3.0e38

VEC_ROWS = [("norm_mix", 8), ("gla_norm", 8), ("pool_scale", 8), ("norm_ffn", 8), ("norm_final", 8),
            ("norm_pre_mix_2", 8), ("norm_post_mix_2", 8), ("norm_pre_mlp_2", 8),
            ("norm_post_mlp_2", 8), ("b_decay_fwd", 4), ("b_decay_bwd", 4), ("conv_w_2", 16),
            ("conv_b_2", 4), ("ml_head_norm_2", 4), ("q_norm_2", 2), ("kv_norm_2", 1)]
VEC = {}
NVEC = 0
for _name, _n in VEC_ROWS:
    VEC[_name] = NVEC
    NVEC += _n

G = 4
F1 = D_FF // P
F2 = D_FF2 // P
G1 = [G] * (F1 // G) + ([F1 % G] if F1 % G else [])
G2 = [G] * (F2 // G)
U_IN = 0
N_IN = 45
U_YA = U_IN + N_IN
U_WO = U_YA + KT
U_F1 = U_WO + KT
N_F1 = 2 * F1 + KT * len(G1)
U_IN2 = U_F1 + N_F1
N_IN2 = 17
U_QKV = U_IN2 + N_IN2
U_WO2 = U_QKV + 16
U_F2 = U_WO2 + KT
N_F2 = F2 + KT * len(G2)
U_END = U_F2 + N_F2

NORMS = [("mix", 8), ("ffn", 8), ("final", 8), ("mix2", 0), ("post_mix", 8),
         ("mlp", 8), ("post_mlp", 8)]
NORM_AT = {}
SQ_BASE = {}
_b = 0
for _i, (_name, _n) in enumerate(NORMS):
    NORM_AT[_name] = _i
    SQ_BASE[_name] = _b
    _b += _n

THREE = {U_IN2 + 4} | {U_QKV + 2 * h for h in range(8)}
LANDED = []
_c = [0, 0]
for _u in range(U_END):
    _c[_u % 2] += 48 if _u in THREE else 16
    LANDED.append(_c[_u % 2])


def par(u):
    return u % 2


def nth(u):
    return u // 2 + 1


class Step:

    def __init__(self, c, s=0, i=0):
        self.c, self.s, self.i = c, s, i

    def __add__(self, k):
        return Step(self.c + k, self.s, self.i)

    def times(self, m, plus=0):
        v = self.c * m + plus
        return self.i * (self.s * m) + v if self.s else v

    @property
    def par(self):
        return self.c % 2

    def nth(self, plus=0):
        v = self.c // 2 + 1 + plus
        return self.i * (self.s // 2) + v if self.s else v

    def landed(self):
        return self.i * (8 * self.s) + LANDED[self.c] if self.s else LANDED[self.c]


SEMS = ("p_norm pt_out w_hi w_split unit_done sq_done sq_added norm_sum norm_mean rstd_ready hi_ready lo_ready "
        "consts_ready vec_loaded vec_t xt_tr cols_ready xt_ev x_spilled gla_loaded "
        "qk_loaded v_loaded r_loaded wup_zero z_ready vt_ready sc_ready kdt_ready kv_ready "
        "o_ready o_sum o_stored z_log vtok_ready e_ready sc_fwd kdtok_ready osq_ready r_silu o_rstd o_hi "
        "rmask_ready z_min la_ready b_step dec_ready qk_weighted sc_tile state_step o_norm o_gate "
        "o_lo wpool_loaded u_loaded yb_ready gates_sig merged_hi pool_consts pool_step "
        "pooled_ready merged_lo yb_scaled merged_ready gate_silu act_hi act_full act_lo fin_done "
        "mla_loaded latent_hi rope_sin kr_copied vh_tok p_ready mixa_hi ang_step "
        "latent_lo cs_moved lat_loaded side_sq lat_sum lat_mean lat_rstd lat_normed q_copied q_a q_rope rs_inv mixa_lo s_stat "
        "vh_t s_ready pt_ready pv_ready gates_loaded conv_loaded mv_loaded om_loaded "
        "f_log mq_stored  qk_back w_summed num_copied den_ready hsq_sum conv_silu mv_tok om_sig st_exp h_sq h_rstd mixm_hi ml_consts w_ready "
        "m_step g_step conv_step st_w h_step mixm_lo am_t mv_t st_ready ho_ready "
        "y_scaled x_added up_sq sq_hi sq_lo acc_zero out_t out_ev").split()
PAIRED = ("x_loaded o_back gab_loaded  r_stored stored unit_out w_landed x_back").split()


def two_block_kernel(nc, A, out):
    ctx = ExitStack()

    def dram(name, shape):
        return nc.dram_tensor(name, shape, F32, kind="Internal").ap()

    x_in = A["x"][0]
    w_in = A["w_in"][0].rearrange("(k p) n -> p k n", p=P)
    w_ya = A["w_branch_gla"][0].rearrange("(k p) n -> p k n", p=P)
    w_out = A["w_out"][0].rearrange("(k p) n -> p k n", p=P)
    w_f1 = A["w_ffn_in"][0].rearrange("(k p) n -> p k n", p=P)
    w_f1o = A["w_ffn_out"][0].rearrange("(k p) n -> p k n", p=P)
    w_in2 = A["w_in_2"][0].rearrange("(k p) n -> p k n", p=P)
    w_uq = A["w_uq_2"][0].rearrange("(k p) n -> p k n", p=P)
    w_ukv = A["w_ukv_2"][0].rearrange("(k p) n -> p k n", p=P)
    w_out2 = A["w_out_2"][0].rearrange("(k p) n -> p k n", p=P)
    w_up = A["w_up_2"][0].rearrange("(k p) n -> p k n", p=P)
    w_down = A["w_down_2"][0].rearrange("(k p) n -> p k n", p=P)

    proj = dram("proj", (N_IN * P, T))
    proj2 = dram("proj2", (N_IN2 * P, T))
    o_d = dram("gla_out", (D, T))
    x_d = dram("x_feature_major", (D, T))
    x2_d = dram("x_block2", (D, T))
    x3_d = dram("x_after_mixer2", (D, T))
    r_d = dram("mlstm_log_weights", (C * 4, T))
    mq_d = dram("mlstm_q_k", (4 * P, T))

    def tile_of(t, j, n=1):
        return t[j * P:(j + n) * P, :].rearrange("(k p) t -> p k t", p=P)

    with ctx:
        def sb(name, shape, dt=F32, c=ctx):
            return c.enter_context(nc.sbuf_tensor(name, shape, dt))

        S = {n: ctx.enter_context(nc.semaphore(n)) for n in SEMS}
        for n in PAIRED:
            S[n] = [ctx.enter_context(nc.semaphore(f"{n}{i}")) for i in range(2)]
        S["out_stored"] = [ctx.enter_context(nc.semaphore(f"out_stored{i}")) for i in range(4)]
        S["r_bc_loaded"] = [ctx.enter_context(nc.semaphore(f"r_bc_loaded{i}")) for i in range(4)]

        PS = [ctx.enter_context(nc.psum_tensor(f"ps{i}", [P, T], F32)) for i in range(4)]

        acc = sb("acc", [P, KT, T])
        raw = sb("w_raw", [P, 2, KT * P])
        whi = sb("w_hi_t", [P, 2, KT * P], F32R)
        wlo = sb("w_lo_t", [P, 2, KT * P], F32R)
        stage = sb("stage", [P, 2, T])
        ssq = sb("ssq", [P, T])
        rstd = sb("rstd", [P, T])
        ident = sb("ident", [P, P])
        ones = sb("ones", [P, P])
        maskb = sb("maskb", [P, P])
        ident16 = sb("ident16", [P, P], BF16)
        negm16 = sb("negm16", [P, P], BF16)
        cols = sb("cols", [P, NVEC])
        small = sb("small", [P, 64])
        emcol = sb("emcol", [P, 32])
        bytok = sb("bytok", [P, 6 * C])
        gg = sb("gg", [P, KT])

        def col(name, k):
            return cols[:, VEC[name] + k:VEC[name] + k + 1]

        def tok(i):
            return bytok[:, i * C:(i + 1) * C].rearrange("p (c o) -> p c o", o=1)

        def by_tile(t):
            return t.rearrange("p (c t) -> p c t", c=C)

        with ExitStack() as s:
            vtok = sb("vtok", [P, C, 256], F32, s)
            sct = sb("sct", [P, C, P], F32, s)
            St = sb("states", [P, 2, C, 256], F32, s)
            qi = sb("qi", [P, 2, T], F32, s)
            qs = sb("qs", [P, T], F32, s)
            ks = sb("ks", [P, T], F32, s)
            lt = sb("lt", [P, T], F32, s)
            kdtok = sb("kdtok", [P, C, P], F32, s)
            bt = sb("bt", [P, T], F32, s)
            kd = sb("kd", [P, T], F32, s)
            mn = sb("mn", [P, T], F32, s)
            wup = sb("wup", [32, 2, HALF], F32, s)
            with ExitStack() as s2:
                xin = sb("xin", [P, C, T], F32, s2)
                vrow = sb("vrow", [P, P], F32, s2)
            with ExitStack() as s2:
                h1hi = sb("h1hi", [P, KT, T], F32R, s2)
                h1lo = sb("h1lo", [P, KT, T], F32R, s2)
        s_m2 = ExitStack()
        m2hi = sb("m2hi", [P, KT, T], F32R, s_m2)
        m2lo = sb("m2lo", [P, KT, T], F32R, s_m2)
        with ExitStack() as s:
            m1hi = sb("m1hi", [P, KT, T], F32R, s)
            m1lo = sb("m1lo", [P, KT, T], F32R, s)
            wpool = sb("wpool", [P, 4, 256], F32, s)
        with ExitStack() as s:
            g1hi = sb("g1hi", [P, KT, T], F32R, s)
            g1lo = sb("g1lo", [P, KT, T], F32R, s)
        with ExitStack() as s:
            kT = sb("kT", [P, 8, T], F32, s)
            Vt = sb("Vt", [P, C, 8, 64], F32, s)
            x4 = sb("x4", [P, 4, T], F32, s)
        with ExitStack() as s:
            qk = sb("qk", [P, 2, T], F32, s)
            ering = sb("ering", [P, 4, T], F32, s)
            Wt = sb("Wt", [P, 3, T], F32, s)
            wsum = sb("wsum", [P, T], F32, s)
            vtok2 = sb("vtok2", [P, 2, C, P], F32, s)
        s_m2.close()
        with ExitStack() as s:
            lat_place = sb("lat_place", [P, 3, T], F32, s)
            lat = sb("lat", [P, 3, T], F32, s)
            lat_r = sb("lat_r", [P, 2, T], F32, s)
            lat_s = sb("lat_s", [P, 3, T], F32, s)
            cb = sb("cb", [P, 4, T + 4], F32, s)
        with ExitStack() as s:
            a2hi = sb("a2hi", [P, KT, T], F32R, s)
            a2lo = sb("a2lo", [P, KT, T], F32R, s)
            h3hi = sb("h3hi", [P, KT, T], F32R, s)
            h3lo = sb("h3lo", [P, KT, T], F32R, s)
        with ExitStack() as s:
            orow = sb("orow", [P, 4, T], F32, s)
            orow_rest = sb("orow_rest", [P, 4, T], F32, s)
            sq8 = sb("sq8", [P, KT, T], F32, s)
            xr_place = sb("xr_place", [P, KT, T], F32, s)
            xr = sb("xr", [P, KT, T], F32, s)

        oback = [acc[:, a, :] for a in (0, 1, 2, 3, 6, 7)] + [kd[:, :], bt[:, :]]
        O_ORDER = (0, 1, 2, 3, 4, 7, 6, 5)
        gq, gk, gv, gr = acc[:, 0, :], acc[:, 1, :], acc[:, 2:4, :], acc[:, 4:6, :]
        rmask, bm = acc[:, 6, :], acc[:, 7, :]
        lrT = ssq[0:32, :]
        block = ctx.enter_context(nc.Block())


        def load_unit(sp, u, src, nk=KT, parts=None):
            if u.c >= 2:
                sp.wait_ge(S["w_split"], u.times(1, -1))
            dst = raw[:, u.par, 0:nk * P].rearrange("p (k c) -> p k c", k=nk)
            for (a, b, s_) in parts or [(0, P, src)]:
                sp.dma_start(dst[:, :, a:b], s_).then_inc(S["w_landed"][u.par], 16)

        def split_unit(pool, u, nk=KT):
            n = nk * P
            r, h, lo = raw[:, u.par, 0:n], whi[:, u.par, 0:n], wlo[:, u.par, 0:n]
            pool.wait_ge(S["w_landed"][u.par], u.landed())
            if u.c >= 2:
                pool.wait_ge(S["unit_done"], u.times(1, -1))
            pool.tensor_tensor(h, r, ones[:, 0:1].to_broadcast([P, n]), ALU.mult).then_inc(S["w_hi"], 1)
            pool.wait_ge(S["w_hi"], u.times(1, 1))
            pool.tensor_tensor(lo, r, h.bitcast(F32), ALU.subtract).then_inc(S["w_split"], 1)

        def mm_unit(pe, u, xhi, xlo, nk=KT, wait_k=None, pair=None):
            pe.wait_ge(S["w_split"], u.times(1, 1))
            if pair is not None:
                pe.wait_ge(S["unit_out"][(u.c - 1) % 2], nth(u.c - 1))
            elif u.c >= 2:
                pe.wait_ge(S["unit_out"][u.par], u.nth(-1))
            out = PS[u.par if pair is None else pair]
            for k in range(nk):
                if wait_k:
                    wait_k(k)
                w_h = whi[:, u.par, k * P:(k + 1) * P]
                w_l = wlo[:, u.par, k * P:(k + 1) * P]
                for n, (w, x) in enumerate(((w_h, xhi), (w_h, xlo), (w_l, xhi))):
                    for b in range(2):
                        mm = pe.matmul(out[:, b * HALF:(b + 1) * HALF], w,
                                       x[:, k, b * HALF:(b + 1) * HALF],
                                       start=(k == 0 and n == 0), stop=(k == nk - 1 and n == 2))
            mm.then_inc(S["unit_done"], 1)


        def norm_square(act, name, k, src):
            m = SQ_BASE[name] + k
            if m >= 2:
                act.wait_ge(S["sq_added"], m - 1)
            act.activation(stage[:, m % 2, :], src, ACT.Square).then_inc(S["sq_done"], 1)

        def norm_add(dve, name, k, src=None):
            m = SQ_BASE[name] + k
            sq = stage[:, m % 2, :] if src is None else src
            n = NORM_AT[name]
            dve.wait_ge(S["sq_done"], m + 1)
            if k == 0:
                if n:
                    dve.wait_ge(S["rstd_ready"], n)
                dve.tensor_copy(ssq[:, :], sq).then_inc(S["sq_added"], 1)
            else:
                dve.wait_ge(S["sq_added"], m)
                dve.tensor_tensor(ssq[:, :], ssq[:, :], sq, ALU.add).then_inc(S["sq_added"], 1)

        def sum_tokens(pe, pair, tiles):
            for c in range(C):
                for k, src in enumerate(tiles):
                    mm = pe.matmul(PS[pair][:, c * P:(c + 1) * P], src[:, c * P:(c + 1) * P], ones[:, :],
                                   start=(k == 0), stop=(k == len(tiles) - 1))
            return mm

        def spread_tokens(pe, pair, diagonal):
            for b in range(2):
                mm = pe.matmul(PS[pair][:, b * HALF:(b + 1) * HALF], ones[:, :],
                               diagonal[:, b * HALF:(b + 1) * HALF], start=True, stop=True)
            return mm

        def diagonal(dve, out, i):
            return dve.tensor_tensor(by_tile(out), ident[:, :].rearrange("p (o t) -> p o t", o=1)
                                     .to_broadcast([P, C, P]), tok(i).to_broadcast([P, C, P]), ALU.mult)

        def norm_sum(pe, name, nk):
            pe.wait_ge(S["sq_added"], SQ_BASE[name] + nk)
            sum_tokens(pe, 2, [ssq]).then_inc(S["norm_sum"], 1)

        def norm_spread(pe, name):
            pe.wait_ge(S["norm_mean"], 3 * (NORM_AT[name] + 1))
            spread_tokens(pe, 2, ssq).then_inc(S["norm_sum"], 1)

        def norm_mean(dve, name, nk):
            n = NORM_AT[name] + 1
            dve.wait_ge(S["norm_sum"], 2 * n - 1)
            dve.tensor_scalar(tok(0), by_tile(PS[2][:, :])[:, :, 0:1], 1.0 / (nk * P), EPS, ALU.mult, ALU.add)\
               .then_inc(S["norm_mean"], 1)
            dve.wait_ge(S["norm_mean"], 3 * n - 2)
            dve.reciprocal(tok(0), tok(0)).then_inc(S["norm_mean"], 1)
            dve.wait_ge(S["norm_mean"], 3 * n - 1)
            diagonal(dve, ssq[:, :], 0).then_inc(S["norm_mean"], 1)

        def norm_root(act, name, dst):
            act.wait_ge(S["norm_sum"], 2 * (NORM_AT[name] + 1))
            act.activation(dst, PS[2][:, :], ACT.Sqrt).then_inc(S["rstd_ready"], 1)

        def spread_at(pe, name, k0=3):
            return lambda k: norm_spread(pe, name) if k == k0 else None

        def scale_hi(act, k, src, g, hi):
            act.activation(hi[:, k, :], src, ACT.Copy, scale=g).then_inc(S["hi_ready"], 1)

        def scale_lo(dve, at, k, src, g, hi, lo):
            dve.wait_ge(S["hi_ready"], at + k + 1)
            dve.scalar_tensor_tensor(out=lo[:, k, :], in0=src, scalar=g, in1=hi[:, k, :].bitcast(F32),
                                     op0=ALU.mult, op1=ALU.subtract).then_inc(S["lo_ready"], 1)

        OPERAND = {"mix": 0, "ffn": 8, "mix2": 16, "mlp": 24}

        def norm_act(act, name, ready, g=None, hi=None, src=acc, nk=KT, dst=rstd):
            for k in range(nk):
                ready(act, k)
                if hi is not None:
                    scale_hi(act, k, src[:, k, :], col(g, k), hi)
                norm_square(act, name, k, src[:, k, :])
            norm_root(act, name, dst[:, :])

        def norm_dve(dve, name, ready, g=None, hi=None, lo=None, src=acc, nk=KT):
            for k in range(nk):
                if hi is not None:
                    scale_lo(dve, OPERAND[name], k, src[:, k, :], col(g, k), hi, lo)
                norm_add(dve, name, k)
            norm_mean(dve, name, nk)

        def lo_wait(pe, name):
            return lambda k: pe.wait_ge(S["lo_ready"], OPERAND[name] + k + 1)

        def no_wait(eng, k):
            pass

        def stores_before(u, first, before):
            f = first if first % 2 == u.par else first + 1
            return u.nth(-(f // 2 + 1) + before[u.par])

        def store_dve(dve, u, first, before, pair=None):
            dve.wait_ge(S["unit_done"], u.times(1, 1))
            if not (u.s == 0 and stores_before(u, first, before) == 0):
                v = stores_before(u, first, before)
                dve.wait_ge(S["stored"][u.par], v * 16)
            dve.tensor_tensor(stage[:, u.par, :], PS[u.par if pair is None else pair][:, :], rstd[:, :],
                              ALU.mult).then_inc(S["unit_out"][u.par], 1)

        def store_act(act, u, dst):
            act.wait_ge(S["unit_out"][u.par], u.nth())
            act.dma_start(dst, stage[:, u.par, :]).then_inc(S["stored"][u.par], 16)

        ALL_IN = (16 * ((N_IN + 1) // 2), 16 * (N_IN // 2))
        B2 = ((N_IN + 1) // 2, N_IN // 2)
        N0_IN2 = sum((U_IN2 + j) % 2 == 0 for j in range(N_IN2))
        ALL_IN2 = (ALL_IN[0] + 16 * N0_IN2, ALL_IN[1] + 16 * (N_IN2 - N0_IN2))

        def all_stored(eng, counts):
            for i in range(2):
                eng.wait_ge(S["stored"][i], counts[i])

        def ffn_order(groups, per_tile, u0, name):
            order = [("in", 0)]
            for g in range(1, len(groups)):
                order += [("in", g), ("out", g - 1)]
            order.append(("out", len(groups) - 1))
            seg, u = [], u0
            for kind, g in order:
                seg.append((kind, g, u))
                u += per_tile * groups[g] if kind == "in" else KT
            return seg

        SEG1 = ffn_order(G1, 2, U_F1, "f1")
        SEG2 = ffn_order(G2, 1, U_F2, "f2")

        def run_ffn(eng, seg, groups, per_tile, do):
            full = sum(g == G for g in groups)
            loops = (full - 1) // 2
            stride = 2 * (per_tile * G + KT)
            do(eng, seg[0][0], Step(0), Step(seg[0][2]), G)
            with eng.Fori(0, loops) as i:
                for kind, g, u in seg[1:5]:
                    do(eng, kind, Step(g, 2, i), Step(u, stride, i), G)
            for kind, g, u in seg[1 + 4 * loops:]:
                do(eng, kind, Step(g), Step(u), groups[g])

        N_CONST = 9

        def start_pool(pool):
            pool.memset(ident[:, :], 0.0).then_inc(S["consts_ready"], 1)
            pool.memset(ones[:, :], 1.0).then_inc(S["consts_ready"], 1)
            pool.memset(maskb[:, :], 1.0).then_inc(S["consts_ready"], 1)
            pool.memset(negm16[:, :], 0.0).then_inc(S["consts_ready"], 1)
            pool.memset(ident16[:, :], 0.0).then_inc(S["consts_ready"], 1)
            pool.wait_ge(S["consts_ready"], 5)
            pool.affine_select(out=ident[:, :], in_=ident[:, :], compare_op=ALU.not_equal, fill=1.0, base=0,
                               pattern=[[-1, P]], channel_multiplier=1).then_inc(S["consts_ready"], 1)
            pool.affine_select(out=maskb[:, :], in_=maskb[:, :], compare_op=ALU.is_gt, fill=0.0, base=0,
                               pattern=[[-1, P]], channel_multiplier=1).then_inc(S["consts_ready"], 1)
            pool.affine_select(out=negm16[:, :], in_=negm16[:, :], compare_op=ALU.is_ge, fill=-BIG, base=0,
                               pattern=[[-1, P]], channel_multiplier=1).then_inc(S["consts_ready"], 1)
            pool.affine_select(out=ident16[:, :], in_=ident16[:, :], compare_op=ALU.not_equal, fill=1.0, base=0,
                               pattern=[[-1, P]], channel_multiplier=1).then_inc(S["consts_ready"], 1)

        def start_sp(sp):
            def load_x(h):
                sp.dma_start(xin[:, 4 * h:4 * h + 4, :],
                             x_in[4 * h * P:(4 * h + 4) * P, :].rearrange("(c p) d -> p c d", p=P))\
                  .then_inc(S["x_loaded"][h], 16)

            load_x(0)
            for name, n in VEC_ROWS:
                v = A[name][0] if len(A[name].shape) > 1 else A[name]
                if len(v.shape) == 2:
                    v = v.rearrange("a n -> (a n)")
                sp.dma_start(vrow[VEC[name]:VEC[name] + n, :], v.rearrange("(k p) -> k p", p=P))\
                  .then_inc(S["vec_loaded"], 16)
            load_x(1)

        def start_pe(pe):
            pe.wait_ge(S["consts_ready"], N_CONST)
            for h in range(2):
                if h == 1:
                    pe.wait_ge(S["vec_loaded"], 16 * len(VEC_ROWS))
                    pe.transpose(PS[2][:, 0:NVEC], vrow[0:NVEC, :], ident[0:NVEC, 0:NVEC]).then_inc(S["vec_t"], 1)
                pe.wait_ge(S["x_loaded"][h], 16)
                for k in range(KT):
                    n = h * KT + k
                    if n >= 4:
                        pe.wait_ge(S["xt_ev"], n - 3)
                    bank = PS[n % 4 // 2][:, n % 2 * HALF:n % 2 * HALF + HALF]
                    for c in range(4):
                        tr = pe.transpose(bank[:, c * P:(c + 1) * P],
                                          xin[:, 4 * h + c, k * P:(k + 1) * P], ident[:, :])
                    tr.then_inc(S["xt_tr"], 1)

        def start_act(act):
            for h in range(2):
                if h == 1:
                    act.wait_ge(S["vec_t"], 1)
                    act.activation(cols[:, :], PS[2][:, 0:NVEC], ACT.Copy).then_inc(S["cols_ready"], 1)
                for k in range(KT):
                    n = h * KT + k
                    act.wait_ge(S["xt_tr"], n + 1)
                    act.activation(acc[:, k, h * HALF:(h + 1) * HALF],
                                   PS[n % 4 // 2][:, n % 2 * HALF:n % 2 * HALF + HALF], ACT.Copy)\
                       .then_inc(S["xt_ev"], 1)
            act.wait_ge(S["xt_ev"], 2 * KT)
            act.dma_start(tile_of(x_d, 0, KT), acc[:, :, :]).then_inc(S["x_spilled"], 16)
            act.wait_ge(S["cols_ready"], 1)

        LR0 = 3072
        REST0 = LR0 + 32

        def in_steps(eng, do):
            for j in range(2):
                do(eng, Step(j), j * P, j)
            with eng.Fori(0, 11) as i:
                for j in range(2):
                    do(eng, Step(2 + j, 2, i), i * (2 * P) + (2 + j) * P, None, i * (2 * P) + (2 + j) * P)
            do(eng, Step(24), LR0, 24)

        def in_sp(sp):
            def do(e, u, c0, j, r0=None):
                load_unit(e, u, w_in[:, :, bass.ds(c0, P)] if j is None else w_in[:, :, c0:c0 + P])
            in_steps(sp, do)

        def in_pool(pool):
            in_steps(pool, lambda e, u, c0, j, r0=None: split_unit(e, u))

        def in_pe(pe):
            def do(e, u, c0, j, r0=None):
                first = j == 0
                mm_unit(e, u, h1hi, h1lo, wait_k=lo_wait(e, "mix") if first else
                        spread_at(e, "mix") if j == 1 else None)
                if first:
                    norm_sum(e, "mix", KT)
            in_steps(pe, do)

        def in_act(act):
            def do(e, u, c0, j, r0=None):
                store_act(e, u, proj[bass.ds(r0, P), :] if j is None else proj[j * P:(j + 1) * P, :])
            in_steps(act, do)

        def in_dve(dve):
            dve.wait_ge(S["rstd_ready"], NORM_AT["mix"] + 1)
            in_steps(dve, lambda e, u, c0, j, r0=None: store_dve(e, u, 0, (0, 0)))

        NORM16 = 1.0 / 16.0
        QSCALE = float(P) ** -0.5
        MID, END = (63, 64), (P - 1, 0)
        Ering = [lt[:, :], mn[:, :]]
        MID0 = 25
        MIDS = (N_IN - MID0) // GH

        def order(d):
            return list(range(C)) if d == 0 else list(range(C - 1, -1, -1))

        def mid_weights(sp, u):
            c0 = REST0 + (u - MID0) * P
            if u < N_IN:
                load_unit(sp, Step(u), w_in[:, :, c0:c0 + P])
            else:
                ya_wo_unit(sp, u - N_IN)

        def gla_sp(sp):
            for u in (MID0, MID0 + 1):
                mid_weights(sp, u)
            sp.wait_ge(S["x_spilled"], 16)
            for i in range(2):
                sp.wait_ge(S["stored"][i], 16 * ((MID0 + 1 - i) // 2))
            sp.dma_start(lrT, proj[24 * P:24 * P + 32, :]).then_inc(S["gla_loaded"], 16)

            def qkv(h):
                if h:
                    sp.wait_ge(S["qk_weighted"], 8 * h)
                sp.dma_start(gq, proj[h * P:(h + 1) * P, :]).then_inc(S["qk_loaded"], 16)
                sp.dma_start(gk, proj[(4 + h) * P:(5 + h) * P, :]).then_inc(S["qk_loaded"], 16)
                if h:
                    sp.wait_ge(S["vt_ready"], 2 * h)
                sp.dma_start(gv, tile_of(proj, 8 + 2 * h, 2)).then_inc(S["v_loaded"], 16)

            def gate(h):
                if h:
                    sp.wait_ge(S["o_gate"], 4 * h)
                sp.dma_start(gr, tile_of(proj, 16 + 2 * h, 2)).then_inc(S["r_loaded"], 16)

            qkv(0)
            gate(0)
            for h in range(GH):
                for i in range(MIDS):
                    u = Step(MID0 + MIDS * h + i)
                    sp.wait_ge(S["unit_out"][u.par], u.nth())
                    sp.dma_start(proj[u.c * P:(u.c + 1) * P, :], stage[:, u.par, :])\
                      .then_inc(S["stored"][u.par], 16)
                    mid_weights(sp, u.c + 2)
                    if i == 2 and h < GH - 1:
                        qkv(h + 1)
                    if i == 2 and h == GH - 1:
                        sp.wait_ge(S["qk_weighted"], 8 * GH)
                        sp.wait_ge(S["vt_ready"], 2 * GH)
                        sp.wait_ge(S["o_stored"], 32 * (GH - 1))
                        for k in range(6):
                            sp.dma_start(oback[k], o_d[k * P:(k + 1) * P, :]).then_inc(S["o_back"][k // 5], 16)
                if h < GH - 1:
                    gate(h + 1)

        def mid_pool(pool):
            for u in range(MID0, N_IN):
                split_unit(pool, Step(u))

        def wup_pool(pool):
            pool.memset(wup[:, :, :], 0.0).then_inc(S["wup_zero"], 1)

        def wup_sp(sp):
            sp.wait_ge(S["wup_zero"], 1)
            sp.dma_start(wup[0:16, 0, :], A["w_decay_up_fwd"][0]).then_inc(S["gla_loaded"], 16)
            sp.dma_start(wup[16:32, 1, :], A["w_decay_up_bwd"][0]).then_inc(S["gla_loaded"], 16)

        def gla_pe(pe):
            pe.wait_ge(S["gla_loaded"], 48)
            pe.wait_ge(S["unit_out"][1], MID0 // 2)

            def z(h, d):
                if d == 0 and h:
                    pe.wait_ge(S["o_rstd"], h)
                if d == 1:
                    pe.wait_ge(S["sc_fwd"], h + 1)
                for b in range(2):
                    mm = pe.matmul(PS[3 - 2 * d][:, b * HALF:(b + 1) * HALF], wup[:, d, h * P:(h + 1) * P],
                                   lrT[:, b * HALF:(b + 1) * HALF], start=True, stop=True)
                mm.then_inc(S["z_ready"], 1)

            def turn_v(h):
                pe.wait_ge(S["v_loaded"], 16 * (h + 1))
                if h:
                    pe.wait_ge(S["o_gate"], 4 * h - 1)
                for half in range(2):
                    if half:
                        pe.wait_ge(S["z_min"], 2 * h + 1)
                        pe.wait_ge(S["z_log"], 6 * h + 1)
                    for c in range(4):
                        for e in range(2):
                            tr = pe.transpose(PS[2 + half][:, c * 256 + e * P:c * 256 + (e + 1) * P],
                                              gv[:, e, (4 * half + c) * P:(4 * half + c + 1) * P], ident[:, :])
                    tr.then_inc(S["vt_ready"], 1)

            def scores(h, d):
                n = 2 * h + d
                pe.wait_ge(S["qk_weighted"], 4 * n + 3)
                if d == 0 and h:
                    pe.wait_ge(S["o_gate"], 4 * h - 3)
                if d == 1:
                    pe.wait_ge(S["z_min"], n + 1)
                    pe.wait_ge(S["z_log"], 3 * n + 1)
                for c in range(C):
                    mm = pe.matmul(PS[1][:, c * P:(c + 1) * P], ks[:, c * P:(c + 1) * P],
                                   qs[:, c * P:(c + 1) * P], start=True, stop=True)
                mm.then_inc(S["sc_ready"], 1)

            def turn_k(h, d):
                n = 2 * h + d
                pe.wait_ge(S["qk_weighted"], 4 * n + 4)
                pe.wait_ge(S["vtok_ready"], 2 * h + 2)
                if n:
                    pe.wait_ge(S["state_step"], 7 * n)
                for c in range(C):
                    tr = pe.transpose(PS[2][:, c * P:(c + 1) * P], kd[:, c * P:(c + 1) * P], ident[:, :])
                tr.then_inc(S["kdt_ready"], 1)

            def keys_values(h, d):
                pe.wait_ge(S["kdtok_ready"], 2 * h + d + 1)
                for i, c in enumerate(order(d)[:C - 1]):
                    mm = pe.matmul(PS[3 - i // 4][:, i % 4 * 256:(i % 4 + 1) * 256], kdtok[:, c, :],
                                   vtok[:, c, :], start=True, stop=True)
                    if i == 3:
                        mm.then_inc(S["kv_ready"], 1)
                mm.then_inc(S["kv_ready"], 1)

            def output(h):
                pe.wait_ge(S["sc_tile"], h + 1)
                pe.wait_ge(S["state_step"], 14 * h + 14)
                pe.wait_ge(S["qk_weighted"], 8 * h + 5)
                for e in range(2):
                    for c in range(C):
                        o = PS[1 + e][:, c * P:(c + 1) * P]
                        terms = [(vtok[:, c, e * P:(e + 1) * P], sct[:, c, :])]
                        if c > 0:
                            terms.append((St[:, 0, c, e * P:(e + 1) * P], qi[:, 0, c * P:(c + 1) * P]))
                        if c < C - 1:
                            terms.append((St[:, 1, c, e * P:(e + 1) * P], qi[:, 1, c * P:(c + 1) * P]))
                        for i, (w, x) in enumerate(terms):
                            mm = pe.matmul(o, w, x, start=(i == 0), stop=(i == len(terms) - 1))
                    mm.then_inc(S["o_ready"], 1)

            def square_sum(h):
                pe.wait_ge(S["o_norm"], 4 * h + 1)
                sum_tokens(pe, 3, [mn]).then_inc(S["o_sum"], 1)

            def spread_norm(h):
                pe.wait_ge(S["o_norm"], 4 * h + 4)
                spread_tokens(pe, 3, mn).then_inc(S["o_sum"], 1)

            def mid_unit(h, i, amid=None):
                mm_unit(pe, Step(MID0 + MIDS * h + i), h1hi, h1lo, pair=0, wait_k=amid)

            for h in range(GH):
                z(h, 0)
                mid_unit(h, 0)
                turn_v(h)
                scores(h, 0)
                turn_k(h, 0)
                z(h, 1)
                keys_values(h, 0)
                mid_unit(h, 1)
                mid_unit(h, 2)
                scores(h, 1)
                turn_k(h, 1)
                keys_values(h, 1)
                mid_unit(h, 3)
                output(h)
                mid_unit(h, 4, lambda k: square_sum(h) if k == 3 else spread_norm(h) if k == 6 else None)

        def high_o(act, k):
            if k < 6:
                act.wait_ge(S["o_back"][k // 5], 16 if k == 5 else 80)
            act.activation(m2hi[:, k, :], oback[k], ACT.Copy).then_inc(S["o_hi"], 1)

        def low_o(dve, k):
            dve.wait_ge(S["o_hi"], O_ORDER.index(k) + 1)
            if k == 5:
                dve.wait_ge(S["o_lo"], O_ORDER.index(7) + 1)
            dve.tensor_tensor(m2lo[:, k, :], oback[k], m2hi[:, k, :].bitcast(F32), ALU.subtract)\
               .then_inc(S["o_lo"], 1)

        def gla_act(act):
            def store_o(h):
                for e in range(2):
                    act.wait_ge(S["o_gate"], 2 * (2 * h + e + 1))
                    act.dma_start(o_d[(2 * h + e) * P:(2 * h + e + 1) * P, :], (kd if e == 0 else bt)[:, :])\
                       .then_inc(S["o_stored"], 16)

            for h in range(GH):
                for d in range(2):
                    n = 2 * h + d
                    bias = col("b_decay_bwd" if d else "b_decay_fwd", h)
                    act.wait_ge(S["z_ready"], n + 1)
                    if n:
                        act.wait_ge(S["qk_weighted"], 4 * n - 1)
                    act.activation(lt[:, :], PS[3 - 2 * d][:, :], ACT.Abs, bias=bias).then_inc(S["z_log"], 1)
                    act.wait_ge(S["z_log"], 3 * n + 1)
                    act.activation(lt[:, :], lt[:, :], ACT.Exp, scale=-1.0).then_inc(S["z_log"], 1)
                    act.wait_ge(S["z_log"], 3 * n + 2)
                    act.activation(lt[:, :], lt[:, :], ACT.Ln, bias=1.0).then_inc(S["z_log"], 1)
                    if d == 0 and h:
                        store_o(h - 1)
                    for i, (ready, src, scale) in enumerate(
                            ((1, bt, NORM16), (2, bm, NORM16), (2, bm, -NORM16), (3, bm, NORM16))):
                        m = 4 * n + i
                        act.wait_ge(S["b_step"], 3 * n + ready)
                        if m >= 2:
                            act.wait_ge(S["qk_weighted"], m - 1)
                        act.activation(Ering[m % 2], src[:, :], ACT.Exp, scale=scale).then_inc(S["e_ready"], 1)
                    if d == 0:
                        for half in range(2):
                            act.wait_ge(S["vt_ready"], 2 * h + half + 1)
                            if h:
                                act.wait_ge(S["o_ready"], 2 * h)
                            act.activation(vtok[:, 4 * half:4 * half + 4, :],
                                           PS[2 + half][:, :].rearrange("p (c e) -> p c e", c=4), ACT.Copy)\
                               .then_inc(S["vtok_ready"], 1)
                    if d == 0:
                        act.wait_ge(S["sc_ready"], n + 1)
                        if h:
                            act.wait_ge(S["o_ready"], 2 * h)
                        act.activation(sct[:, :, :], PS[1][:, :].rearrange("p (c s) -> p c s", c=C), ACT.Copy)\
                           .then_inc(S["sc_fwd"], 1)
                    act.wait_ge(S["kdt_ready"], n + 1)
                    if n:
                        act.wait_ge(S["kv_ready"], 2 * n)
                    act.activation(kdtok[:, :, :], PS[2][:, :].rearrange("p (c s) -> p c s", c=C), ACT.Copy)\
                       .then_inc(S["kdtok_ready"], 1)
                for e in range(2):
                    act.wait_ge(S["o_ready"], 2 * h + e + 1)
                    act.activation((qs if e == 0 else ks)[:, :], PS[1 + e][:, :], ACT.Square)\
                       .then_inc(S["osq_ready"], 1)
                act.wait_ge(S["r_loaded"], 16 * (h + 1))
                act.activation(gr, gr, ACT.Silu).then_inc(S["r_silu"], 1)
                act.wait_ge(S["o_sum"], 2 * h + 2)
                act.activation(mn[:, :], PS[3][:, :], ACT.Sqrt).then_inc(S["o_rstd"], 1)
                if h == GH - 1:
                    for k in O_ORDER[:5]:
                        high_o(act, k)

        def gla_dve(dve):
            dve.wait_ge(S["x_spilled"], 16)
            dve.memset(rmask, 1.0).then_inc(S["rmask_ready"], 1)
            dve.wait_ge(S["rmask_ready"], 1)
            r3 = rmask.rearrange("p (c t) -> p c t", c=C)
            dve.memset(r3[:, :, 0:1], 0.0).then_inc(S["rmask_ready"], 1)
            dve.wait_ge(S["rmask_ready"], 2)
            dve.wait_ge(S["cols_ready"], 1)

            def evacuate(h, i):
                store_dve(dve, Step(MID0 + MIDS * h + i), 0, (0, 0), pair=0)

            for h in range(GH):
                for d in range(2):
                    n = 2 * h + d
                    bias = col("b_decay_bwd" if d else "b_decay_fwd", h)
                    dve.wait_ge(S["z_log"], 3 * n + 1)
                    if n:
                        dve.wait_ge(S["qk_weighted"], 4 * n)
                    if h and d == 0:
                        dve.wait_ge(S["o_gate"], 4 * h)
                    dve.tensor_scalar(mn[:, :], PS[3 - 2 * d][:, :], bias, 0.0, ALU.add, ALU.min)\
                       .then_inc(S["z_min"], 1)
                    dve.wait_ge(S["z_log"], 3 * n + 3)
                    dve.wait_ge(S["z_min"], n + 1)
                    dve.tensor_tensor(mn[:, :], mn[:, :], lt[:, :], ALU.subtract).then_inc(S["la_ready"], 1)
                    dve.wait_ge(S["la_ready"], n + 1)
                    if n:
                        dve.wait_ge(S["e_ready"], 4 * n)
                    if h and d == 0:
                        dve.wait_ge(S["o_stored"], 32 * h)
                    st = slice(None) if d == 0 else slice(None, None, -1)
                    dve.tensor_tensor_scan(bt[:, st], rmask, mn[:, st], 0.0, ALU.mult, ALU.add)\
                       .then_inc(S["b_step"], 1)
                    dve.wait_ge(S["b_step"], 3 * n + 1)
                    b3 = bt[:, :].rearrange("p (c t) -> p c t", c=C)
                    bm3 = bm.rearrange("p (c t) -> p c t", c=C)
                    dve.tensor_tensor(bm3, b3, b3[:, :, MID[d]:MID[d] + 1].to_broadcast([P, C, P]),
                                      ALU.subtract).then_inc(S["b_step"], 1)
                    if d == 0:
                        dve.wait_ge(S["qk_loaded"], 32 * (h + 1))
                    if d == 1:
                        evacuate(h, 1)
                    m = 4 * n
                    dve.wait_ge(S["e_ready"], m + 1)
                    e3 = Ering[0].rearrange("p (c t) -> p c t", c=C)
                    dve.tensor_copy(small[:, 40:40 + C].rearrange("p (c o) -> p c o", o=1),
                                    e3[:, :, END[d]:END[d] + 1]).then_inc(S["dec_ready"], 1)
                    if h:
                        dve.wait_ge(S["o_ready"], 2 * h)
                    dve.scalar_tensor_tensor(out=qi[:, d, :], in0=gq, scalar=QSCALE, in1=Ering[0],
                                             op0=ALU.mult, op1=ALU.mult).then_inc(S["qk_weighted"], 1)
                    dve.wait_ge(S["e_ready"], m + 2)
                    if n:
                        dve.wait_ge(S["sc_ready"], n)
                    if h and d == 0:
                        dve.wait_ge(S["o_norm"], 4 * h - 3)
                    dve.scalar_tensor_tensor(out=qs[:, :], in0=gq, scalar=QSCALE, in1=Ering[1],
                                             op0=ALU.mult, op1=ALU.mult).then_inc(S["qk_weighted"], 1)
                    dve.wait_ge(S["e_ready"], m + 3)
                    dve.tensor_tensor(bm3, b3[:, :, END[d]:END[d] + 1].to_broadcast([P, C, P]), b3,
                                      ALU.subtract).then_inc(S["b_step"], 1)
                    dve.tensor_tensor(ks[:, :], gk, Ering[0], ALU.mult).then_inc(S["qk_weighted"], 1)
                    if d == 0:
                        evacuate(h, 0)
                    dve.wait_ge(S["e_ready"], m + 4)
                    if n:
                        dve.wait_ge(S["kdt_ready"], n)
                    dve.tensor_tensor(kd[:, :], gk, Ering[1], ALU.mult).then_inc(S["qk_weighted"], 1)
                    if d == 1:
                        evacuate(h, 2)
                    if d == 1:
                        dve.wait_ge(S["sc_ready"], n + 1)
                        dve.wait_ge(S["sc_fwd"], h + 1)
                        dve.copy_predicated(
                            sct[:, :, :],
                            maskb[:, :].bitcast(I32).rearrange("p (o s) -> p o s", o=1).to_broadcast([P, C, P]),
                            PS[1][:, :].rearrange("p (c s) -> p c s", c=C)).then_inc(S["sc_tile"], 1)
                    od = order(d)
                    dve.wait_ge(S["dec_ready"], n + 1)
                    for i in range(C - 1):
                        if i == 0:
                            dve.wait_ge(S["kv_ready"], 2 * n + 1)
                        if i == 4:
                            dve.wait_ge(S["kv_ready"], 2 * n + 2)
                        kv = PS[3 - i // 4][:, i % 4 * 256:(i % 4 + 1) * 256]
                        if i == 0:
                            ins = dve.tensor_copy(St[:, d, od[1], :], kv)
                        else:
                            dve.wait_ge(S["state_step"], (C - 1) * n + i)
                            ins = dve.scalar_tensor_tensor(
                                out=St[:, d, od[i + 1], :], in0=St[:, d, od[i], :],
                                scalar=small[:, 40 + od[i]:41 + od[i]], in1=kv, op0=ALU.mult, op1=ALU.add)
                        ins.then_inc(S["state_step"], 1)
                evacuate(h, 3)
                dve.wait_ge(S["osq_ready"], 2 * h + 2)
                dve.tensor_tensor(mn[:, :], qs[:, :], ks[:, :], ALU.add).then_inc(S["o_norm"], 1)
                dve.wait_ge(S["o_sum"], 2 * h + 1)
                dve.tensor_scalar(tok(0), by_tile(PS[3][:, :])[:, :, 0:1], 1.0 / 256, EPS, ALU.mult, ALU.add)\
                   .then_inc(S["o_norm"], 1)
                dve.wait_ge(S["o_norm"], 4 * h + 2)
                dve.reciprocal(tok(0), tok(0)).then_inc(S["o_norm"], 1)
                dve.wait_ge(S["o_norm"], 4 * h + 3)
                diagonal(dve, mn[:, :], 0).then_inc(S["o_norm"], 1)
                evacuate(h, 4)
                if h == GH - 1:
                    for k in O_ORDER[:2]:
                        low_o(dve, k)
                dve.wait_ge(S["o_rstd"], h + 1)
                dve.wait_ge(S["r_silu"], h + 1)
                dve.wait_ge(S["kdt_ready"], 2 * h + 2)
                for e in range(2):
                    t = (kd if e == 0 else bt)[:, :]
                    dve.scalar_tensor_tensor(out=t, in0=PS[1 + e][:, :], scalar=col("gla_norm", 2 * h + e),
                                             in1=mn[:, :], op0=ALU.mult, op1=ALU.mult)\
                       .then_inc(S["o_gate"], 1)
                    dve.wait_ge(S["o_gate"], 2 * (2 * h + e + 1) - 1)
                    dve.tensor_tensor(t, t, gr[:, e, :], ALU.mult).then_inc(S["o_gate"], 1)

        ub, csb, pooled = acc[:, 0, :], acc[:, 1:3, :].rearrange("p a t -> p (a t)"), acc[:, 3, :]
        gab = [(acc[:, 4, :], acc[:, 6, :]), (acc[:, 5, :], acc[:, 7, :])]
        ones_row = ssq
        Z0 = 8

        def ya_wo_unit(sp, j):
            w = w_ya if j < KT else w_out
            load_unit(sp, Step(U_YA + j), w[:, :, j % KT * P:(j % KT + 1) * P])

        def merge_sp(sp):
            sp.wait_ge(S["unit_done"], N_IN)
            sp.dma_start(wpool[:, :, :], A["w_pool_group"][0].rearrange("g c d -> c g d"))\
              .then_inc(S["wpool_loaded"], 16)
            all_stored(sp, ALL_IN)
            for j in range(KT):
                g = j // 2
                sp.wait_ge(S["o_lo"], (1, KT)[j > 0])
                if j % 2 == 0:
                    if g:
                        sp.wait_ge(S["pooled_ready"], g)
                    sp.dma_start(ub, proj[(25 + g) * P:(26 + g) * P, :]).then_inc(S["u_loaded"], 16)
                if j == 0:
                    sp.wait_ge(S["o_lo"], 5)
                    sp.wait_ge(S["o_gate"], 4 * GH)
                if j >= 2:
                    sp.wait_ge(S["merged_ready"], j - 1)
                a, b = gab[j % 2]
                sp.dma_start(a, proj[(29 + j) * P:(30 + j) * P, :]).then_inc(S["gab_loaded"][j % 2], 16)
                sp.dma_start(b, proj[(37 + j) * P:(38 + j) * P, :]).then_inc(S["gab_loaded"][j % 2], 16)
                ya_wo_unit(sp, j + 2)

        def merge_pe(pe):
            pe.wait_ge(S["o_gate"], 4 * GH - 3)
            for j in range(KT):
                mm_unit(pe, Step(U_YA + j), m2hi, m2lo,
                        wait_k=(lambda k: pe.wait_ge(S["o_lo"], k + 1 if k < 5 else KT)) if j == 0 else None)
                pe.wait_ge(S["wpool_loaded"], 16)
                pe.wait_ge(S["pooled_ready"], j // 2 + 1)
                if j:
                    pe.wait_ge(S["yb_scaled"], j)
                for b in range(2):
                    mm = pe.matmul(PS[2][:, b * HALF:(b + 1) * HALF], wpool[:, j // 2, j % 2 * P:(j % 2 + 1) * P],
                                   pooled[:, b * HALF:(b + 1) * HALF], start=True, stop=True)
                mm.then_inc(S["yb_ready"], 1)

        def merge_act(act):
            act.wait_ge(S["o_gate"], 4 * GH)
            for k in O_ORDER[5:]:
                high_o(act, k)
            for j in range(KT):
                a, b = gab[j % 2]
                act.wait_ge(S["gab_loaded"][j % 2], 32 * (j // 2 + 1))
                act.activation(a, a, ACT.Sigmoid).then_inc(S["gates_sig"], 1)
                act.activation(b, b, ACT.Sigmoid).then_inc(S["gates_sig"], 1)
                act.wait_ge(S["merged_ready"], j + 1)
                act.activation(m1hi[:, j, :], stage[:, j % 2, :], ACT.Copy).then_inc(S["merged_hi"], 1)

        def merge_dve(dve):
            for k in O_ORDER[2:]:
                low_o(dve, k)
            all_stored(dve, ALL_IN)
            dve.wait_ge(S["z_ready"], 2 * GH)
            dve.memset(ones_row[:, :], 1.0).then_inc(S["pool_consts"], 1)
            dve.memset(csb[:, 0:Z0 + 1], 0.0).then_inc(S["pool_consts"], 1)
            dve.wait_ge(S["pool_consts"], 1)

            def pool(g):
                w = 2 << g
                h = w // 2
                dve.wait_ge(S["u_loaded"], 16 * (g + 1))
                dve.tensor_tensor_scan(csb[:, Z0 + 1:Z0 + 1 + T], ones_row[:, :], ub, 0.0, ALU.mult, ALU.add)\
                   .then_inc(S["pool_step"], 1)
                dve.wait_ge(S["pool_step"], 3 * g + 1)
                dve.tensor_copy(csb[:, Z0 + 1 + T:Z0 + 8 + T], csb[:, Z0 + T:Z0 + T + 1].to_broadcast([P, 7]))\
                   .then_inc(S["pool_step"], 1)
                dve.wait_ge(S["pool_step"], 3 * g + 2)
                dve.wait_ge(S["pool_consts"], 2)
                if g:
                    dve.wait_ge(S["yb_ready"], 2 * g)
                dve.tensor_tensor(pooled, csb[:, Z0 + h:Z0 + h + T], csb[:, Z0 - h:Z0 - h + T], ALU.subtract)\
                   .then_inc(S["pool_step"], 1)
                dve.wait_ge(S["pool_step"], 3 * g + 3)
                edges = [(t, t + h) for t in range(h)] + [(t, T - t + h) for t in range(T - h + 1, T)]
                dve.scalar_tensor_tensor(out=pooled[:, h:T - h + 1], in0=pooled[:, h:T - h + 1], scalar=1.0 / w,
                                         in1=ub[:, h:T - h + 1], op0=ALU.mult, op1=ALU.subtract)
                for n, (t, count) in enumerate(edges):
                    ins = dve.scalar_tensor_tensor(out=pooled[:, t:t + 1], in0=pooled[:, t:t + 1],
                                                   scalar=1.0 / count, in1=ub[:, t:t + 1],
                                                   op0=ALU.mult, op1=ALU.subtract)
                ins.then_inc(S["pooled_ready"], 1)

            def split_lo(j):
                dve.wait_ge(S["merged_hi"], j + 1)
                dve.tensor_tensor(m1lo[:, j, :], stage[:, j % 2, :], m1hi[:, j, :].bitcast(F32), ALU.subtract)\
                   .then_inc(S["merged_lo"], 1)

            for j in range(KT):
                a, b = gab[j % 2]
                u = Step(U_YA + j)
                if j % 2 == 0:
                    pool(j // 2)
                if j:
                    split_lo(j - 1)
                dve.wait_ge(S["yb_ready"], j + 1)
                dve.wait_ge(S["gates_sig"], 2 * j + 2)
                dve.scalar_tensor_tensor(out=b, in0=PS[2][:, :], scalar=col("pool_scale", j), in1=b,
                                         op0=ALU.mult, op1=ALU.mult).then_inc(S["yb_scaled"], 1)
                dve.wait_ge(S["unit_done"], u.times(1, 1))
                dve.wait_ge(S["gates_sig"], 2 * j + 1)
                dve.tensor_tensor(a, PS[u.par][:, :], a, ALU.mult).then_inc(S["unit_out"][u.par], 1)
                dve.wait_ge(S["unit_out"][u.par], u.nth())
                dve.wait_ge(S["yb_scaled"], j + 1)
                dve.tensor_tensor(stage[:, j % 2, :], a, b, ALU.add).then_inc(S["merged_ready"], 1)
            split_lo(KT - 1)

        def wo_sp(sp):
            sp.wait_ge(S["merged_ready"], KT)
            sp.wait_ge(S["pooled_ready"], 4)
            sp.wait_ge(S["yb_ready"], KT)
            for i in range(2):
                sp.dma_start(acc[:, 4 * i:4 * i + 4, :], tile_of(x_d, 4 * i, 4)).then_inc(S["x_back"][i], 16)
            for j in range(KT + 2, 2 * KT):
                ya_wo_unit(sp, j)

        def wo_pe(pe):
            for j in range(KT):
                mm_unit(pe, Step(U_WO + j), m1hi, m1lo,
                        wait_k=(lambda k: pe.wait_ge(S["merged_lo"], k + 1)) if j == 0 else None)

        def add_dve(dve, u, j, ready=None):
            dve.wait_ge(S["unit_done"], u.times(1, 1))
            dve.tensor_tensor(acc[:, j, :], PS[u.par][:, :], acc[:, j, :], ALU.add)\
               .then_inc(S["unit_out"][u.par], 1)

        def wo_dve(dve):
            def ffn_tile(k):
                scale_lo(dve, OPERAND["ffn"], k, acc[:, k, :], col("norm_ffn", k), m2hi, m2lo)
                norm_add(dve, "ffn", k)

            for j in range(KT):
                if j % 4 == 0:
                    dve.wait_ge(S["x_back"][j // 4], 16)
                add_dve(dve, Step(U_WO + j), j)
                if j:
                    ffn_tile(j - 1)
            ffn_tile(KT - 1)
            norm_mean(dve, "ffn", KT)

        def after_unit(u0):
            def ready(eng, k):
                u = Step(u0 + k)
                eng.wait_ge(S["unit_out"][u.par], u.nth())
            return ready

        def slot1(g, size):
            return G * g.par + G - size

        def f1_sp(sp):
            def do(e, kind, g, u, size):
                for t in range(size if kind == "in" else 0):
                    c0 = g.times(G * P, t * P)
                    load_unit(e, u + 2 * t, w_f1[:, :, bass.ds(c0, P)])
                    c1 = g.times(G * P, D_FF + t * P)
                    load_unit(e, u + (2 * t + 1), w_f1[:, :, bass.ds(c1, P)])
                for j in range(KT if kind == "out" else 0):
                    load_unit(e, u + j, w_f1o[:, bass.ds(g.times(G), size), j * P:(j + 1) * P], size)
            run_ffn(sp, SEG1, G1, 2, do)

        def f1_pool(pool):
            def do(e, kind, g, u, size):
                for t in range(2 * size if kind == "in" else KT):
                    split_unit(e, u + t, KT if kind == "in" else size)
                    if u.c == U_IN2 - KT and t >= 3:
                        fin_pool(e, t - 3)
            run_ffn(pool, SEG1, G1, 2, do)

        def f1_pe(pe):
            def do(e, kind, g, u, size):
                if kind == "in":
                    for t in range(2 * size):
                        start = u.s == 0 and g.c == 0
                        mm_unit(e, u + t, m2hi, m2lo, wait_k=lo_wait(e, "ffn") if start and t == 0 else
                                spread_at(e, "ffn") if start and t == 1 else None)
                        if start and t == 0:
                            norm_sum(e, "ffn", KT)
                else:
                    e.wait_ge(S["act_lo"], g.times(G, size))
                    s0 = slot1(g, size)
                    for j in range(KT):
                        mm_unit(e, u + j, m1hi[:, s0:s0 + size, :], m1lo[:, s0:s0 + size, :], size)
            run_ffn(pe, SEG1, G1, 2, do)

        def f1_act(act):
            def do(e, kind, g, u, size):
                for t in range(size if kind == "in" else 0):
                    ug = u + 2 * t
                    e.wait_ge(S["unit_out"][ug.par], ug.nth())
                    e.activation(stage[:, 0, :], stage[:, 0, :], ACT.Silu).then_inc(S["gate_silu"], 1)
                    e.wait_ge(S["act_full"], g.times(G, t + 1))
                    e.activation(m1hi[:, slot1(g, size) + t, :], ssq[:, :], ACT.Copy).then_inc(S["act_hi"], 1)
            run_ffn(act, SEG1, G1, 2, do)

        def f1_dve(dve):
            def do(e, kind, g, u, size):
                if kind == "out":
                    for j in range(KT):
                        add_dve(e, u + j, j)
                        if u.c == U_IN2 - KT:
                            fin_dve_tile(e, j)
                    return
                for t in range(size):
                    n = g.times(G, t + 1)
                    ug, uu = u + 2 * t, u + (2 * t + 1)
                    e.wait_ge(S["unit_done"], ug.times(1, 1))
                    e.tensor_tensor(stage[:, 0, :], PS[ug.par][:, :], rstd[:, :], ALU.mult)\
                     .then_inc(S["unit_out"][ug.par], 1)
                    e.wait_ge(S["unit_out"][ug.par], ug.nth())
                    e.wait_ge(S["unit_done"], uu.times(1, 1))
                    e.tensor_tensor(stage[:, 1, :], PS[uu.par][:, :], rstd[:, :], ALU.mult)\
                     .then_inc(S["unit_out"][uu.par], 1)
                    e.wait_ge(S["unit_out"][uu.par], uu.nth())
                    e.wait_ge(S["gate_silu"], n)
                    e.tensor_tensor(ssq[:, :], stage[:, 0, :], stage[:, 1, :], ALU.mult)\
                     .then_inc(S["act_full"], 1)
                    e.wait_ge(S["act_hi"], n)
                    e.wait_ge(S["act_full"], n)
                    e.tensor_tensor(m1lo[:, slot1(g, size) + t, :], ssq[:, :],
                                    m1hi[:, slot1(g, size) + t, :].bitcast(F32), ALU.subtract)\
                     .then_inc(S["act_lo"], 1)
            dve.wait_ge(S["rstd_ready"], NORM_AT["ffn"] + 1)
            run_ffn(dve, SEG1, G1, 2, do)

        sq2, ssq2, r1 = lat_s, lat_r[:, 0, :], lat_r[:, 1, :]

        def last_tiles(eng, k):
            if k >= KT - 2:
                eng.wait_ge(S["unit_done"], U_IN2)

        def fin_act(act):
            ready = after_unit(U_IN2 - KT)
            act.wait_ge(S["cols_ready"], 2)
            for k in range(KT):
                ready(act, k)
                last_tiles(act, k)
                scale_hi(act, k, acc[:, k, :], gg[:, k:k + 1], g1hi)
                norm_square(act, "final", k, acc[:, k, :])
                if k >= 2:
                    act.wait_ge(S["fin_done"], k - 1)
                act.activation(sq2[:, k % 2, :], acc[:, k, :], ACT.Square, scale=col("norm_final", k))\
                   .then_inc(S["side_sq"], 1)
            f = 2 * NORM_AT["final"]
            act.wait_ge(S["norm_sum"], f + 3)
            act.activation(r1, PS[2][:, :], ACT.Sqrt).then_inc(S["rstd_ready"], 1)
            act.wait_ge(S["norm_sum"], f + 4)
            act.activation(rstd[:, :], PS[3][:, :], ACT.Sqrt).then_inc(S["rstd_ready"], 1)

        def fin_pool(pool, k):
            m = SQ_BASE["final"] + k
            pool.wait_ge(S["sq_done"], m + 1)
            if k == 0:
                pool.wait_ge(S["act_lo"], F1)
                pool.tensor_tensor(ssq[:, :], stage[:, m % 2, :], ones[:, 0:1].to_broadcast([P, T]), ALU.mult)\
                    .then_inc(S["sq_added"], 1)
            else:
                pool.wait_ge(S["sq_added"], m)
                pool.tensor_tensor(ssq[:, :], ssq[:, :], stage[:, m % 2, :], ALU.add)\
                    .then_inc(S["sq_added"], 1)

        def fin_dve_tile(dve, k):
            scale_lo(dve, OPERAND["mix2"], k, acc[:, k, :], gg[:, k:k + 1], g1hi, g1lo)
            dve.wait_ge(S["side_sq"], k + 1)
            if k == 0:
                dve.tensor_copy(ssq2, sq2[:, 0, :]).then_inc(S["fin_done"], 1)
            else:
                dve.wait_ge(S["fin_done"], k)
                dve.tensor_tensor(ssq2, ssq2, sq2[:, k % 2, :], ALU.add).then_inc(S["fin_done"], 1)

        def fin_pe(pe):
            norm_sum(pe, "final", KT)
            pe.wait_ge(S["fin_done"], KT)
            sum_tokens(pe, 3, [ssq2]).then_inc(S["norm_sum"], 1)

        def fin_spread(pe):
            f = 3 * NORM_AT["final"]
            pe.wait_ge(S["norm_mean"], f + 3)
            spread_tokens(pe, 2, ssq).then_inc(S["norm_sum"], 1)
            pe.wait_ge(S["norm_mean"], f + 6)
            spread_tokens(pe, 3, ssq2).then_inc(S["norm_sum"], 1)

        def fin_means(dve):
            norm_mean(dve, "final", KT)
            dve.wait_ge(S["norm_sum"], 2 * NORM_AT["final"] + 2)
            dve.scalar_tensor_tensor(out=tok(1), in0=by_tile(PS[3][:, :])[:, :, 0:1], scalar=1.0 / D,
                                     in1=tok(0), op0=ALU.mult, op1=ALU.mult).then_inc(S["fin_done"], 1)
            dve.wait_ge(S["fin_done"], KT + 1)
            dve.tensor_scalar(tok(1), tok(1), EPS, None, ALU.add).then_inc(S["fin_done"], 1)
            dve.wait_ge(S["fin_done"], KT + 2)
            dve.reciprocal(tok(1), tok(1)).then_inc(S["fin_done"], 1)
            dve.wait_ge(S["fin_done"], KT + 3)
            dve.tensor_tensor(tok(1), tok(1), tok(0), ALU.mult).then_inc(S["norm_mean"], 1)
            dve.wait_ge(S["norm_mean"], 3 * NORM_AT["final"] + 4)
            diagonal(dve, ssq2, 1).then_inc(S["norm_mean"], 2)

        FIN0 = KT + 3

        def fin_dve(dve):
            dve.wait_ge(S["rstd_ready"], NORM_AT["final"] + 1)
            for k in range(KT):
                dve.scalar_tensor_tensor(out=acc[:, k, :], in0=acc[:, k, :], scalar=col("norm_final", k),
                                         in1=r1, op0=ALU.mult, op1=ALU.mult).then_inc(S["fin_done"], 1)

        def spill2_act(act):
            act.wait_ge(S["fin_done"], FIN0 + KT)
            act.dma_start(tile_of(x2_d, 0, KT), acc[:, :, :]).then_inc(S["x_spilled"], 16)

        KR0 = 1928
        IN2_COLS = [j * P for j in range(12)] + [1536, 1544, 1672, 1800]
        IN2_ORDER = [12, 13, 14, 15, 16] + list(range(12))

        def in2_sp(sp):
            for j, t in enumerate(IN2_ORDER):
                if t < 16:
                    load_unit(sp, Step(U_IN2 + j), w_in2[:, :, IN2_COLS[t]:IN2_COLS[t] + P])
                else:
                    load_unit(sp, Step(U_IN2 + j), None, parts=[
                        (0, 96, w_in2[:, :, KR0 - 64:KR0 + 32]), (96, 112, w_in2[:, :, KR0 + 16:KR0 + 32]),
                        (112, 128, w_in2[:, :, KR0:KR0 + 16])])
                if j == 4:
                    gates_sp(sp)
                if j == 8:
                    for i in range(3, 5):
                        sp.wait_ge(S["stored"][(U_IN2 + i) % 2], stored2(i))
                    sp.dma_start(lat[:, :, :], tile_of(proj2, 13, 3)).then_inc(S["lat_loaded"], 16)
                    sp.dma_start(KR, proj2[16 * P + 64:17 * P, :]).then_inc(S["lat_loaded"], 16)
                if j == 12:
                    for i in range(7, 9):
                        sp.wait_ge(S["stored"][(U_IN2 + i) % 2], stored2(i))
                    sp.dma_start(cb[:, :, 3:3 + T], tile_of(proj2, 0, 4)).then_inc(S["conv_loaded"], 16)
                if 8 <= j < 12:
                    rows_sp(sp, 2 * (j - 8))

        def stored2(j):
            return ALL_IN[(U_IN2 + j) % 2] + 16 * (j // 2 + 1)

        def in2_pool(pool):
            for j in range(N_IN2):
                if j:
                    split_unit(pool, Step(U_IN2 + j))
                if j == 0:
                    pool.wait_ge(S["unit_done"], U_IN2)
                    pool.memset(cb[:, :, 0:3], 0.0).then_inc(S["ml_consts"], 1)

        def in2_pe(pe):
            for j in range(N_IN2):
                mm_unit(pe, Step(U_IN2 + j), g1hi, g1lo, wait_k=lo_wait(pe, "mix2") if j == 0 else
                        (lambda k: fin_spread(pe) if k == 3 else None) if j == 1 else None)
                if j == 0:
                    fin_pe(pe)
                if j == 8:
                    pe.wait_ge(S["g_step"], 3 * C - 1)
                    pe.wait_ge(S["rstd_ready"], NORM_AT["mix2"] + 1)
                    for w, row in enumerate((arow, mrow)):
                        for i in range(C):
                            tr = pe.transpose(PS[2][:, 32 * w + 4 * i:32 * w + 4 * i + 4],
                                              row[:, i * P:(i + 1) * P], ident[0:4, 0:4])
                    tr.then_inc(S["am_t"], 1)
                if j == 9:
                    pe.wait_ge(S["side_sq"], KT + 3)
                    sum_tokens(pe, 3, [lat_s[:, 0, :], lat_s[:, 1, :]]).then_inc(S["lat_sum"], 1)
                    sum_tokens(pe, 2, [lat_s[:, 2, :]]).then_inc(S["lat_sum"], 1)
                if j == 11:
                    for i in range(2):
                        pe.wait_ge(S["lat_mean"], 3 * i + 3)
                        spread_tokens(pe, 3 - i, lat_r[:, i, :]).then_inc(S["lat_sum"], 1)

        def in2_act(act):
            for j in range(N_IN2):
                t = IN2_ORDER[j]
                store_act(act, Step(U_IN2 + j), proj2[t * P:(t + 1) * P, :])
                if j == 0:
                    spill2_act(act)
                if j == 2:
                    gates_act(act)
                if j == 8:
                    act.wait_ge(S["am_t"], 1)
                    act.activation(acol, PS[2][:, 0:32], ACT.Copy)
                    act.activation(emcol[:, :], PS[2][:, 32:64], ACT.Exp, scale=-1.0)
                    act.wait_ge(S["lat_loaded"], 32)
                    for k in range(3):
                        act.activation(lat_s[:, k, :], lat[:, k, :], ACT.Square).then_inc(S["side_sq"], 1)
                if j == 9:
                    act.wait_ge(S["ang_step"], 10)
                    act.activation(CS, CSQ, ACT.Sin).then_inc(S["rope_sin"], 1)
                if j == 11:
                    for i in range(2):
                        act.wait_ge(S["lat_sum"], 4)
                        act.activation(lat_r[:, i, :], PS[3 - i][:, :], ACT.Sqrt).then_inc(S["lat_rstd"], 1)
                if j == 12:
                    for k in range(3):
                        act.wait_ge(S["lat_normed"], k + 1)
                        gain = col("q_norm_2", k) if k < 2 else col("kv_norm_2", 0)
                        act.activation(m2hi[:, k, :], lat[:, k, :], ACT.Copy, scale=gain)\
                           .then_inc(S["latent_hi"], 1)
                if 13 <= j < 17:
                    t = j - 13
                    act.wait_ge(S["conv_step"], 4 * t + 4)
                    act.activation(cq[:, t, :], cq[:, t, :], ACT.Silu).then_inc(S["conv_silu"], 1)
                    act.wait_ge(S["conv_silu"], t + 1)
                    act.dma_start(mq_d[t * P:(t + 1) * P, :], cq[:, t, :]).then_inc(S["mq_stored"], 16)

        def in2_dve(dve):
            dve.wait_ge(S["rstd_ready"], NORM_AT["mix2"] + 1)
            for j in range(N_IN2):
                store_dve(dve, Step(U_IN2 + j), U_IN2, B2)
                if j == 0:
                    fin_dve(dve)
                if j == 3:
                    gates_dve(dve)
                if 4 <= j < 8:
                    rows_dve(dve, 2 * (j - 4))
                    rows_dve(dve, 2 * (j - 4) + 1)
                if j == 8:
                    angles(dve, 0)
                if j == 9:
                    angles(dve, 1)
                if j == 10:
                    lat_means(dve)
                    rope_key(dve)
                if j == 12:
                    for k in range(3):
                        dve.wait_ge(S["lat_rstd"], k // 2 + 1)
                        dve.tensor_tensor(lat[:, k, :], lat[:, k, :], lat_r[:, k // 2, :], ALU.mult)\
                           .then_inc(S["lat_normed"], 1)
                if j == 13:
                    for k in range(3):
                        gain = col("q_norm_2", k) if k < 2 else col("kv_norm_2", 0)
                        dve.wait_ge(S["latent_hi"], k + 1)
                        dve.scalar_tensor_tensor(out=m2lo[:, k, :], in0=lat[:, k, :], scalar=gain,
                                                 in1=m2hi[:, k, :].bitcast(F32), op0=ALU.mult,
                                                 op1=ALU.subtract).then_inc(S["latent_lo"], 1)
                if 12 <= j < 16:
                    conv_dve(dve, j - 12)

        ig, lf, fz, mrow = acc[0:4, 0, :], acc[0:4, 1, :], acc[0:4, 2, :], acc[0:4, 3, :]
        grow, arow, on4 = acc[0:4, 4, :], acc[0:4, 7, :], ssq[0:4, :]
        rrow = [acc[0:4, 5, :], acc[0:4, 6, :]]
        acol = small[:, 0:32]
        cq = acc[:, 3:7, :]
        RP = slice(64, 128)
        NOPE, RO, SW = slice(0, 64), slice(64, 96), slice(96, 128)
        CS, CSQ, KR, KROPE = acc[RP, 0, :], acc[RP, 1, :], acc[RP, 2, :], acc[RO, 7, :]
        ptab = small[:, 36:39]
        MAGIC = 12582912.0
        PI = 3.1415925
        TWO_PI = (6.28125, 0.0019350051879882812, 3.019915981956753e-07)

        def angles(dve, part):
            if part == 0:
                dve.wait_ge(S["mla_loaded"], 32)
                dve.tensor_copy(CS, CSQ.bitcast(I32)).then_inc(S["ang_step"], 1)
                dve.wait_ge(S["ang_step"], 1)
                dve.tensor_scalar(CS, CS, ptab[RP, 0:1], None, ALU.mult).then_inc(S["ang_step"], 1)
                dve.wait_ge(S["ang_step"], 2)
                dve.tensor_scalar(CSQ, CS, ptab[RP, 1:2], 0.15915494309189535, ALU.add, ALU.mult)\
                   .then_inc(S["ang_step"], 1)
                dve.wait_ge(S["ang_step"], 3)
                dve.tensor_scalar(CSQ, CSQ, MAGIC, None, ALU.add).then_inc(S["ang_step"], 1)
                dve.wait_ge(S["ang_step"], 4)
                dve.tensor_scalar(CSQ, CSQ, MAGIC, None, ALU.subtract).then_inc(S["ang_step"], 1)
                return
            for i, part in enumerate(TWO_PI):
                dve.wait_ge(S["ang_step"], 3 + i + 2)
                dve.scalar_tensor_tensor(out=CS, in0=CSQ, scalar=-part, in1=CS,
                                         op0=ALU.mult, op1=ALU.add).then_inc(S["ang_step"], 1)
            dve.wait_ge(S["ang_step"], 8)
            dve.tensor_scalar(CSQ, CS, ptab[RP, 1:2], PI, ALU.add, ALU.min).then_inc(S["ang_step"], 1)
            dve.wait_ge(S["ang_step"], 9)
            dve.tensor_scalar(CSQ, CSQ, -PI, None, ALU.max).then_inc(S["ang_step"], 1)

        def lat_means(dve):
            for i, n in enumerate((2, 1)):
                dve.wait_ge(S["lat_sum"], i + 1)
                dve.tensor_scalar(tok(i), by_tile(PS[3 - i][:, :])[:, :, 0:1], 1.0 / (n * P), EPS,
                                  ALU.mult, ALU.add).then_inc(S["lat_mean"], 1)
                dve.wait_ge(S["lat_mean"], 3 * i + 1)
                dve.reciprocal(tok(i), tok(i)).then_inc(S["lat_mean"], 1)
                dve.wait_ge(S["lat_mean"], 3 * i + 2)
                diagonal(dve, lat_r[:, i, :], i).then_inc(S["lat_mean"], 1)

        def rope_key(dve):
            dve.wait_ge(S["rope_sin"], 1)
            dve.tensor_scalar(CS, CS, ptab[RP, 2:3], None, ALU.mult).then_inc(S["ang_step"], 1)
            dve.wait_ge(S["ang_step"], 11)
            dve.wait_ge(S["lat_loaded"], 32)
            dve.tensor_tensor(KROPE, acc[RO, 2, :], acc[RO, 0, :], ALU.mult).then_inc(S["ang_step"], 1)
            dve.tensor_tensor(acc[RO, 1, :], acc[SW, 2, :], acc[SW, 0, :], ALU.mult).then_inc(S["ang_step"], 1)
            dve.wait_ge(S["ang_step"], 13)
            dve.tensor_tensor(KROPE, KROPE, acc[RO, 1, :], ALU.add).then_inc(S["ang_step"], 1)

        def gates_sp(sp):
            sp.wait_ge(S["x_spilled"], 32)
            sp.wait_ge(S["stored"][U_IN2 % 2], stored2(0))
            sp.dma_start(CSQ.bitcast(I32), A["positions_2"].to_broadcast([64, T])).then_inc(S["mla_loaded"], 16)
            sp.dma_start(ptab, A["rope_table"]).then_inc(S["mla_loaded"], 16)
            sp.dma_start(ig, proj2[12 * P:12 * P + 4, :]).then_inc(S["gates_loaded"], 16)
            sp.dma_start(fz, proj2[12 * P + 4:12 * P + 8, :]).then_inc(S["gates_loaded"], 16)
            sp.dma_start(small[0:4, 60:61], A["b_gates_2"][:, 0:4].rearrange("a h -> h a"))\
              .then_inc(S["gates_loaded"], 16)
            sp.dma_start(small[0:4, 61:62], A["b_gates_2"][:, 4:8].rearrange("a h -> h a"))\
              .then_inc(S["gates_loaded"], 16)

        def rows_sp(sp, first):
            for J in (first, first + 1):
                sp.wait_ge(S["g_step"], 3 * J + 3)
                sp.dma_start(r_d[J * 4:J * 4 + 4, J * P:T], rrow[J % 2][:, J * P:T])\
                  .then_inc(S["r_stored"][J % 2], 16)

        def gates_act(act):
            act.wait_ge(S["gates_loaded"], 64)
            bf = small[0:4, 61:62]
            act.activation(lf, fz, ACT.Abs, bias=bf).then_inc(S["f_log"], 1)
            act.wait_ge(S["f_log"], 1)
            act.activation(lf, lf, ACT.Exp, scale=-1.0).then_inc(S["f_log"], 1)
            act.wait_ge(S["f_log"], 2)
            act.activation(lf, lf, ACT.Ln, bias=1.0).then_inc(S["f_log"], 1)

        def gates_dve(dve):
            dve.wait_ge(S["gates_loaded"], 64)
            bi, bf = small[0:4, 60:61], small[0:4, 61:62]
            dve.memset(on4, 1.0).then_inc(S["m_step"], 1)
            dve.tensor_scalar(ig, ig, bi, None, ALU.add).then_inc(S["m_step"], 1)
            dve.wait_ge(S["f_log"], 1)
            dve.tensor_scalar(fz, fz, bf, 0.0, ALU.add, ALU.min).then_inc(S["m_step"], 1)
            dve.wait_ge(S["f_log"], 3)
            dve.wait_ge(S["m_step"], 3)
            dve.tensor_tensor(lf, fz, lf, ALU.subtract).then_inc(S["m_step"], 1)
            dve.wait_ge(S["m_step"], 4)
            dve.wait_ge(S["m_step"], 2)
            dve.tensor_tensor_scan(mrow, lf, ig, 0.0, ALU.add, ALU.max).then_inc(S["m_step"], 1)

        def rows_dve(dve, J):
            dve.wait_ge(S["m_step"], 5)
            s = slice(J * P, T)
            b = slice(J * P, (J + 1) * P)
            if J:
                dve.wait_ge(S["g_step"], 3 * J)
            dve.tensor_tensor_scan(grow[:, s], on4[:, s], lf[:, s], 0.0, ALU.mult, ALU.add)\
               .then_inc(S["g_step"], 1)
            dve.wait_ge(S["g_step"], 3 * J + 1)
            dve.tensor_tensor(arow[:, b], ig[:, b], grow[:, b], ALU.subtract).then_inc(S["g_step"], 1)
            if J >= 2:
                dve.wait_ge(S["r_stored"][J % 2], 16 * (J // 2))
            dve.tensor_tensor(rrow[J % 2][:, s], grow[:, s], mrow[:, s], ALU.subtract)\
               .then_inc(S["g_step"], 1)

        def conv_dve(dve, t):
            dve.wait_ge(S["ml_consts"], 1)
            dve.wait_ge(S["conv_loaded"], 16)
            dve.wait_ge(S["am_t"], 1)
            for i in range(2):
                dve.wait_ge(S["r_stored"][i], 16 * C // 2)
            dve.tensor_scalar(cq[:, t, :], cb[:, t, 3:3 + T], col("conv_w_2", 12 + t), col("conv_b_2", t),
                              ALU.mult, ALU.add).then_inc(S["conv_step"], 1)
            for k in range(3):
                dve.wait_ge(S["conv_step"], 4 * t + k + 1)
                dve.scalar_tensor_tensor(out=cq[:, t, :], in0=cb[:, t, k:k + T],
                                         scalar=col("conv_w_2", 4 * k + t), in1=cq[:, t, :],
                                         op0=ALU.mult, op1=ALU.add).then_inc(S["conv_step"], 1)

        ROT, VTH = x4[:, 0, :], x4[:, 3, :]
        QK_SCALE = 96.0 ** -0.5
        qT = acc
        NQ = [(h, i) for h in range(8) for i in range(C)]

        def mla_sp(sp):
            for h in range(8):
                q0 = h * 96
                load_unit(sp, Step(U_QKV + 2 * h), None, 2, parts=[
                    (0, 96, w_uq[:, :, q0:q0 + 96]), (96, 112, w_uq[:, :, q0 + 80:q0 + 96]),
                    (112, 128, w_uq[:, :, q0 + 64:q0 + 80])])
                load_unit(sp, Step(U_QKV + 2 * h + 1), w_ukv[:, :, h * P:(h + 1) * P], 1)

        def mla_pool(pool):
            for h in range(8):
                split_unit(pool, Step(U_QKV + 2 * h), 2)
                split_unit(pool, Step(U_QKV + 2 * h + 1), 1)

        def vt_act(act, h):
            act.wait_ge(S["vh_t"], h + 1)
            act.activation(Vt[:, :, h, :], PS[3][:, 0:HALF].rearrange("p (c e) -> p c e", c=C), ACT.Copy)\
               .then_inc(S["vh_tok"], 1)

        def mla_act(act):
            act.wait_ge(S["unit_done"], U_QKV)
            act.wait_ge(S["ang_step"], 14)
            act.wait_ge(S["cs_moved"], 1)
            for h in range(8):
                uq, uk = Step(U_QKV + 2 * h), Step(U_QKV + 2 * h + 1)
                if h == 3:
                    act.wait_ge(S["mq_stored"], 64)
                act.wait_ge(S["unit_done"], uq.times(1, 1))
                act.activation(qT[NOPE, h, :], PS[uq.par][NOPE, :], ACT.Copy).then_inc(S["q_copied"], 1)
                act.wait_ge(S["unit_done"], uk.times(1, 1))
                act.activation(kT[NOPE, h, :], PS[uk.par][NOPE, :], ACT.Copy)
                if h:
                    act.wait_ge(S["vh_t"], h)
                act.activation(VTH[RP, :], PS[uk.par][RP, :], ACT.Copy).then_inc(S["unit_out"][uk.par], 1)
                act.activation(kT[RO, h, :], KROPE, ACT.Copy).then_inc(S["kr_copied"], 1)
                if h:
                    vt_act(act, h - 1)
            vt_act(act, 7)
            for n, (h, i) in enumerate(NQ):
                N = (i + 1) * P
                act.wait_ge(S["s_stat"], 2 * n + 2)
                if n >= 2:
                    act.wait_ge(S["pt_ready"], n - 1)
                act.activation(x4[:, n % 2, 0:N], PS[n % 2][:, 0:N], ACT.Exp, bias=sm(n, 1), scale=QK_SCALE,
                               accum_out=sm(n, 2)).then_inc(S["p_ready"], 1)
                if n:
                    pt_copy(act, n - 1)
                if n > 1 and (n - 2) % 16 == 15:
                    mixa(act, (n - 2) // 16)
            pt_copy(act, 63)
            mixa(act, 3)

        def sm(n, what):
            c = 40 + 5 * (n % 2) + what
            return small[:, c:c + 1]

        def pt_copy(act, n):
            N = (NQ[n][1] + 1) * P
            act.wait_ge(S["pt_ready"], n + 1)
            if n >= 2:
                act.wait_ge(S["pv_ready"], n - 1)
            act.activation(x4[:, 2 + n % 2, 0:N], PS[2][:, 0:N], ACT.Copy).then_inc(S["pt_out"], 1)

        def mixa(act, pair):
            act.wait_ge(S["pv_ready"], 16 * (pair + 1))
            act.activation(m2hi[:, 4 + pair, :], PS[3][:, :], ACT.Copy).then_inc(S["mixa_hi"], 1)

        def mla_dve(dve):
            dve.wait_ge(S["unit_done"], U_QKV)
            dve.wait_ge(S["ang_step"], 11)
            dve.tensor_copy(ROT[RP, :], CS).then_inc(S["cs_moved"], 1)
            dve.wait_ge(S["cs_moved"], 1)
            for h in range(8):
                uq = Step(U_QKV + 2 * h)
                q = PS[uq.par]
                dve.wait_ge(S["q_copied"], h + 1)
                if h:
                    dve.wait_ge(S["q_rope"], h)
                if h == 7:
                    dve.wait_ge(S["kr_copied"], 8)
                dve.tensor_tensor(qT[RO, h, :], q[RO, :], ROT[RO, :], ALU.mult).then_inc(S["q_a"], 1)
                dve.tensor_tensor(x4[RO, 1, :], q[SW, :], ROT[SW, :], ALU.mult).then_inc(S["unit_out"][uq.par], 1)
                dve.wait_ge(S["unit_out"][uq.par], uq.nth())
                dve.wait_ge(S["q_a"], h + 1)
                dve.tensor_tensor(qT[RO, h, :], qT[RO, h, :], x4[RO, 1, :], ALU.add).then_inc(S["q_rope"], 1)

            def normalise(n):
                N = (NQ[n][1] + 1) * P
                dve.wait_ge(S["p_ready"], n + 1)
                dve.reciprocal(sm(n, 3), sm(n, 2)).then_inc(S["rs_inv"], 1)
                dve.wait_ge(S["rs_inv"], n + 1)
                dve.tensor_scalar(x4[:, n % 2, 0:N], x4[:, n % 2, 0:N], sm(n, 3), None, ALU.mult)\
                   .then_inc(S["p_norm"], 1)

            def mixa_low(pair):
                dve.wait_ge(S["mixa_hi"], pair + 1)
                dve.tensor_tensor(m2lo[:, 4 + pair, :], PS[3][:, :], m2hi[:, 4 + pair, :].bitcast(F32),
                                  ALU.subtract).then_inc(S["mixa_lo"], 1)

            for n, (h, i) in enumerate(NQ):
                N = (i + 1) * P
                dve.wait_ge(S["s_ready"], n + 1)
                dve.tensor_reduce(sm(n, 0), PS[n % 2][:, 0:N], AX.X, ALU.max).then_inc(S["s_stat"], 1)
                dve.wait_ge(S["s_stat"], 2 * n + 1)
                dve.tensor_scalar(sm(n, 1), sm(n, 0), -QK_SCALE, None, ALU.mult).then_inc(S["s_stat"], 1)
                if n:
                    normalise(n - 1)
                if n > 1 and (n - 2) % 16 == 15:
                    mixa_low((n - 2) // 16)
            normalise(63)
            mixa_low(3)

        def mla_pe(pe):
            def turn_values(h):
                uk = Step(U_QKV + 2 * h + 1)
                pe.wait_ge(S["unit_out"][uk.par], uk.nth())
                if h:
                    pe.wait_ge(S["vh_tok"], h)
                else:
                    pe.wait_ge(S["lat_rstd"], 2)
                for c in range(C):
                    tr = pe.transpose(PS[3][:, c * 64:(c + 1) * 64], VTH[RP, c * P:(c + 1) * P],
                                      ident[RP, RP])
                tr.then_inc(S["vh_t"], 1)

            pe.wait_ge(S["latent_lo"], 3)
            for h in range(8):
                mm_unit(pe, Step(U_QKV + 2 * h), m2hi, m2lo, 2)
                if h:
                    turn_values(h - 1)
                mm_unit(pe, Step(U_QKV + 2 * h + 1), m2hi[:, 2:3, :], m2lo[:, 2:3, :], 1)
            turn_values(7)
            pe.wait_ge(S["q_rope"], 8)
            pe.wait_ge(S["kr_copied"], 8)
            pe.wait_ge(S["vh_tok"], 8)

            def scores(n):
                h, i = NQ[n]
                N = (i + 1) * P
                if n >= 2:
                    pe.wait_ge(S["p_ready"], n - 1)
                for b in range(0, N, HALF):
                    w = min(HALF, N - b)
                    pe.matmul(PS[n % 2][:, b:b + w], qT[0:96, h, i * P:(i + 1) * P],
                              kT[0:96, h, b:b + w], start=True, stop=True)
                mm = pe.matmul(PS[n % 2][:, N - P:N], ident16[:, :], negm16[:, :], start=False, stop=True,
                               skip_group_check=True)
                mm.then_inc(S["s_ready"], 1)

            def turn(n):
                pe.wait_ge(S["p_norm"], n + 1)
                if n:
                    pe.wait_ge(S["pt_out"], n)
                for j in range(NQ[n][1] + 1):
                    tr = pe.transpose(PS[2][:, j * P:(j + 1) * P], x4[:, n % 2, j * P:(j + 1) * P], ident[:, :])
                tr.then_inc(S["pt_ready"], 1)

            def values(n):
                h, i = NQ[n]
                if n % 16 == 0 and n:
                    pe.wait_ge(S["mixa_lo"], n // 16)
                pe.wait_ge(S["pt_out"], n + 1)
                o = PS[3][h % 2 * 64:h % 2 * 64 + 64, i * P:(i + 1) * P]
                for j in range(i + 1):
                    mm = pe.matmul(o, Vt[:, j, h, :], x4[:, 2 + n % 2, j * P:(j + 1) * P], start=(j == 0), stop=(j == i))
                mm.then_inc(S["pv_ready"], 1)

            scores(0)
            scores(1)
            for n in range(64):
                if n + 2 < 64:
                    scores(n + 2)
                turn(n)
                if n:
                    values(n - 1)
            values(63)

        NS = 4 * C
        hn, sqb, vTm = acc[:, 0, :], acc[:, 2, :], acc[:, 3, :]
        omT = [acc[:, 4, :], acc[:, 5, :]]
        HS = 11

        def om_sp(sp, h):
            if h >= 2:
                sp.wait_ge(S["h_step"], HS * (h - 1))
            sp.dma_start(omT[h % 2], proj2[(8 + h) * P:(9 + h) * P, :]).then_inc(S["om_loaded"], 16)

        def mlstm_sp(sp):
            sp.wait_ge(S["mq_stored"], 64)
            sp.dma_start(stage[:, 0, :], mq_d[0:P, :]).then_inc(S["qk_back"], 16)
            sp.dma_start(stage[:, 1, :], mq_d[2 * P:3 * P, :]).then_inc(S["qk_back"], 16)
            sp.wait_ge(S["mixa_lo"], 4)
            sp.dma_start(vTm, proj2[4 * P:5 * P, :]).then_inc(S["mv_loaded"], 16)
            for n in range(NS):
                h, J = n // C, n % C
                if n >= 4:
                    sp.wait_ge(S["st_w"], n - 3)
                sp.dma_start(ering[:, n % 4, J * P:T],
                             r_d[J * 4 + h:J * 4 + h + 1, J * P:T].to_broadcast([P, T - J * P]))\
                  .then_inc(S["r_bc_loaded"][n % 4], 16)
                if J == 2 and h < 3:
                    sp.wait_ge(S["mv_t"], h + 1)
                    sp.dma_start(vTm, proj2[(5 + h) * P:(6 + h) * P, :]).then_inc(S["mv_loaded"], 16)
                if n == 2:
                    om_sp(sp, 0)
                    for i in range(2):
                        sp.dma_start(qk[:, i, :], mq_d[(2 * i + 1) * P:(2 * i + 2) * P, :])\
                          .then_inc(S["qk_back"], 16)
                if J == 7 and h < 3:
                    om_sp(sp, h + 1)

        def vtok_act(act, h):
            act.wait_ge(S["mv_t"], h + 1)
            if h >= 2:
                act.wait_ge(S["ho_ready"], C * (h - 1))
            act.activation(vtok2[:, h % 2, :, :], PS[3][:, :].rearrange("p (c e) -> p c e", c=C), ACT.Copy)\
               .then_inc(S["mv_tok"], 1)

        def gate_act(act, h):
            act.wait_ge(S["om_loaded"], 16 * (h + 1))
            act.activation(omT[h % 2], omT[h % 2], ACT.Sigmoid).then_inc(S["om_sig"], 1)

        def num_act(act, h):
            act.wait_ge(S["ho_ready"], C * (h + 1))
            act.activation(sqb, PS[2][:, :], ACT.Square).then_inc(S["h_sq"], 1)
            act.activation(hn, PS[2][:, :], ACT.Copy).then_inc(S["num_copied"], 1)

        def root_act(act, h):
            act.wait_ge(S["h_step"], HS * h + 7)
            act.activation(tok(2), tok(2), ACT.Sqrt).then_inc(S["h_rstd"], 1)

        def high_act(act, h):
            act.wait_ge(S["h_step"], HS * h + 11)
            act.activation(m2hi[:, h, :], hn, ACT.Copy).then_inc(S["mixm_hi"], 1)

        def mlstm_act(act):
            vtok_act(act, 0)
            for n in range(NS):
                h, J = n // C, n % C
                act.wait_ge(S["r_bc_loaded"][n % 4], 16 * (n // 4 + 1))
                act.activation(ering[:, n % 4, J * P:T], ering[:, n % 4, J * P:T], ACT.Exp,
                               bias=acol[:, 4 * J + h:4 * J + h + 1]).then_inc(S["st_exp"], 1)
                if h and J == 0:
                    num_act(act, h - 1)
                if J == 2:
                    gate_act(act, h)
                if h and J == 2:
                    root_act(act, h - 1)
                if h and J == 5:
                    high_act(act, h - 1)
                if J == 7 and h < 3:
                    vtok_act(act, h + 1)
            for part in (num_act, root_act, high_act):
                part(act, 3)

        def mlstm_pool(pool):
            for n in range(NS):
                h, J = n // C, n % C
                pool.wait_ge(S["st_w"], n + 1)
                blk = Wt[:, n % 3, J * P:(J + 1) * P]
                pool.affine_select(out=blk, in_=blk, compare_op=ALU.is_ge, fill=0.0, base=0,
                                   pattern=[[1, P]], channel_multiplier=-1).then_inc(S["w_ready"], 1)
                pool.wait_ge(S["w_ready"], n + 1)
                if J == 0:
                    if h:
                        pool.wait_ge(S["den_ready"], h)
                    pool.tensor_tensor(wsum[:, :], Wt[:, n % 3, :], ones[:, 0:1].to_broadcast([P, T]), ALU.mult)\
                        .then_inc(S["w_summed"], 1)
                else:
                    pool.wait_ge(S["w_summed"], n)
                    pool.tensor_tensor(wsum[:, J * P:T], wsum[:, J * P:T], Wt[:, n % 3, J * P:T], ALU.add)\
                        .then_inc(S["w_summed"], 1)

        def outputs(dve, h, first, last):
            den, em = by_tile(PS[3][:, :])[:, :, 0:1], emcol[:, h:32:4].rearrange("p (c o) -> p c o", o=1)
            for step in range(first, last + 1):
                if step > 1:
                    dve.wait_ge(S["h_step"], HS * h + step - 1)
                if step == 1:
                    dve.wait_ge(S["den_ready"], h + 1)
                    ins = dve.scalar_tensor_tensor(out=tok(0), in0=den, scalar=-1.0, in1=em,
                                                   op0=ALU.mult, op1=ALU.max)
                if step == 2:
                    ins = dve.tensor_tensor(tok(0), den, tok(0), ALU.max)
                if step == 3:
                    ins = dve.reciprocal(tok(0), tok(0))
                if step == 4:
                    ins = dve.tensor_tensor(tok(1), tok(0), tok(0), ALU.mult)
                if step == 5:
                    dve.wait_ge(S["hsq_sum"], 2 * h + 1)
                    ins = dve.scalar_tensor_tensor(out=tok(2), in0=den, scalar=1.0 / P, in1=tok(1),
                                                   op0=ALU.mult, op1=ALU.mult)
                if step == 6:
                    ins = dve.tensor_scalar(tok(2), tok(2), EPS, None, ALU.add)
                if step == 7:
                    ins = dve.reciprocal(tok(2), tok(2))
                if step == 8:
                    dve.wait_ge(S["h_rstd"], h + 1)
                    ins = dve.tensor_tensor(tok(0), tok(0), tok(2), ALU.mult)
                if step == 9:
                    ins = diagonal(dve, sqb, 0)
                if step == 10:
                    dve.wait_ge(S["num_copied"], h + 1)
                    dve.wait_ge(S["hsq_sum"], 2 * h + 2)
                    ins = dve.tensor_tensor(hn, PS[3][:, :], hn, ALU.mult)
                if step == 11:
                    dve.wait_ge(S["om_sig"], h + 1)
                    ins = dve.scalar_tensor_tensor(out=hn, in0=hn, scalar=col("ml_head_norm_2", h),
                                                   in1=omT[h % 2], op0=ALU.mult, op1=ALU.mult)
                ins.then_inc(S["h_step"], 1)

        def low_dve(dve, h):
            dve.wait_ge(S["mixm_hi"], h + 1)
            dve.tensor_tensor(m2lo[:, h, :], hn, m2hi[:, h, :].bitcast(F32), ALU.subtract)\
               .then_inc(S["mixm_lo"], 1)

        def mlstm_dve(dve):
            for n in range(NS):
                h, J = n // C, n % C
                s = slice(J * P, T)
                dve.wait_ge(S["st_exp"], n + 1)
                dve.wait_ge(S["st_ready"], n + 1)
                if n >= 3:
                    dve.wait_ge(S["ho_ready"], n - 2)
                    dve.wait_ge(S["w_summed"], n - 2)
                dve.scalar_tensor_tensor(out=Wt[:, n % 3, s], in0=PS[n % 2][:, s], scalar=0.125,
                                         in1=ering[:, n % 4, s], op0=ALU.mult, op1=ALU.mult)\
                   .then_inc(S["st_w"], 1)
                if h and J == 0:
                    outputs(dve, h - 1, 1, 4)
                if h and J == 1:
                    outputs(dve, h - 1, 5, 7)
                if h and J == 2:
                    outputs(dve, h - 1, 8, 9)
                if h and J == 4:
                    outputs(dve, h - 1, 10, 11)
                if h and J == 6:
                    low_dve(dve, h - 1)
            outputs(dve, 3, 1, HS)
            low_dve(dve, 3)

        def mlstm_pe(pe):
            def turn_v(h):
                pe.wait_ge(S["mv_loaded"], 16 * (h + 1))
                if h >= 2:
                    pe.wait_ge(S["h_step"], HS * (h - 2) + 10)
                for c in range(C):
                    tr = pe.transpose(PS[3][:, c * P:(c + 1) * P], vTm[:, c * P:(c + 1) * P], ident[:, :])
                tr.then_inc(S["mv_t"], 1)

            def scores(n):
                h, J = n // C, n % C
                hp = slice(h % 2 * 64, h % 2 * 64 + 64)
                src = stage if h < 2 else qk
                if n == 2 * C:
                    pe.wait_ge(S["qk_back"], 64)
                if n >= 2:
                    pe.wait_ge(S["st_w"], n - 1)
                for a, b in ((J * P, HALF), (max(J * P, HALF), T)):
                    if a < b:
                        mm = pe.matmul(PS[n % 2][:, a:b], src[hp, 1, J * P:(J + 1) * P],
                                       src[hp, 0, a:b], start=True, stop=True)
                mm.then_inc(S["st_ready"], 1)

            def numerator(n):
                h, J = n // C, n % C
                pe.wait_ge(S["w_ready"], n + 1)
                if J == 0:
                    pe.wait_ge(S["mv_tok"], h + 1)
                    if h:
                        pe.wait_ge(S["num_copied"], h)
                for a, b in ((J * P, HALF), (max(J * P, HALF), T)):
                    if a < b:
                        mm = pe.matmul(PS[2][:, a:b], vtok2[:, h % 2, J, :], Wt[:, n % 3, a:b],
                                       start=(J == 0), stop=(J == b // P - 1), skip_group_check=True)
                mm.then_inc(S["ho_ready"], 1)

            def denominator(h):
                pe.wait_ge(S["w_summed"], C * (h + 1))
                pe.wait_ge(S["mv_tok"], min(h + 2, 4))
                if h == 3:
                    pe.wait_ge(S["h_step"], HS * 2 + 10)
                sum_tokens(pe, 3, [wsum]).then_inc(S["den_ready"], 1)

            def square_sum(h):
                pe.wait_ge(S["h_sq"], h + 1)
                pe.wait_ge(S["h_step"], HS * h + 2)
                sum_tokens(pe, 3, [sqb]).then_inc(S["hsq_sum"], 1)

            def scale_out(h):
                pe.wait_ge(S["h_step"], HS * h + 9)
                spread_tokens(pe, 3, sqb).then_inc(S["hsq_sum"], 1)

            turn_v(0)
            pe.wait_ge(S["qk_back"], 32)
            scores(0)
            scores(1)
            for n in range(NS):
                h, J = n // C, n % C
                if h and J == 1:
                    square_sum(h - 1)
                if h and J == 4:
                    scale_out(h - 1)
                if J == 6 and h < 3:
                    turn_v(h + 1)
                numerator(n)
                if n + 2 < NS:
                    scores(n + 2)
                if J == C - 1:
                    denominator(h)
            square_sum(3)
            scale_out(3)

        def wo2_sp(sp):
            sp.wait_ge(S["mixm_lo"], 4)
            for j in range(2, KT):
                load_unit(sp, Step(U_WO2 + j), w_out2[:, :, j * P:(j + 1) * P])
                residual_back(sp, x2_d, j)

        def residual_back(sp, x_d_, j):
            for k in (range(j - 2, j - 1) if j < KT - 1 else range(KT - 3, KT)):
                sp.dma_start(xr[:, k, :], x_d_[k * P:(k + 1) * P, :]).then_inc(S["x_back"][k // 4], 16)

        def wo2_pe(pe):
            for j in range(KT):
                if j == 0:
                    pe.wait_ge(S["mixm_lo"], 4)
                mm_unit(pe, Step(U_WO2 + j), m2hi, m2lo)
            norm_sum(pe, "post_mix", KT)
            norm_spread(pe, "post_mix")

        def wo2_act(act):
            for j in range(KT):
                u = Step(U_WO2 + j)
                act.wait_ge(S["unit_done"], u.times(1, 1))
                norm_square(act, "post_mix", j, PS[u.par][:, :])
                act.activation(acc[:, j, :], PS[u.par][:, :], ACT.Copy, scale=col("norm_post_mix_2", j))\
                   .then_inc(S["unit_out"][u.par], 1)
            norm_root(act, "post_mix", rstd[:, :])

        def wo2_dve(dve):
            norm_dve(dve, "post_mix", no_wait)
            dve.wait_ge(S["rstd_ready"], NORM_AT["post_mix"] + 1)
            for k in range(KT):
                dve.tensor_tensor(acc[:, k, :], acc[:, k, :], rstd[:, :], ALU.mult).then_inc(S["y_scaled"], 1)
                if k:
                    scale_lo(dve, OPERAND["mlp"], k - 1, acc[:, k - 1, :], col("norm_pre_mlp_2", k - 1),
                             h3hi, h3lo)
            scale_lo(dve, OPERAND["mlp"], KT - 1, acc[:, KT - 1, :], col("norm_pre_mlp_2", KT - 1), h3hi, h3lo)
            for k in range(KT):
                norm_add(dve, "mlp", k, sq8[:, k, :])
            norm_mean(dve, "mlp", KT)

        def x3_pool(pool):
            for k in range(KT):
                pool.wait_ge(S["y_scaled"], k + 1)
                pool.wait_ge(S["x_back"][k // 4], 16 + 64)
                pool.tensor_tensor(acc[:, k, :], acc[:, k, :], xr[:, k, :], ALU.add).then_inc(S["x_added"], 1)

        def x3_act(act):
            for k in range(KT):
                act.wait_ge(S["x_added"], k + 1)
                scale_hi(act, k, acc[:, k, :], col("norm_pre_mlp_2", k), h3hi)
                act.activation(sq8[:, k, :], acc[:, k, :], ACT.Square).then_inc(S["sq_done"], 1)
            spill3_act(act)
            norm_root(act, "mlp", rstd[:, :])

        def spill3_act(act):
            act.wait_ge(S["x_added"], KT)
            act.dma_start(tile_of(x3_d, 0, KT), acc[:, :, :]).then_inc(S["x_spilled"], 16)

        def f2_sp(sp):
            def do(e, kind, g, u, size):
                for t in range(size if kind == "in" else 0):
                    if u.s == 0 and g.c == 0 and t < 2:
                        continue
                    load_unit(e, u + t, w_up[:, :, bass.ds(g.times(G * P, t * P), P)])
                for j in range(KT if kind == "out" else 0):
                    load_unit(e, u + j, w_down[:, bass.ds(g.times(G), size), j * P:(j + 1) * P], size)
                    if u.c == U_END - KT and j >= 2:
                        e.wait_ge(S["unit_done"], U_END - KT)
                        residual_back(e, x3_d, j)
            run_ffn(sp, SEG2, G2, 1, do)

        def f2_pool(pool):
            def do(e, kind, g, u, size):
                for t in range(size if kind == "in" else KT):
                    split_unit(e, u + t, KT if kind == "in" else size)
                    if u.s == 0 and u.c + t == U_F2 + 1:
                        x3_pool(e)
            run_ffn(pool, SEG2, G2, 1, do)

        def f2_pe(pe):
            def do(e, kind, g, u, size):
                if kind == "in":
                    for t in range(size):
                        start = u.s == 0 and g.c == 0
                        mm_unit(e, u + t, h3hi, h3lo, wait_k=lo_wait(e, "mlp") if start and t == 0 else
                                spread_at(e, "mlp") if start and t == 1 else None)
                        if start and t == 0:
                            norm_sum(e, "mlp", KT)
                else:
                    e.wait_ge(S["sq_lo"], g.times(G, size))
                    s0 = G * g.par
                    for j in range(KT):
                        mm_unit(e, u + j, a2hi[:, s0:s0 + size, :], a2lo[:, s0:s0 + size, :], size)
            run_ffn(pe, SEG2, G2, 1, do)

        def f2_act(act):
            def do(e, kind, g, u, size):
                for t in range(size if kind == "in" else 0):
                    n = g.times(G, t + 1)
                    ut = u + t
                    e.wait_ge(S["unit_out"][ut.par], ut.nth())
                    e.activation(stage[:, 1, :], stage[:, 0, :], ACT.Square).then_inc(S["up_sq"], 1)
                    e.wait_ge(S["up_sq"], n)
                    e.activation(a2hi[:, G * g.par + t, :], stage[:, 1, :], ACT.Copy).then_inc(S["sq_hi"], 1)
            run_ffn(act, SEG2, G2, 1, do)

        def f2_dve(dve):
            def do(e, kind, g, u, size):
                if kind == "out":
                    for j in range(KT):
                        if j % 4 == 0:
                            e.wait_ge(S["acc_zero"], j // 4 + 1)
                        add_dve(e, u + j, j)
                        if u.c == U_END - KT and j:
                            norm_add(e, "post_mlp", j - 1)
                    return
                for t in range(size):
                    n = g.times(G, t + 1)
                    ut = u + t
                    e.wait_ge(S["unit_done"], ut.times(1, 1))
                    e.scalar_tensor_tensor(out=stage[:, 0, :], in0=PS[ut.par][:, :], scalar=0.0,
                                           in1=rstd[:, :], op0=ALU.max, op1=ALU.mult)\
                     .then_inc(S["unit_out"][ut.par], 1)
                    e.wait_ge(S["sq_hi"], n)
                    e.tensor_tensor(a2lo[:, G * g.par + t, :], stage[:, 1, :],
                                    a2hi[:, G * g.par + t, :].bitcast(F32), ALU.subtract)\
                     .then_inc(S["sq_lo"], 1)
                    if u.s == 0 and g.c == 0 and t >= 2:
                        e.wait_ge(S["x_spilled"], 48)
                        z = slice(4 * (t - 2), 4 * (t - 2) + 4)
                        e.memset(acc[:, z, :], 0.0).then_inc(S["acc_zero"], 1)
            dve.wait_ge(S["rstd_ready"], NORM_AT["mlp"] + 1)
            run_ffn(dve, SEG2, G2, 1, do)

        def end_sp(sp):
            for c in range(C):
                sp.wait_ge(S["out_ev"], c + 1)
                sp.dma_start(out[0, c * P:(c + 1) * P, :], orow[:, c % 4, :]).then_inc(S["out_stored"][c % 4], 16)
            for i in range(4):
                sp.wait_ge(S["out_stored"][i], 16 * C // 4)

        def end_dve(dve):
            norm_add(dve, "post_mlp", KT - 1)
            norm_mean(dve, "post_mlp", KT)
            dve.wait_ge(S["rstd_ready"], NORM_AT["post_mlp"] + 1)
            for b in range(2):
                t = slice(b * HALF, (b + 1) * HALF)
                for k in range(KT):
                    dve.scalar_tensor_tensor(out=acc[:, k, t], in0=acc[:, k, t],
                                             scalar=col("norm_post_mlp_2", k), in1=rstd[:, t],
                                             op0=ALU.mult, op1=ALU.mult).then_inc(S["y_scaled"], 1)

        def end_pool(pool):
            for b in range(2):
                t = slice(b * HALF, (b + 1) * HALF)
                for k in range(KT):
                    pool.wait_ge(S["y_scaled"], KT * (b + 1) + k + 1)
                    pool.wait_ge(S["x_back"][k // 4], 16 + 2 * 64)
                    pool.tensor_tensor(acc[:, k, t], acc[:, k, t], xr[:, k, t], ALU.add)\
                        .then_inc(S["x_added"], 1)

        def end_pe(pe):
            norm_sum(pe, "post_mlp", KT)
            norm_spread(pe, "post_mlp")
            for c in range(C):
                pe.wait_ge(S["x_added"], KT * (2 + c // 4))
                if c >= 2:
                    pe.wait_ge(S["out_ev"], c - 1)
                for k in range(KT):
                    tr = pe.transpose(PS[c % 2][:, k * P:(k + 1) * P], acc[:, k, c * P:(c + 1) * P], ident[:, :])
                tr.then_inc(S["out_t"], 1)

        def end_act(act):
            for c in range(C):
                act.wait_ge(S["out_t"], c + 1)
                if c >= 4:
                    act.wait_ge(S["out_stored"][c % 4], 16 * (c // 4))
                act.activation(orow[:, c % 4, :], PS[c % 2][:, :], ACT.Copy).then_inc(S["out_ev"], 1)

        @block.sync
        def _(sp):
            start_sp(sp)
            wup_sp(sp)
            in_sp(sp)
            gla_sp(sp)
            merge_sp(sp)
            wo_sp(sp)
            f1_sp(sp)
            in2_sp(sp)
            mla_sp(sp)
            all_stored(sp, ALL_IN2)
            for j in range(2):
                load_unit(sp, Step(U_WO2 + j), w_out2[:, :, j * P:(j + 1) * P])
            mlstm_sp(sp)
            wo2_sp(sp)
            for t in range(2):
                load_unit(sp, Step(U_F2 + t), w_up[:, :, t * P:(t + 1) * P])
            f2_sp(sp)
            end_sp(sp)

        @block.gpsimd
        def _(pool):
            start_pool(pool)
            wup_pool(pool)
            in_pool(pool)
            mid_pool(pool)
            for j in range(2 * KT):
                split_unit(pool, Step(U_YA + j))
            f1_pool(pool)
            fin_pool(pool, KT - 3)
            split_unit(pool, Step(U_IN2))
            for k in (KT - 2, KT - 1):
                fin_pool(pool, k)
            in2_pool(pool)
            mla_pool(pool)
            for j in range(2):
                split_unit(pool, Step(U_WO2 + j))
            mlstm_pool(pool)
            for j in range(2, KT):
                split_unit(pool, Step(U_WO2 + j))
            f2_pool(pool)
            end_pool(pool)

        @block.scalar
        def _(act):
            start_act(act)
            norm_act(act, "mix", no_wait, "norm_mix", h1hi)
            in_act(act)
            gla_act(act)
            merge_act(act)
            norm_act(act, "ffn", after_unit(U_WO), "norm_ffn", m2hi)
            f1_act(act)
            fin_act(act)
            in2_act(act)
            mla_act(act)
            mlstm_act(act)
            wo2_act(act)
            x3_act(act)
            f2_act(act)
            norm_act(act, "post_mlp", after_unit(U_END - KT))
            end_act(act)

        @block.tensor
        def _(pe):
            start_pe(pe)
            in_pe(pe)
            gla_pe(pe)
            merge_pe(pe)
            wo_pe(pe)
            f1_pe(pe)
            in2_pe(pe)
            mla_pe(pe)
            mlstm_pe(pe)
            wo2_pe(pe)
            f2_pe(pe)
            end_pe(pe)

        @block.vector
        def _(dve):
            norm_dve(dve, "mix", no_wait, "norm_mix", h1hi, h1lo)
            dve.tensor_tensor(gg[:, :], cols[:, VEC["norm_final"]:VEC["norm_final"] + KT],
                              cols[:, VEC["norm_pre_mix_2"]:VEC["norm_pre_mix_2"] + KT], ALU.mult)\
               .then_inc(S["cols_ready"], 1)
            in_dve(dve)
            gla_dve(dve)
            merge_dve(dve)
            wo_dve(dve)
            f1_dve(dve)
            fin_means(dve)
            in2_dve(dve)
            mla_dve(dve)
            mlstm_dve(dve)
            wo2_dve(dve)
            f2_dve(dve)
            end_dve(dve)


OUTS = [((1, T, D), "float32")]


def rope_table():
    import numpy as np
    inv = (1.0 / (10000.0 ** (np.arange(0, 32, 2, dtype=np.float32) / 32))).astype(np.float32)
    t = np.zeros((P, 3), np.float32)
    t[:, 2] = 1.0
    for q in range(4):
        r = slice(64 + 16 * q, 80 + 16 * q)
        t[r, 0] = inv
        t[r, 1] = np.pi / 2 if q < 2 else 0.0
        t[r, 2] = -1.0 if q == 2 else 1.0
    return t


def kernel(**inputs):
    import numpy as np
    import concourse.bacc as bacc
    from concourse.bass_utils import run_bass_kernel_spmd

    nc = bacc.Bacc("TRN2", target_bir_lowering=False, num_devices=1)
    arrays, aps = {}, {}
    for name, a in {**inputs, "rope_table": rope_table()}.items():
        a = np.ascontiguousarray(a)
        arrays[f"in_{name}"] = a
        aps[name] = nc.dram_tensor(f"in_{name}", a.shape, mybir.dt.from_np(a.dtype), kind="ExternalInput").ap()
    shape, dtype = OUTS[0]
    out = nc.dram_tensor("out_0", shape, mybir.dt.from_np(np.dtype(dtype)), kind="ExternalOutput").ap()
    two_block_kernel(nc, aps, out)
    r = run_bass_kernel_spmd(nc, [arrays], core_ids=[0])
    return r.results[0]["out_0"]
```
